# Optimizing a Trainium2 kernel written in Bass

```python
import math
import jax, jax.numpy as jnp
from jax import lax
import numpy as np

D_MODEL = 1024
BATCH = 1
SEQ = 512
DEPTH = 2

ATT_HEADS = 8
ATT_KV_GROUPS = 2
ATT_HPG = ATT_HEADS // ATT_KV_GROUPS
HEAD_DIM = 64
D_ATT = ATT_HEADS * HEAD_DIM
D_KV = ATT_KV_GROUPS * HEAD_DIM
N_BRANCH = 3
CMP_LEN = 32
CMP_STRIDE = 16
CMP_HIDDEN = 256
SLC_BLOCK = 64
SLC_TOPN = 16
WINDOW = 512
Q_BLOCK = 128
SEL_FORCE = 1.0e4
REL_BUCKETS = 32
REL_MAX_DIST = 128
GMLP_GROUPS = 4
GMLP_GROUP_DIM = 64
D_GMLP = GMLP_GROUPS * GMLP_GROUP_DIM
GMLP_CHUNK = 128
SSM_HEADS = 4
SSM_HEAD_DIM = 64
D_SSM = SSM_HEADS * SSM_HEAD_DIM
SSM_GROUPS = 2
SSM_STATE = 128
SSM_CONV = 4
SSM_CHUNK = 256
D_XBC = D_SSM + 2 * SSM_GROUPS * SSM_STATE
D_MIX = D_ATT + D_GMLP + D_SSM
D_ATT_IN = D_ATT + 6 * D_KV + ATT_HEADS * N_BRANCH
D_GMLP_IN = 2 * D_GMLP
D_SSM_IN = D_SSM + D_XBC + SSM_HEADS
D_IN = D_ATT_IN + D_GMLP_IN + D_SSM_IN
D_FF = 2816
N_SUB = 3
ALPHA = (2 * DEPTH) ** 0.25
BETA = (8 * DEPTH) ** -0.25
LN_EPS = 1e-5


def layer_norm(x, g, b):
    xf = x.astype(jnp.float32)
    mu = xf.mean(-1, keepdims=True)
    var = jnp.square(xf - mu).mean(-1, keepdims=True)
    return ((xf - mu) * lax.rsqrt(var + LN_EPS)).astype(x.dtype) * g + b

def swiglu(h, w1, w3, w2):
    return (jax.nn.silu(h @ w1) * (h @ w3)) @ w2

def masked_softmax(s, mask):
    s = jnp.where(mask, s.astype(jnp.float32), -jnp.inf)
    m = jnp.max(s, axis=-1, keepdims=True)
    m = jnp.where(jnp.isfinite(m), m, 0.0)
    p = jnp.exp(s - m)
    return p / jnp.maximum(p.sum(-1, keepdims=True), 1e-30)

def rel_bucket(dist):
    n = jnp.maximum(dist, 0)
    max_exact = REL_BUCKETS // 2
    nf = jnp.maximum(n, 1).astype(jnp.float32)
    large = max_exact + (jnp.log(nf / max_exact) / math.log(REL_MAX_DIST / max_exact)
                         * (REL_BUCKETS - max_exact)).astype(jnp.int32)
    large = jnp.minimum(large, REL_BUCKETS - 1)
    return jnp.where(n < max_exact, n, large)

def nsa_attention(q, k_cmp, v_cmp, k_slc, v_slc, k_win, v_win, gates, rel_bias,
                  cmp_pe, cmp_w1, cmp_b1, cmp_w2):
    Bn, T = q.shape[:2]
    G, I, Dh = ATT_KV_GROUPS, ATT_HPG, HEAD_DIM
    n_cmp = (T - CMP_LEN) // CMP_STRIDE + 1
    n_slc = T // SLC_BLOCK
    n_qb = T // Q_BLOCK
    top_n = min(SLC_TOPN, n_slc)
    kw_len = Q_BLOCK + WINDOW

    cmp_start = np.arange(n_cmp) * CMP_STRIDE
    blk_idx = cmp_start[:, None] + np.arange(CMP_LEN)[None, :]

    def compress(kv, j):
        blocks = kv[:, blk_idx] + cmp_pe[j][None, None, :, None, :]
        blocks = blocks.transpose(0, 3, 1, 2, 4).reshape(Bn, G, n_cmp, CMP_LEN * Dh)
        return jax.nn.gelu(blocks @ cmp_w1[j] + cmp_b1[j]) @ cmp_w2[j]

    kc, vc = compress(k_cmp, 0), compress(v_cmp, 1)
    cmp_end = jnp.asarray(cmp_start + CMP_LEN - 1, jnp.int32)
    slc_start = np.arange(n_slc) * SLC_BLOCK
    overlap = np.clip(np.minimum(cmp_start[:, None] + CMP_LEN, slc_start[None, :] + SLC_BLOCK)
                      - np.maximum(cmp_start[:, None], slc_start[None, :]), 0, None)
    overlap = jnp.asarray(overlap / CMP_LEN, jnp.float32)

    ks = k_slc.transpose(0, 2, 1, 3).reshape(Bn, G, n_slc, SLC_BLOCK, Dh)
    vs = v_slc.transpose(0, 2, 1, 3).reshape(Bn, G, n_slc, SLC_BLOCK, Dh)
    pad_w = ((0, 0), (0, 0), (WINDOW, 0), (0, 0))
    kw = jnp.pad(k_win.transpose(0, 2, 1, 3), pad_w)
    vw = jnp.pad(v_win.transpose(0, 2, 1, 3), pad_w)

    win_dist = np.arange(Q_BLOCK)[:, None] + WINDOW - np.arange(kw_len)[None, :]
    win_mask = jnp.asarray((win_dist >= 0) & (win_dist < WINDOW))
    win_bias = rel_bias[rel_bucket(jnp.asarray(win_dist, jnp.int32))]
    win_bias = win_bias.reshape(Q_BLOCK, kw_len, G, I).transpose(2, 3, 0, 1)
    rb = rel_bias.reshape(REL_BUCKETS, G, I)
    gather_blocks = jax.vmap(jax.vmap(lambda kb, s: kb[s]))
    bias_by_group = jax.vmap(lambda tb, bk: tb[bk], in_axes=(1, 1), out_axes=1)

    qb_all = q.reshape(Bn, n_qb, Q_BLOCK, G, I, Dh).transpose(1, 0, 3, 4, 2, 5) * (Dh ** -0.5)
    gb_all = gates.reshape(Bn, n_qb, Q_BLOCK, G, I, N_BRANCH).transpose(1, 0, 3, 4, 2, 5)

    def block(args):
        b_idx, qb, gb = args
        start = b_idx * Q_BLOCK
        t = start + jnp.arange(Q_BLOCK, dtype=jnp.int32)
        dist_c = t[:, None] - cmp_end[None, :]
        bias_c = rel_bias[rel_bucket(dist_c)].reshape(Q_BLOCK, n_cmp, G, I).transpose(2, 3, 0, 1)
        p_c = masked_softmax(jnp.einsum('bgiqd,bgkd->bgiqk', qb, kc) + bias_c, dist_c >= 0)
        o_c = jnp.einsum('bgiqk,bgkd->bgiqd', p_c.astype(vc.dtype), vc)
        imp = jnp.einsum('bgiqk,kn->bgqn', p_c, overlap)
        cur = (t // SLC_BLOCK)[:, None]
        blk = jnp.arange(n_slc, dtype=jnp.int32)[None, :]
        forced = (blk == 0) | (blk == cur) | (blk == cur - 1)
        imp = jnp.where(forced, SEL_FORCE, jnp.where(blk <= cur, imp, -SEL_FORCE))
        _, sel = lax.top_k(imp, top_n)
        k_sel = gather_blocks(ks, sel).reshape(Bn, G, Q_BLOCK, top_n * SLC_BLOCK, Dh)
        v_sel = gather_blocks(vs, sel).reshape(Bn, G, Q_BLOCK, top_n * SLC_BLOCK, Dh)
        pos_sel = (sel[..., None] * SLC_BLOCK + jnp.arange(SLC_BLOCK, dtype=jnp.int32)
                   ).reshape(Bn, G, Q_BLOCK, top_n * SLC_BLOCK)
        dist_s = t[None, None, :, None] - pos_sel
        bias_s = bias_by_group(rb, rel_bucket(dist_s)).transpose(0, 1, 4, 2, 3)
        p_s = masked_softmax(jnp.einsum('bgiqd,bgqkd->bgiqk', qb, k_sel) + bias_s,
                             (dist_s >= 0)[:, :, None])
        o_s = jnp.einsum('bgiqk,bgqkd->bgiqd', p_s.astype(v_sel.dtype), v_sel)
        kb = lax.dynamic_slice_in_dim(kw, start, kw_len, axis=2)
        vb = lax.dynamic_slice_in_dim(vw, start, kw_len, axis=2)
        pos_w = start - WINDOW + jnp.arange(kw_len, dtype=jnp.int32)
        p_w = masked_softmax(jnp.einsum('bgiqd,bgkd->bgiqk', qb, kb) + win_bias,
                             win_mask & (pos_w >= 0)[None, :])
        o_w = jnp.einsum('bgiqk,bgkd->bgiqd', p_w.astype(vb.dtype), vb)
        return gb[..., 0:1] * o_c + gb[..., 1:2] * o_s + gb[..., 2:3] * o_w

    o = lax.map(block, (jnp.arange(n_qb, dtype=jnp.int32), qb_all, gb_all))
    return o.transpose(1, 0, 4, 2, 3, 5).reshape(Bn, T, ATT_HEADS * Dh)

def gmlp_spatial_gating(uv, ln_g, ln_b, ws, bs):
    Bn, T, _ = uv.shape
    u, v = jnp.split(jax.nn.gelu(uv), 2, axis=-1)
    v = layer_norm(v, ln_g, ln_b)
    v = v.reshape(Bn, T // GMLP_CHUNK, GMLP_CHUNK, GMLP_GROUPS, GMLP_GROUP_DIM)
    causal = jnp.tril(jnp.ones((GMLP_CHUNK, GMLP_CHUNK), dtype=bool))
    w = jnp.where(causal[None], ws, 0.0)
    sv = jnp.einsum('gts,bcsgd->bctgd', w, v) + bs.T[None, None, :, :, None]
    return u * sv.reshape(Bn, T, D_GMLP)

def segsum(a):
    L = a.shape[-1]
    cs = jnp.cumsum(a, axis=-1)
    mask = jnp.tril(jnp.ones((L, L), dtype=bool))
    return jnp.where(mask, cs[..., :, None] - cs[..., None, :], -jnp.inf)

def ssd_chunked(X, A, Bh, Ch):
    Bn, T, H, P = X.shape
    nc = -(-T // SSM_CHUNK)
    pad = nc * SSM_CHUNK - T
    def chunk(a):
        a = jnp.pad(a, [(0, 0), (0, pad)] + [(0, 0)] * (a.ndim - 2))
        return a.reshape(Bn, nc, SSM_CHUNK, *a.shape[2:])
    X, A, Bh, Ch = chunk(X), chunk(A), chunk(Bh), chunk(Ch)
    A = A.transpose(0, 3, 1, 2)
    A_cs = jnp.cumsum(A, axis=-1)
    Lmat = jnp.exp(segsum(A))
    scores = jnp.einsum('bclhn,bcshn->bhcls', Ch, Bh) * Lmat
    y_diag = jnp.einsum('bhcls,bcshp->bclhp', scores, X)
    decay = jnp.exp(A_cs[..., -1:] - A_cs)
    states = jnp.einsum('bclhn,bhcl,bclhp->bchpn', Bh, decay, X)
    chunk_decay = jnp.exp(A_cs[..., -1])

    def step(h, inp):
        s_c, dec = inp
        return dec[:, :, None, None] * h + s_c, h

    h0 = jnp.zeros((Bn, H, P, Bh.shape[-1]), X.dtype)
    _, prev = lax.scan(step, h0, (states.transpose(1, 0, 2, 3, 4), chunk_decay.transpose(2, 0, 1)))
    prev = prev.transpose(1, 0, 2, 3, 4)
    y_off = jnp.einsum('bclhn,bchpn,bhcl->bclhp', Ch, prev, jnp.exp(A_cs))
    return (y_diag + y_off).reshape(Bn, nc * SSM_CHUNK, H, P)[:, :T]

def mamba2_ssd(zxbcdt, conv_w, conv_b, dt_bias, a_log, d_skip, norm_g):
    Bn, T, _ = zxbcdt.shape
    z, xbc, dt = jnp.split(zxbcdt, [D_SSM, D_SSM + D_XBC], axis=-1)
    xbc = lax.conv_general_dilated(xbc, conv_w[:, None, :], window_strides=(1,),
                                   padding=[(SSM_CONV - 1, 0)],
                                   dimension_numbers=('NWC', 'WIO', 'NWC'),
                                   feature_group_count=D_XBC) + conv_b
    xbc = jax.nn.silu(xbc)
    xs, Bm, Cm = jnp.split(xbc, [D_SSM, D_SSM + SSM_GROUPS * SSM_STATE], axis=-1)
    dt = jax.nn.softplus((dt + dt_bias).astype(jnp.float32))
    A = -jnp.exp(a_log.astype(jnp.float32))
    X = xs.reshape(Bn, T, SSM_HEADS, SSM_HEAD_DIM)
    rep = SSM_HEADS // SSM_GROUPS
    Bh = jnp.repeat(Bm.reshape(Bn, T, SSM_GROUPS, SSM_STATE), rep, axis=2).astype(jnp.float32)
    Ch = jnp.repeat(Cm.reshape(Bn, T, SSM_GROUPS, SSM_STATE), rep, axis=2).astype(jnp.float32)
    y = ssd_chunked(X.astype(jnp.float32) * dt[..., None], A * dt, Bh, Ch)
    y = y + X.astype(jnp.float32) * d_skip.astype(jnp.float32)[:, None]
    g = (y.reshape(Bn, T, D_SSM) * jax.nn.silu(z.astype(jnp.float32))).reshape(Bn, T, SSM_GROUPS, -1)
    g = g * lax.rsqrt(jnp.mean(jnp.square(g), axis=-1, keepdims=True) + LN_EPS)
    return g.reshape(Bn, T, D_SSM).astype(zxbcdt.dtype) * norm_g

def hybrid_mixer(h, rel_bias, w_in, w_out, cmp_pe, cmp_w1, cmp_b1, cmp_w2,
                 gmlp_ln_g, gmlp_ln_b, gmlp_ws, gmlp_bs,
                 conv_w, conv_b, dt_bias, a_log, d_skip, norm_g):
    Bn, T, _ = h.shape
    proj = h @ w_in
    att_in, gmlp_in, ssm_in = jnp.split(proj, [D_ATT_IN, D_ATT_IN + D_GMLP_IN], axis=-1)
    cuts = [D_ATT + i * D_KV for i in range(7)]
    q, kc, vc, ks, vs, kw, vw, g = jnp.split(att_in, cuts, axis=-1)
    kvr = lambda a: a.reshape(Bn, T, ATT_KV_GROUPS, HEAD_DIM)
    gates = jax.nn.sigmoid(g).reshape(Bn, T, ATT_HEADS, N_BRANCH)
    o_att = nsa_attention(q.reshape(Bn, T, ATT_HEADS, HEAD_DIM), kvr(kc), kvr(vc), kvr(ks), kvr(vs),
                          kvr(kw), kvr(vw), gates, rel_bias, cmp_pe, cmp_w1, cmp_b1, cmp_w2)
    o_gmlp = gmlp_spatial_gating(gmlp_in, gmlp_ln_g, gmlp_ln_b, gmlp_ws, gmlp_bs)
    o_ssm = mamba2_ssd(ssm_in, conv_w, conv_b, dt_bias, a_log, d_skip, norm_g)
    return jnp.concatenate([o_att, o_gmlp, o_ssm], axis=-1) @ w_out

def post_norm_residual(x, y, gate, weight, g, b):
    return layer_norm(ALPHA * x + weight * (1.0 + gate) * y, g, b)

def first_inputs(seed: int = 0) -> dict:
    key = jax.random.key(seed)
    k = jax.random.split(key, 30)
    nrm = lambda kk, shape, s: jax.random.normal(kk, shape, jnp.float32) * s
    L = DEPTH
    dt_init = jnp.exp(jax.random.uniform(k[25], (L, SSM_HEADS), jnp.float32,
                                         math.log(1e-3), math.log(1e-1)))
    return {
        "x": nrm(k[0], (BATCH, SEQ, D_MODEL), 1.0),
        "c": nrm(k[1], (BATCH, D_MODEL), 1.0),
        "rel_bias": nrm(k[2], (REL_BUCKETS, ATT_HEADS), 0.5),
        "ada_w": nrm(k[3], (L, D_MODEL, N_SUB * 3 * D_MODEL), 0.5 * D_MODEL ** -0.5),
        "ada_b": nrm(k[4], (L, N_SUB * 3 * D_MODEL), 0.02),
        "ln_g": 1.0 + nrm(k[5], (L, N_SUB, D_MODEL), 0.02),
        "ln_b": nrm(k[6], (L, N_SUB, D_MODEL), 0.02),
        "ffn_w1": nrm(k[7], (L, 2, D_MODEL, D_FF), BETA * D_MODEL ** -0.5),
        "ffn_w3": nrm(k[8], (L, 2, D_MODEL, D_FF), BETA * D_MODEL ** -0.5),
        "ffn_w2": nrm(k[9], (L, 2, D_FF, D_MODEL), BETA * D_FF ** -0.5),
        "w_in": nrm(k[10], (L, D_MODEL, D_IN), D_MODEL ** -0.5),
        "w_out": nrm(k[11], (L, D_MIX, D_MODEL), BETA * D_MIX ** -0.5),
        "cmp_pe": nrm(k[12], (L, 2, CMP_LEN, HEAD_DIM), 0.1),
        "cmp_w1": nrm(k[13], (L, 2, CMP_LEN * HEAD_DIM, CMP_HIDDEN), (CMP_LEN * HEAD_DIM) ** -0.5),
        "cmp_b1": nrm(k[14], (L, 2, CMP_HIDDEN), 0.02),
        "cmp_w2": nrm(k[15], (L, 2, CMP_HIDDEN, HEAD_DIM), 1.5 * CMP_HIDDEN ** -0.5),
        "gmlp_ln_g": 1.0 + nrm(k[16], (L, D_GMLP), 0.02),
        "gmlp_ln_b": nrm(k[17], (L, D_GMLP), 0.02),
        "gmlp_ws": nrm(k[18], (L, GMLP_GROUPS, GMLP_CHUNK, GMLP_CHUNK), GMLP_CHUNK ** -0.5),
        "gmlp_bs": 1.0 + nrm(k[19], (L, GMLP_GROUPS, GMLP_CHUNK), 0.02),
        "ssm_conv_w": nrm(k[20], (L, SSM_CONV, D_XBC), SSM_CONV ** -0.5),
        "ssm_conv_b": nrm(k[21], (L, D_XBC), 0.02),
        "ssm_dt_bias": dt_init + jnp.log(-jnp.expm1(-dt_init)),
        "ssm_a_log": jnp.log(jax.random.uniform(k[22], (L, SSM_HEADS), jnp.float32, 1.0, 16.0)),
        "ssm_d": 1.0 + nrm(k[23], (L, SSM_HEADS), 0.02),
        "ssm_norm_g": 1.0 + nrm(k[24], (L, D_SSM), 0.02),
    }

def first_block(x, c, rel_bias, ada_w, ada_b, ln_g, ln_b, ffn_w1, ffn_w3, ffn_w2, w_in, w_out,
              cmp_pe, cmp_w1, cmp_b1, cmp_w2, gmlp_ln_g, gmlp_ln_b, gmlp_ws, gmlp_bs,
              ssm_conv_w, ssm_conv_b, ssm_dt_bias, ssm_a_log, ssm_d, ssm_norm_g):
    Bn = x.shape[0]
    for l in range(DEPTH):
        mod = (jax.nn.silu(c) @ ada_w[l] + ada_b[l]).reshape(Bn, N_SUB, 3, D_MODEL)
        shift, scale, gate = mod[:, :, 0, None], mod[:, :, 1, None], mod[:, :, 2, None]
        h = x * (1.0 + scale[:, 0]) + shift[:, 0]
        y = swiglu(h, ffn_w1[l, 0], ffn_w3[l, 0], ffn_w2[l, 0])
        x = post_norm_residual(x, y, gate[:, 0], 0.5, ln_g[l, 0], ln_b[l, 0])
        h = x * (1.0 + scale[:, 1]) + shift[:, 1]
        y = hybrid_mixer(h, rel_bias, w_in[l], w_out[l], cmp_pe[l], cmp_w1[l], cmp_b1[l], cmp_w2[l],
                         gmlp_ln_g[l], gmlp_ln_b[l], gmlp_ws[l], gmlp_bs[l],
                         ssm_conv_w[l], ssm_conv_b[l], ssm_dt_bias[l], ssm_a_log[l], ssm_d[l],
                         ssm_norm_g[l])
        x = post_norm_residual(x, y, gate[:, 1], 1.0, ln_g[l, 1], ln_b[l, 1])
        h = x * (1.0 + scale[:, 2]) + shift[:, 2]
        y = swiglu(h, ffn_w1[l, 1], ffn_w3[l, 1], ffn_w2[l, 1])
        x = post_norm_residual(x, y, gate[:, 2], 0.5, ln_g[l, 2], ln_b[l, 2])
    return x


_first_inputs = first_inputs


def first_inputs(seed=0):
    import zlib

    import numpy as np

    out = dict(_first_inputs(seed))
    spreads = {}
    factors = {'ada_b': 3.363,
     'cmp_pe': 3.236,
     'cmp_b1': 8.0,
     'gmlp_ln_g': 8.0,
     'gmlp_ln_b': 8.0,
     'gmlp_bs': 8.0,
     'ssm_conv_b': 7.623,
     'ssm_d': 8.0,
     'ssm_norm_g': 8.0}
    for name, (base, spread) in spreads.items():
        noise = np.random.default_rng([zlib.crc32(name.encode()), seed]).standard_normal(out[name].shape)
        drawn = base * np.exp(spread * noise) if base else spread * noise
        out[name] = __import__('jax').numpy.asarray(drawn.astype(out[name].dtype))
    for name, factor in factors.items():
        out[name] = (out[name] * factor).astype(out[name].dtype)
    return out


_narrow_inputs = first_inputs


def first_inputs(seed=0):
    out = dict(_narrow_inputs(seed))
    wider = {'rel_bias': 3.89,
     'cmp_b1': 4.15,
     'gmlp_ln_g': 5.78,
     'gmlp_ln_b': 6.32,
     'gmlp_bs': 4.23,
     'ssm_d': 3.42,
     'ssm_norm_g': 3.37}
    for name, times in wider.items():
        mean = out[name].mean()
        out[name] = (mean + times * (out[name] - mean)).astype(out[name].dtype)
    return out


N_HEADS = D_MODEL // HEAD_DIM
INNER = N_HEADS * HEAD_DIM
ROT_DIM = HEAD_DIM // 4
ROPE_THETA = 500000.0
DSWA_GROUPS = ((128, 1), (512, 4), (2048, 16))
N_GROUPS = len(DSWA_GROUPS)
BLOCK = 128
N_MIXERS = 2
EPS = 1e-6
FOX_IN = 4 * INNER + N_HEADS
DSW_IN = 3 * N_GROUPS * INNER + INNER


def rms_norm(x, g):
    xf = x.astype(jnp.float32)
    y = xf * lax.rsqrt(jnp.mean(xf * xf, axis=-1, keepdims=True) + EPS) * g.astype(jnp.float32)
    return y.astype(x.dtype)

def rotary_tables(positions):
    inv_freq = ROPE_THETA ** (-jnp.arange(0, ROT_DIM, 2, dtype=jnp.float32) / ROT_DIM)
    ang = positions.astype(jnp.float32)[..., None] * inv_freq
    return jnp.cos(ang), jnp.sin(ang)

def apply_partial_rotary(t, cos, sin):
    half = ROT_DIM // 2
    c = cos[:, :, None, None, :].astype(t.dtype)
    s = sin[:, :, None, None, :].astype(t.dtype)
    t1, t2, rest = t[..., :half], t[..., half:ROT_DIM], t[..., ROT_DIM:]
    return jnp.concatenate([t1 * c - t2 * s, t2 * c + t1 * s, rest], axis=-1)

def fox_attention(q, k, v, c):
    B, S, H, dh = q.shape
    nq = S // BLOCK
    scale = dh ** -0.5
    qb = q.reshape(B, nq, BLOCK, H, dh).transpose(1, 0, 2, 3, 4)
    cb = c.reshape(B, nq, BLOCK, H).transpose(1, 0, 3, 2)
    c_k = c.transpose(0, 2, 1)
    key_pos = jnp.arange(S)

    def one_block(args):
        qi, ci, bi = args
        s = jnp.einsum('bqhd,bkhd->bhqk', qi, k).astype(jnp.float32) * scale
        s = s + ci[..., None] - c_k[:, :, None, :]
        q_pos = bi * BLOCK + jnp.arange(BLOCK)
        mask = key_pos[None, :] <= q_pos[:, None]
        s = jnp.where(mask, s, -jnp.inf)
        p = jax.nn.softmax(s, axis=-1).astype(v.dtype)
        return jnp.einsum('bhqk,bkhd->bqhd', p, v)

    o = lax.map(one_block, (qb, cb, jnp.arange(nq)))
    return o.transpose(1, 0, 2, 3, 4).reshape(B, S, H, dh)

def fox_mixer(h, w_in, b_f, q_g, k_g):
    B, S, _ = h.shape
    proj = h @ w_in
    q = rms_norm(proj[..., :INNER].reshape(B, S, N_HEADS, HEAD_DIM), q_g)
    k = rms_norm(proj[..., INNER:2 * INNER].reshape(B, S, N_HEADS, HEAD_DIM), k_g)
    v = proj[..., 2 * INNER:3 * INNER].reshape(B, S, N_HEADS, HEAD_DIM)
    gate = proj[..., 3 * INNER:4 * INNER]
    f_logit = proj[..., 4 * INNER:].astype(jnp.float32) + b_f.astype(jnp.float32)
    c = jnp.cumsum(jax.nn.log_sigmoid(f_logit), axis=1)
    o = fox_attention(q, k, v, c)
    return o.reshape(B, S, INNER), gate

def _band(t):
    prev = jnp.concatenate([jnp.zeros_like(t[:, :1]), t[:, :-1]], axis=1)
    return jnp.concatenate([prev, t], axis=2)

def dilated_window_attention(q, k, v, window, dilation):
    B, S, H, dh = q.shape
    r = dilation
    L = S // r
    n_back = window // r
    nb = -(-L // BLOCK)
    Lp = nb * BLOCK
    scale = dh ** -0.5

    def to_blocks(t):
        t = t.reshape(B, L, r, H, dh).transpose(0, 2, 1, 3, 4).reshape(B * r, L, H, dh)
        t = jnp.pad(t, ((0, 0), (0, Lp - L), (0, 0), (0, 0)))
        return t.reshape(B * r, nb, BLOCK, H, dh)

    qb, kb, vb = to_blocks(q), to_blocks(k), to_blocks(v)
    s = jnp.einsum('znqhd,znkhd->znhqk', qb, _band(kb)).astype(jnp.float32) * scale
    q_idx = jnp.arange(nb)[:, None] * BLOCK + jnp.arange(BLOCK)[None, :]
    k_idx = jnp.arange(nb)[:, None] * BLOCK - BLOCK + jnp.arange(2 * BLOCK)[None, :]
    dist = q_idx[:, :, None] - k_idx[:, None, :]
    mask = (dist >= 0) & (dist <= n_back) & (k_idx[:, None, :] >= 0)
    s = jnp.where(mask[None, :, None], s, -jnp.inf)
    lse = jax.nn.logsumexp(s, axis=-1)
    p = jnp.exp(s - lse[..., None]).astype(v.dtype)
    o = jnp.einsum('znhqk,znkhd->znqhd', p, _band(vb))
    o = o.reshape(B * r, Lp, H, dh)[:, :L]
    o = o.reshape(B, r, L, H, dh).transpose(0, 2, 1, 3, 4).reshape(B, S, H, dh)
    lse = lse.transpose(0, 1, 3, 2).reshape(B * r, Lp, H)[:, :L]
    lse = lse.reshape(B, r, L, H).transpose(0, 2, 1, 3).reshape(B, S, H)
    return o, lse

def dsw_mixer(h, cos, sin, w_in, q_g, k_g):
    B, S, _ = h.shape
    proj = h @ w_in
    qkv = proj[..., :3 * N_GROUPS * INNER].reshape(B, S, 3, N_GROUPS, N_HEADS, HEAD_DIM)
    gate = proj[..., 3 * N_GROUPS * INNER:]
    q = apply_partial_rotary(rms_norm(qkv[:, :, 0], q_g[:, None, :]), cos, sin)
    k = apply_partial_rotary(rms_norm(qkv[:, :, 1], k_g[:, None, :]), cos, sin)
    v = qkv[:, :, 2]
    outs, lses = [], []
    for g, (window, dilation) in enumerate(DSWA_GROUPS):
        o_g, lse_g = dilated_window_attention(q[:, :, g], k[:, :, g], v[:, :, g], window, dilation)
        outs.append(o_g)
        lses.append(lse_g)
    wts = jax.nn.softmax(jnp.stack(lses, axis=0), axis=0).astype(v.dtype)
    o = jnp.einsum('gbsh,gbshd->bshd', wts, jnp.stack(outs, axis=0))
    return o.reshape(B, S, INNER), gate

def second_inputs(seed: int = 0) -> dict:
    key = jax.random.key(seed)
    ks = jax.random.split(key, 13)
    n_fox = (DEPTH + 1) // N_MIXERS
    n_dsw = DEPTH // N_MIXERS
    f32 = jnp.float32
    x = jax.random.normal(ks[0], (BATCH, SEQ, D_MODEL), f32)
    offset = jax.random.randint(ks[1], (BATCH, 1), 0, 4096, dtype=jnp.int32)
    positions = offset + jnp.arange(SEQ, dtype=jnp.int32)[None, :]
    norm_g = 1.0 + 0.02 * jax.random.normal(ks[2], (DEPTH, D_MODEL), f32)
    fox_w_in = jax.random.normal(ks[3], (n_fox, D_MODEL, FOX_IN), f32) * D_MODEL ** -0.5
    fox_b_f = jax.random.uniform(ks[4], (n_fox, N_HEADS), f32, minval=1.0, maxval=4.0)
    fox_q_norm = 1.0 + 0.02 * jax.random.normal(ks[5], (n_fox, HEAD_DIM), f32)
    fox_k_norm = 1.0 + 0.02 * jax.random.normal(ks[6], (n_fox, HEAD_DIM), f32)
    fox_w_out = jax.random.normal(ks[7], (n_fox, INNER, D_MODEL), f32) * (2 * INNER) ** -0.5
    dsw_w_in = jax.random.normal(ks[8], (n_dsw, D_MODEL, DSW_IN), f32) * D_MODEL ** -0.5
    dsw_q_norm = 1.0 + 0.02 * jax.random.normal(ks[9], (n_dsw, N_GROUPS, HEAD_DIM), f32)
    dsw_k_norm = 1.0 + 0.02 * jax.random.normal(ks[10], (n_dsw, N_GROUPS, HEAD_DIM), f32)
    dsw_w_out = jax.random.normal(ks[11], (n_dsw, INNER, D_MODEL), f32) * (2 * INNER) ** -0.5
    return {"x": x, "positions": positions, "norm_g": norm_g,
            "fox_w_in": fox_w_in, "fox_b_f": fox_b_f, "fox_q_norm": fox_q_norm,
            "fox_k_norm": fox_k_norm, "fox_w_out": fox_w_out,
            "dsw_w_in": dsw_w_in, "dsw_q_norm": dsw_q_norm, "dsw_k_norm": dsw_k_norm,
            "dsw_w_out": dsw_w_out}

def second_block(x, positions, norm_g, fox_w_in, fox_b_f, fox_q_norm, fox_k_norm, fox_w_out,
              dsw_w_in, dsw_q_norm, dsw_k_norm, dsw_w_out):
    cos, sin = rotary_tables(positions)
    for i in range(DEPTH):
        j = i // N_MIXERS
        h = rms_norm(x, norm_g[i])
        if i % N_MIXERS == 0:
            o, gate = fox_mixer(h, fox_w_in[j], fox_b_f[j], fox_q_norm[j], fox_k_norm[j])
            w_out = fox_w_out[j]
        else:
            o, gate = dsw_mixer(h, cos, sin, dsw_w_in[j], dsw_q_norm[j], dsw_k_norm[j])
            w_out = dsw_w_out[j]
        x = x + (o * jax.nn.silu(gate)) @ w_out
    return x


def setup_inputs(seed=0):
    out = dict(first_inputs(seed))
    for name, value in second_inputs(seed + 1).items():
        if name != "x":
            out[name + "_2"] = value
    return out


def reference(
    x, c, rel_bias, ada_w, ada_b, ln_g, ln_b, ffn_w1, ffn_w3, ffn_w2, w_in, w_out, cmp_pe,
    cmp_w1, cmp_b1, cmp_w2, gmlp_ln_g, gmlp_ln_b, gmlp_ws, gmlp_bs, ssm_conv_w, ssm_conv_b,
    ssm_dt_bias, ssm_a_log, ssm_d, ssm_norm_g, positions_2, norm_g_2, fox_w_in_2, fox_b_f_2,
    fox_q_norm_2, fox_k_norm_2, fox_w_out_2, dsw_w_in_2, dsw_q_norm_2, dsw_k_norm_2,
    dsw_w_out_2,
):
    x = first_block(
        x, c, rel_bias, ada_w, ada_b, ln_g, ln_b, ffn_w1, ffn_w3, ffn_w2, w_in, w_out, cmp_pe,
        cmp_w1, cmp_b1, cmp_w2, gmlp_ln_g, gmlp_ln_b, gmlp_ws, gmlp_bs, ssm_conv_w, ssm_conv_b,
        ssm_dt_bias, ssm_a_log, ssm_d, ssm_norm_g,
    )
    return second_block(
        x, positions_2, norm_g_2, fox_w_in_2, fox_b_f_2, fox_q_norm_2, fox_k_norm_2,
        fox_w_out_2, dsw_w_in_2, dsw_q_norm_2, dsw_k_norm_2, dsw_w_out_2,
    )


_drawn_inputs = setup_inputs


def setup_inputs(seed=0):
    import zlib

    import numpy as np

    out = dict(_drawn_inputs(seed))
    spreads = {}
    factors = {'norm_g_2': 7.638,
     'fox_q_norm_2': 8.0,
     'fox_k_norm_2': 8.0,
     'dsw_q_norm_2': 8.0,
     'dsw_k_norm_2': 8.0}
    for name, (base, spread) in spreads.items():
        noise = np.random.default_rng([zlib.crc32(name.encode()), seed]).standard_normal(out[name].shape)
        drawn = base * np.exp(spread * noise) if base else spread * noise
        out[name] = __import__('jax').numpy.asarray(drawn.astype(out[name].dtype))
    for name, factor in factors.items():
        out[name] = (out[name] * factor).astype(out[name].dtype)
    return out
```

```python
from contextlib import ExitStack

import numpy as np

import concourse.bass as bass
from concourse import mybir

F32 = mybir.dt.float32
F32R = mybir.dt.float32r
I32 = mybir.dt.int32
ALU = mybir.AluOpType
ACT = mybir.ActivationFunctionType
AX = mybir.AxisListType

P = 128
T = 512
TT = T // P
D = 1024
KD = D // P
LAYERS = 2
FF = 2816
KF = FF // P
DOWN = (8, 7, 7)
NSUB = 3
NMOD = NSUB * LAYERS
ALPHA = (2 * LAYERS) ** 0.25
HD = 64
QSCALE = -(HD ** -0.5)
BIG = 1.0e30
NCMP = 31
CMPW = 64
TOEP = 896
REV = 1024
DIST0 = 511
PAIRS = 8
GROUPS = 3

RAW_SLOTS = 4
SPLIT_SLOTS = 3
SLOT = KD * P
ACC_BANKS = 3
STAT_N = 1.0 / D

_COLS = [("ada_b", 2 * 72), ("ln_g", 48), ("ln_b", 48), ("cmp_b1", 8), ("pe", 64), ("conv_w", 48), ("conv_b", 12),
         ("ssm_g", 4), ("gmlp_bs", 8), ("norm2", 16), ("fox_qk", 2), ("dsw_qk", 6),
         ("eps5", 1), ("eps6", 1), ("valid", 1), ("one", 1), ("halfpi", 1), ("c", 8)]
COL = {}
NCOL = 0
for _n, _w in _COLS:
    COL[_n] = NCOL
    NCOL += _w
_ROWS = [("dt_b", 8), ("a_log", 8), ("ssm_d", 8), ("b_f", 16), ("gln_g", 512), ("gln_b", 512),
         ("rot_g", 96), ("invf", 8)]
ROW = {}
NROW = 0
for _n, _w in _ROWS:
    ROW[_n] = NROW
    NROW += _w
_CON = [("ident", 128), ("prev", 128), ("causal", 128), ("blockmask", 128), ("ssm_mask", 128),
        ("tril_t", 128), ("ones", 128)]
CON = {}
NCON = 0
for _n, _w in _CON:
    CON[_n] = NCON
    NCON += _w


class Step:
    def __init__(self, kind, n, before, **f):
        self.kind, self.n = kind, n
        self.before = before
        self.f = f

    def __getitem__(self, k):
        return self.f[k]


class Plan:

    def __init__(self):
        self.steps, self.count = [], {}
        self.units = []
        self.nsplit = 0
        self.acc = 0
        self.last_gemm = {}
        self.reader = {}
        self.pending = []

    def add(self, kind, **f):
        n = self.bump(kind)
        s = Step(kind, n, dict(self.count), **f)
        self.steps.append(s)
        return s

    def bump(self, kind):
        n = self.count.get(kind, 0)
        self.count[kind] = n + 1
        return n

    def new_acc(self):
        self.acc += 1
        return self.acc - 1

    def read(self, a, step, role=0):
        self.reader[a] = (step, role)

    def unit(self, kind, where, width, split=True, **f):
        u = len(self.units)
        s = self.add(kind, u=u, split=self.nsplit if split else None, **f)
        self.units.append((where, width, self.nsplit if split else None, u, kind, s.n))
        if split:
            self.nsplit += 1
        return s


def make_plan():
    p = Plan()

    def gemm(src, form, act, acc, kc=KD, k0=0, nc_=P, start=True, stop=True, deps=None, perm=0):
        s = p.unit("gemm", src, kc * nc_, src=src[0], form=form, act=act, acc=acc, kc=kc, k0=k0, nc=nc_,
                   start=start, stop=stop, reads=deps, perm=perm)
        p.last_gemm[acc] = s.n
        return s

    def ada(k):
        for _ in range(min(k, len(p.pending))):
            m, c = p.pending.pop(0)
            l, s = divmod(m, NSUB)
            p.unit("ada", ("ada", (l, s * 24 + c)), D, split=False, m=m, c=c)
            if c == 23:
                p.add("mod", m=m)

    def queue_mod(m):
        if m < NMOD:
            p.pending += [(m, c) for c in range(24)]

    hcount = [0]

    def norm(center, h, x, stats=True):
        am = ar = None
        if stats:
            if center:
                am = p.new_acc()
            ar = p.new_acc()
        sn = p.bump("norm_stats") if stats else None
        s = p.add("norm", center=center, h=h, x=x, stats=stats, am=am, ar=ar, hn=hcount[0], sn=sn)
        if x is not None:
            p.bump("norm_x")
        if stats:
            if center:
                p.read(am, s)
            p.read(ar, s)
        if h is not None:
            hcount[0] += 1
        return hcount[0] - 1

    def project_out(act, srcs, deps, gate, stats):
        last = None
        for d in range(KD):
            a = p.new_acc()
            for j, (src, kc, k0) in enumerate(srcs(d)):
                gemm(src, "FM", act, a, kc=kc, k0=k0, start=j == 0, stop=j == len(srcs(d)) - 1,
                     deps=deps(j) if d == 0 else None)
            s = p.add("resid", d=d, acc=a, gate=gate, stats=stats)
            p.read(a, s)
            if last is not None and stats:
                p.add("stat", d=last["d"], r=last.n, src="resid", center=gate is not None)
            last = s
        if stats:
            p.add("stat", d=last["d"], r=last.n, src="resid", center=gate is not None)

    def ffn(f, hn, m):
        l, j = divmod(f, 2)
        g0 = p.count.get("gate", 0)
        for t in range(KF):
            a1, a3 = p.new_acc(), p.new_acc()
            gemm(("ffn13", (f, t, 0)), "FM", "h", a1, deps=hn if t == 0 else None)
            gemm(("ffn13", (f, t, 1)), "FM", "h", a3)
            s = p.add("gate", t=t, a1=a1, a3=a3)
            p.read(a1, s, 1)
            p.read(a3, s, 3)
            ada(2 if t < 2 else 1)
        ada(24)
        at = [sum(DOWN[:j]) for j in range(len(DOWN) + 1)]
        project_out("gu", lambda d: [((f"ffn2_{j}", (f, d)), DOWN[j], at[j]) for j in range(len(DOWN))],
                    lambda j: g0 + at[j + 1] - 1, gate=(m, 0.5), stats=True)

    def jobs(js):
        base = p.count.get("scores", 0)
        n = len(js)
        for i in range(n + 3):
            if i < n:
                p.add("scores", **js[i])
            if 0 <= i - 2 < n:
                p.add("turn", **js[i - 2])
            if 0 <= i - 3 < n:
                p.add("values", **js[i - 3])
                g = js[i - 3]["group"]
                if i - 3 == n - 1 or js[i - 2]["group"] != g:
                    e = js[i - 3]["evac"]
                    p.add("heads", j=base + i - 3, nd=p.bump("heads_dsw") if e["fam"] == "dsw" else None, **e)
        return base

    gcount = [0]

    def group(js, evac):
        g = gcount[0]
        gcount[0] += 1
        return [dict(j, group=g, slot=i, evac=dict(evac, g=g)) for i, j in enumerate(js)]

    def mixout(tile, dst, scale=None, pair=None, src="heads", t=0):
        a = p.new_acc()
        s = p.add("mixout", tile=tile, dst=dst, scale=scale, pair=pair, acc=a, src=src, t=t,
                  hin=p.bump("mixout_hi") if pair is None else None)
        p.read(a, s)
        return s

    queue_mod(0)
    p.add("start")
    ada(24)
    hn = norm(False, ("mod", 0), None, stats=False)
    for l in range(LAYERS):
        queue_mod(3 * l + 1)
        ffn(2 * l, hn, 3 * l)
        hn = norm(True, ("mod", 3 * l + 1), 3 * l)

        queue_mod(3 * l + 2)
        a = p.new_acc()
        gemm(("small", (l,)), "TM", "h", a, nc_=28, deps=hn)
        s = p.add("gd", l=l, acc=a)
        p.read(a, s)
        for c in range(22):
            a = p.new_acc()
            tm = c in (7, 9) or 10 <= c < 16
            gemm(("win", (l, c)), "TM" if tm else "FM", "h", a)
            s = p.add("proj", l=l, c=c, acc=a)
            p.read(a, s)
            ada(2)
        ada(24)
        for j in range(2):
            a0, a1 = p.new_acc(), p.new_acc()
            for q in range(4):
                p.unit("cmp", ("cmp1", (l, j, q)), 1024, split=False, l=l, j=j, q=q, a0=a0, a1=a1)
            s = p.add("cmph", l=l, j=j, a0=a0, a1=a1)
            p.read(a0, s)
            p.read(a1, s)
            a = p.new_acc()
            s = p.add("cmpo", l=l, j=j, acc=a)
            p.read(a, s)
        for hp in range(4):
            if hp < 3:
                p.add("toep", l=l, hp=hp + 1)
            js = []
            for hh in range(2):
                for br in range(3):
                    js += group([dict(fam="nsa", l=l, h=2 * hp + hh, br=br, i=i) for i in range(TT)],
                                dict(fam="nsa", h=2 * hp + hh, br=br, l=l))
            jobs(js)
            mixout(hp, "h")
        p.add("gln", l=l)
        a = [p.new_acc() for _ in range(2)]
        s = p.add("gsp", l=l, acc=a)
        p.read(a[0], s, 0)
        p.read(a[1], s, 1)
        for t in range(2):
            mixout(4 + t, "h", src="gmlp", t=t)
        a = p.new_acc()
        a2 = p.new_acc()
        s = p.add("cs", l=l, acc=a, acc2=a2)
        p.read(a, s, 0)
        p.read(a2, s, 1)
        for t in range(2):
            a = p.new_acc()
            s = p.add("xtok", l=l, t=t, acc=a)
            p.read(a, s)
        for g in range(2):
            for hh in range(2):
                s = p.add("ssb", l=l, g=g, h=2 * g + hh)
                for i in range(TT):
                    a = p.new_acc()
                    sc = p.add("sss", l=l, g=g, h=2 * g + hh, i=i, acc=a, b=s.n)
                    p.read(a, sc)
                    if i > 0:
                        p.add("ssy", **last_sss)
                    last_sss = dict(h=2 * g + hh, i=i, k=sc.n, hh=hh)
                p.add("ssy", **last_sss)
                p.add("ssg", l=l, h=2 * g + hh, hh=hh, g=g)
            p.add("ssn", l=l, g=g)
            mixout(6 + g, "h", scale=("ssm_g", 2 * l + g), src="ssm")
        mo = p.count["mixout"]
        project_out("h", lambda d: [(("wout", (l, d)), KD, 0)], lambda j: mo - 1,
                    gate=(3 * l + 1, 1.0), stats=True)
        hn = norm(True, ("mod", 3 * l + 2), 3 * l + 1)

        queue_mod(3 * l + 3)
        ffn(2 * l + 1, hn, 3 * l + 2)
        if l == 0:
            hn = norm(True, ("mod", 3), 2)
        else:
            norm(True, None, 5)
            for d in range(KD):
                p.add("sqx", d=d)
                if d:
                    p.add("stat", d=d - 1, r=d - 1, src="sqx", center=False)
            p.add("stat", d=KD - 1, r=KD - 1, src="sqx", center=False)
    hn = norm(False, ("rms", 0), None)
    a = p.new_acc()
    a2 = p.new_acc()
    gemm(("foxf", ()), "TM", "h", a, nc_=16, deps=hn)
    s = p.add("fgate", acc=a, acc2=a2)
    p.read(a, s, 0)
    p.read(a2, s, 1)

    def qk(src, which, col, rot, deps=None):
        a, a2 = p.new_acc(), p.new_acc()
        gemm(src, "TM", "h", a, deps=deps)
        s = p.add("qkn", acc=a, acc2=a2, which=which, col=col, rot=rot,
                  rn=None if rot is None else p.bump("rotated"))
        p.read(a, s, 0)
        p.read(a2, s, 1)

    def vproj(src, slot, perm):
        a = p.new_acc()
        gemm(src, "TM", "h", a, perm=perm)
        s = p.add("vcopy", slot=slot, acc=a)
        p.read(a, s)

    def gproj(src):
        a = p.new_acc()
        gemm(src, "FM", "h", a)
        s = p.add("sgate", acc=a)
        p.read(a, s)

    for hp in range(PAIRS):
        qk(("fox", (hp,)), ("q", 0), ("fox_qk", 0), None)
        qk(("fox", (8 + hp,)), ("k", 0), ("fox_qk", 1), None)
        vproj(("fox", (16 + hp,)), 0, 0)
        gproj(("fox", (24 + hp,)))
        for hh in range(2):
            a = p.new_acc()
            s = p.add("fbias", h=2 * hp + hh, hh=hh, acc=a)
            p.read(a, s)
        js = []
        for hh in range(2):
            js += group([dict(fam="fox", hh=hh, i=i, pair=hp) for i in range(TT)], dict(fam="fox", hh=hh, pair=hp))
        jobs(js)
        mixout(hp, "mix", pair=hp)
    mo = p.count["mixout"]
    project_out("mix", lambda d: [(("foxo", (d,)), KD, 0)], lambda j: mo - 1,
                gate=None, stats=True)
    hn = norm(False, ("rms", 1), None)
    hd = hn
    p.add("rot")
    for hp in range(PAIRS):
        for g in range(GROUPS):
            qk(("dsw", (g * 8 + hp,)), ("q", g), ("dsw_qk", g), g, hd)
            hd = None
            qk(("dsw", (24 + g * 8 + hp,)), ("k", g), ("dsw_qk", 3 + g), 3 + g)
            vproj(("dsw", (48 + g * 8 + hp,)), g, g)
        gproj(("dsw", (72 + hp,)))
        for g in range(GROUPS):
            js = []
            for hh in range(2):
                js += group([dict(fam="dsw", dg=g, hh=hh, i=i, pair=hp) for i in range(TT)],
                            dict(fam="dsw", dg=g, hh=hh, pair=hp))
            jobs(js)
            a, a2 = p.new_acc(), p.new_acc()
            s = p.add("unperm", dg=g, acc=a, acc2=a2)
            p.read(a, s, 0)
            p.read(a2, s, 1)
        p.add("blend", tile=hp)
    mo = p.count["blend"]
    project_out("mix", lambda d: [(("dswo", (d,)), KD, 0)], lambda j: mo - 1,
                gate=None, stats=False)
    p.add("finish")
    return p


def proj_on_act(c):
    return c < 4 or 10 <= c < 22


def proj_ordinal(l, c):
    cs = [x for x in range(22) if proj_on_act(x) == proj_on_act(c)]
    return l * len(cs) + cs.index(c)


def program(nc, A, out):
    plan = make_plan()
    units = plan.units
    with ExitStack() as ctx:
        def sb(name, shape, dt=F32):
            return ctx.enter_context(nc.sbuf_tensor(name, shape, dt))

        def sem(name):
            return ctx.enter_context(nc.semaphore(name))

        x = sb("x", [P, KD, T])
        act_hi = {"h": sb("h_hi", [P, KD, T], F32R)}
        act_lo = {"h": sb("h_lo", [P, KD, T], F32R)}
        raw = [sb(f"raw{i}", [P, SLOT]) for i in range(RAW_SLOTS)]
        w_hi = [sb(f"w_hi{i}", [P, SLOT], F32R) for i in range(SPLIT_SLOTS)]
        w_lo = [sb(f"w_lo{i}", [P, SLOT], F32R) for i in range(SPLIT_SLOTS)]
        cols = sb("cols", [P, NCOL])
        rows = sb("rows", [P, NROW])
        con = sb("con", [P, NCON])
        mod = sb("mod", [P, NMOD, 24])
        modg = sb("modg", [P, NMOD, 16])
        csil = sb("csil", [P, KD])
        st = sb("st", [P, 8])
        st2 = sb("st2", [P, 8])
        tmp_a = [sb(f"tmp_a{i}", [P, T]) for i in range(2)]
        tmp_b = [sb(f"tmp_b{i}", [P, T]) for i in range(2)]
        tmp_h = [sb(f"tmp_h{i}", [P, T]) for i in range(2)]

        def col(name, i=0, n=1):
            return cols[:, COL[name] + i:COL[name] + i + n]

        def row(name, i, n):
            return rows[:, ROW[name] + i:ROW[name] + i + n]

        def cst(name):
            return con[:, CON[name]:CON[name] + P]

        ident = cst("ident")

        with ExitStack() as one:
            act_hi["gu"] = one.enter_context(nc.sbuf_tensor("gu_hi", [P, KF, T], F32R))
            act_lo["gu"] = one.enter_context(nc.sbuf_tensor("gu_lo", [P, KF, T], F32R))
        with ExitStack() as one:
            def ph(name, shape, dt=F32):
                return one.enter_context(nc.sbuf_tensor(name, shape, dt))

            sT = [ph(f"scores{i}", [P, T]) for i in range(2)]
            pT = [ph(f"probs{i}", [P, T]) for i in range(3)]
            ptT = [ph(f"probs_t{i}", [P, T]) for i in range(2)]
            mn = ph("row_min", [P, 8, 4])
            zs = ph("row_sum", [P, 8, 4])
            opair = ph("opair", [P, TT, P])
            otmp = ph("otmp", [P, TT, HD])
            rz = ph("rz", [P, 8])
            with ExitStack() as two:
                def p1(name, shape, dt=F32):
                    return two.enter_context(nc.sbuf_tensor(name, shape, dt))

                q1 = p1("q1", [P, 4, T])
                kd = p1("kd", [P, 4, T])
                v1 = p1("v1", [P, 2, TT, P])
                gates = p1("gates", [P, TT, 24])
                dts = p1("dts", [P, TT, 8])
                dtmp = p1("dtmp", [P, TT, 4])
                dtmp2 = p1("dtmp2", [P, TT, 4])
                toep = p1("toep_bias", [P, 2, 2, TOEP])
                ug = p1("ug", [P, TT, 256])
                vg = p1("vg", [P, TT, 256])
                zg = p1("zg", [P, TT, 256])
                xbc = p1("xbc", [P, 6, T])
                xpad = p1("xpad", [P, T + 3])
                cmpr = p1("cmpr", [P, 2, 16, CMPW])
                b1c = p1("b1c", [P, 2])
                hid = p1("hid", [P, 2, 62])
                cw2 = p1("cw2", [P, 2, 192])
                kc = p1("kc", [P, 2, NCMP])
                vc = p1("vc", [NCMP, 2, HD])
                gw = p1("gw", [P, 4, P])
                bn = p1("bn", [P, TT, 6])
                mv = p1("mv", [P, TT, 2])
                gstd = p1("gstd", [P, TT])
                gm = p1("gm", [P, TT, 256])
                csr = p1("csr", [4, T])
                csc = p1("csc", [P, TT, 4])
                xtok = q1[:, 0:2, :].rearrange("p a (t c) -> p (a t) c", t=2)
                xdt = q1[:, 2:4, :].rearrange("p a (t c) -> p (a t) c", t=2)
            with ExitStack() as two:
                def p2(name, shape, dt=F32):
                    return two.enter_context(nc.sbuf_tensor(name, shape, dt))

                act_hi["mix"] = p2("mix_hi", [P, KD, T], F32R)
                act_lo["mix"] = p2("mix_lo", [P, KD, T], F32R)
                q2 = p2("q2", [P, GROUPS, T])
                k2 = p2("k2", [P, GROUPS, T])
                v2 = p2("v2", [P, GROUPS, TT, P])
                sg = p2("sg", [P, T])
                qn = p2("qn", [P, TT, P])
                ss = p2("ss", [P, 8])
                ss2 = p2("ss2", [P, 8])
                rt = [p2(f"rt{i}", [P, TT, 2, 8]) for i in range(4)]
                fl = p2("fl", [P, TT, 16])
                fl2 = p2("fl2", [P, TT, 16])
                lse = p2("lse", [P, TT, 2])
                rep = p2("rep", [P, TT, P])
                og = p2("og", [P, GROUPS, T])
                lg = p2("lg", [P, GROUPS, T])
                fb = lg[:, 0:2, :]
                crow = og[0:16, 0, :]
                wsum = p2("wsum", [P, T])
                pos_i = p2("pos_i", [P, TT], I32)
                pos = p2("pos", [P, TT])
                ang = p2("ang", [P, TT, 8])
                an2 = p2("an2", [P, TT, 8])
                cs8 = p2("cs8", [P, 2, TT, 8])
                rtab = p2("rtab", [P, 6, 4, TT, 8])
            del two
        with ExitStack() as one:
            rel = one.enter_context(nc.sbuf_tensor("rel", [33, 8], F32))
            onehot = one.enter_context(nc.sbuf_tensor("onehot", [33, REV], F32))
            revs = one.enter_context(nc.sbuf_tensor("revs", [P, 8, REV], F32))
        rev_d = nc.dram_tensor("rev_scratch", (8, P, REV), F32)

        acc_bank = [ctx.enter_context(nc.psum_tensor(f"acc{i}", [P, 512], F32)) for i in range(ACC_BANKS)]
        s_bank = [ctx.enter_context(nc.psum_tensor(f"sps{i}", [P, 512], F32)) for i in range(2)]
        pt_bank = ctx.enter_context(nc.psum_tensor("ptps", [P, 512], F32))
        o_bank = ctx.enter_context(nc.psum_tensor("ops", [P, 512], F32))
        m_bank = ctx.enter_context(nc.psum_tensor("mps", [P, 512], F32))

        head_bank = [o_bank, m_bank]

        def acc(a):
            return acc_bank[a % ACC_BANKS]

        def perm_tiles(ap, g):
            if g == 0:
                return ap.rearrange("p (t j) -> p t j", t=TT)
            return ap.rearrange("p (j t) -> p t j", t=TT)

        s_raw = [sem(f"raw{i}") for i in range(RAW_SLOTS)]
        s_toep = [sem(f"toep{i}") for i in range(2)]
        s_act_chain = sem("act_chain")
        s_ada_mm = sem("ada_mm")
        s_blend_exp = sem("blend_exp")
        s_blend_out = sem("blend_out")
        s_blend_sub = sem("blend_sub")
        s_cmp_mm = sem("cmp_mm")
        s_cmph_act = sem("cmph_act")
        s_cmph_b = sem("cmph_b")
        s_cmpo_mm = sem("cmpo_mm")
        s_cmpo_out = sem("cmpo_out")
        s_const = sem("const")
        s_conv = sem("conv")
        s_cs_back = sem("cs_back")
        s_cs_col = sem("cs_col")
        s_cs_mm = sem("cs_mm")
        s_cs_scan = sem("cs_scan")
        s_csil = sem("csil")
        s_dve_chain = sem("dve_chain")
        s_fbias_mm = sem("fbias_mm")
        s_fbias_out = sem("fbias_out")
        s_fgate_ln = sem("fgate_ln")
        s_fgate_ls = sem("fgate_ls")
        s_fgate_mm = sem("fgate_mm")
        s_fgate_scan = sem("fgate_scan")
        s_fgate_x = sem("fgate_x")
        s_gate_lo = sem("gate_lo")
        s_gate_mul = sem("gate_mul")
        s_gate_silu = sem("gate_silu")
        s_gd_a = sem("gd_a")
        s_gd_ln = sem("gd_ln")
        s_gd_x = sem("gd_x")
        s_gemm_mm = sem("gemm_mm")
        s_gln_mv = sem("gln_mv")
        s_gln_out = sem("gln_out")
        s_gln_std = sem("gln_std")
        s_gsp_mm = sem("gsp_mm")
        s_gsp_out = sem("gsp_out")
        s_h_act = sem("h_act")
        s_h_hi = sem("h_hi")
        s_h_lo = sem("h_lo")
        s_heads_done = sem("heads_done")
        s_heads_ln = sem("heads_ln")
        s_heads_rz = sem("heads_rz")
        s_mixout_hi = sem("mixout_hi")
        s_mixout_lo = sem("mixout_lo")
        s_mixout_mm = sem("mixout_mm")
        s_mod_done = sem("mod_done")
        s_norm_bc = sem("norm_bc")
        s_norm_r = sem("norm_r")
        s_norm_std = sem("norm_std")
        s_norm_t = sem("norm_t")
        s_norm_var = sem("norm_var")
        s_norm_x = sem("norm_x")
        s_p_ready = sem("p_ready")
        s_pos_dma = sem("pos_dma")
        s_proj_act = sem("proj_act")
        s_proj_dve = sem("proj_dve")
        s_pt_copied = sem("pt_copied")
        s_qkn_mm = sem("qkn_mm")
        s_qkn_out = sem("qkn_out")
        s_qkn_qn = sem("qkn_qn")
        s_qkn_rot = sem("qkn_rot")
        s_qkn_sq = sem("qkn_sq")
        s_qkn_ss = sem("qkn_ss")
        s_qkn_std = sem("qkn_std")
        s_rel_big = sem("rel_big")
        s_resid_y = sem("resid_y")
        s_resid_z = sem("resid_z")
        s_rev_copy = sem("rev_copy")
        s_rev_dma = sem("rev_dma")
        s_rev_mm = sem("rev_mm")
        s_rot_ang = sem("rot_ang")
        s_rot_cs = sem("rot_cs")
        s_s_ready = sem("s_ready")
        s_scores_mm = sem("scores_mm")
        s_sgate_out = sem("sgate_out")
        s_small_dma = sem("small_dma")
        s_square = sem("square")
        s_ssb_mask = sem("ssb_mask")
        s_ssb_mm = sem("ssb_mm")
        s_ssg_out = sem("ssg_out")
        s_ssn_out = sem("ssn_out")
        s_ssn_sq = sem("ssn_sq")
        s_ssn_std = sem("ssn_std")
        s_ssn_sum = sem("ssn_sum")
        s_sss_e = sem("sss_e")
        s_sss_mm = sem("sss_mm")
        s_sss_mul = sem("sss_mul")
        s_ssy_mm = sem("ssy_mm")
        s_stat_mm = sem("stat_mm")
        s_stored = sem("stored")
        s_turn_mm = sem("turn_mm")
        s_unperm_l = sem("unperm_l")
        s_unperm_mm = sem("unperm_mm")
        s_unperm_o = sem("unperm_o")
        s_values_mm = sem("values_mm")
        s_vcopy_out = sem("vcopy_out")
        s_w_hi = sem("w_hi")
        s_w_lo = sem("w_lo")
        s_xbc = sem("xbc")
        s_xdt = sem("xdt")
        s_xtok_copy = sem("xtok_copy")
        s_xtok_mm = sem("xtok_mm")
        block = ctx.enter_context(nc.Block())

        def chain_of(eng, s_chain):
            count = [0]

            def link(ins):
                count[0] += 1
                ins.then_inc(s_chain, 1)
                eng.wait_ge(s_chain, count[0])
            return link

        n_const = 6

        def job_q(s):
            if s["fam"] == "nsa":
                b = (s["h"] % 2) * HD
                return q1[b:b + HD, s["h"] // 2, s["i"] * P:(s["i"] + 1) * P]
            b = s["hh"] * HD
            if s["fam"] == "fox":
                return q2[b:b + HD, 0, s["i"] * P:(s["i"] + 1) * P]
            return perm_tiles(q2[b:b + HD, s["dg"], :], s["dg"])[:, s["i"]]

        def job_k(s):
            i = s["i"]
            if s["fam"] == "nsa":
                b, g = (s["h"] % 2) * HD, s["h"] // 4
                if s["br"] == 0:
                    return kc[b:b + HD, g, :]
                return kd[b:b + HD, (s["br"] - 1) * 2 + g, 0:(i + 1) * P]
            b = s["hh"] * HD
            if s["fam"] == "fox":
                return k2[b:b + HD, 0, 0:(i + 1) * P]
            if s["dg"] == 0:
                return k2[b:b + HD, 0, max(i - 1, 0) * P:(i + 1) * P]
            return perm_tiles(k2[b:b + HD, s["dg"], :], s["dg"])[:, i]

        def job_len(s):
            i = s["i"]
            if s["fam"] == "nsa":
                return NCMP if s["br"] == 0 else (i + 1) * P
            if s["fam"] == "fox":
                return (i + 1) * P
            return 2 * P if s["dg"] == 0 and i > 0 else P

        def job_bias(s):
            i, n = s["i"], job_len(s)
            if s["fam"] == "nsa":
                t = toep[:, (s["h"] // 2) % 2, s["h"] % 2, :]
                if s["br"] == 0:
                    at = 415 - i * P
                    return t[:, at:at + 16 * (NCMP - 1) + 1:16]
                return t[:, 384 - i * P:384 - i * P + n]
            if s["fam"] == "fox":
                return fb[:, s["hh"], 0:n]
            if s["dg"] == 0:
                return con[:, CON["causal"] + P - n:CON["causal"] + P]
            return cst("causal") if s["dg"] == 1 else cst("blockmask")

        def job_v(s):
            i = s["i"]
            if s["fam"] == "nsa":
                g = s["h"] // 4
                if s["br"] == 0:
                    return [vc[:, g, :]]
                return [v1[:, s["br"] - 1, t, g * HD:(g + 1) * HD] for t in range(i + 1)]
            b = s["hh"] * HD
            if s["fam"] == "fox":
                return [v2[:, 0, t, b:b + HD] for t in range(i + 1)]
            ts = ([i - 1] if s["dg"] == 0 and i > 0 else []) + [i]
            return [v2[:, s["dg"], t, b:b + HD] for t in ts]

        def o_slot(s):
            return head_bank[s["group"] % 2][:, s["slot"] * HD:(s["slot"] + 1) * HD]

        xbc_of = {"x": 0, "B": 2, "C": 4}

        @block.sync
        def _(sp):
            sp.dma_start(cols[:, :], A["cols"]).then_inc(s_const, 16)
            sp.dma_start(con[:, :], A["con"]).then_inc(s_const, 16)
            sp.dma_start(rows[:, :], A["rows"].partition_broadcast(P)).then_inc(s_const, 16)
            sp.dma_start(x[:, :, :], A["x"]).then_inc(s_const, 16)
            sp.dma_start(onehot[:, :], A["onehot"]).then_inc(s_const, 16)
            sp.dma_start(rel[0:32, :], A["rel_bias"]).then_inc(s_const, 16)
            for src, width, split, u, kind, n in units:
                slot = u % RAW_SLOTS
                if u >= RAW_SLOTS:
                    _, _, s0, _, k0, n0 = units[u - RAW_SLOTS]
                    if k0 == "gemm":
                        sp.wait_ge(s_w_lo, s0 + 1)
                    elif k0 == "ada":
                        sp.wait_ge(s_ada_mm, n0 + 1)
                    else:
                        sp.wait_ge(s_cmp_mm, n0 + 1)
                name, idx = src
                ap = A[name]
                for i in idx:
                    ap = ap[i]
                sp.dma_start(raw[slot][:, 0:width], ap).then_inc(s_raw[slot], 16)
            for d in range(KD):
                sp.wait_ge(s_resid_z, plan.count["resid"] - KD + d + 1)
                sp.dma_start(out[d], x[:, d, :]).then_inc(s_stored, 16)
            sp.wait_ge(s_stored, 16 * KD)

        def loaded(eng, u):
            eng.wait_ge(s_raw[u % RAW_SLOTS], 16 * (u // RAW_SLOTS + 1))

        splits = [(u, width) for (_, width, s, u, _, _) in units if s is not None]
        ahead, k = [], 0
        for u in range(len(units)):
            while k < len(splits) and splits[k][0] <= u:
                k += 1
            m = k
            while m < min(k + 2, len(splits)) and splits[m][0] <= u + RAW_SLOTS - 1:
                m += 1
            ahead.append(max(m - 1, ahead[-1] if ahead else 0))

        @block.gpsimd
        def _(pool):
            def w_low(k):
                u, width = splits[k]
                pool.wait_ge(s_w_hi, k + 1)
                nc.gpsimd.tensor_tensor(w_lo[k % SPLIT_SLOTS][:, 0:width], raw[u % RAW_SLOTS][:, 0:width],
                                            w_hi[k % SPLIT_SLOTS][:, 0:width].bitcast(F32), ALU.subtract).then_inc(s_w_lo, 1)

            def h_low(s):
                for d in range(KD):
                    n = s["hn"] * KD + d
                    pool.wait_ge(s_h_hi, n + 1)
                    nc.gpsimd.tensor_tensor(act_lo["h"][:, d, :], tmp_h[d % 2][:, :],
                                                act_hi["h"][:, d, :].bitcast(F32), ALU.subtract).then_inc(s_h_lo, 1)

            low_at = 0
            for s in plan.steps:
                if s.kind in ("gemm", "ada", "cmp"):
                    while low_at <= ahead[s["u"]]:
                        w_low(low_at)
                        low_at += 1
                elif s.kind == "norm" and s["h"] is not None:
                    h_low(s)

        @block.scalar
        def _(act):
            link = chain_of(act, s_act_chain)
            A_ = nc.scalar.activation
            act.wait_ge(s_const, 16 * n_const)
            hi_at = [0]

            def w_high_up_to(k):
                while hi_at[0] <= k:
                    j = hi_at[0]
                    u, width = splits[j]
                    loaded(act, u)
                    if j >= SPLIT_SLOTS:
                        act.wait_ge(s_gemm_mm, j - SPLIT_SLOTS + 1)
                    A_(w_hi[j % SPLIT_SLOTS][:, 0:width], raw[u % RAW_SLOTS][:, 0:width], ACT.Copy).then_inc(s_w_hi, 1)
                    hi_at[0] += 1

            def start(s):
                A_(csil[:, :], col("c", 0, KD), ACT.Silu).then_inc(s_csil, 1)
                act.wait_ge(s_rev_copy, 16)
                act.dma_start(rev_d.rearrange("h p c -> p h c"), revs[:, :, :]).then_inc(s_rev_dma, 16)
                act.wait_ge(s_rev_dma, 16)

            def load_toep(l, hp):
                n = l * 4 + hp
                for hh in range(2):
                    src = bass.AP(rev_d, (2 * hp + hh) * P * REV + P - 1, [[REV - 1, P], [1, TOEP]])
                    act.dma_start(toep[:, hp % 2, hh, :], src).then_inc(s_toep[hp % 2], 16)
                return n

            def unit(s):
                w_high_up_to(ahead[s["u"]])

            def gate(s):
                n = s.n
                act.wait_ge(s_gemm_mm, plan.last_gemm[s["a1"]] + 1)
                if n >= 2:
                    act.wait_ge(s_gate_mul, n - 1)
                A_(tmp_a[n % 2][:, :], acc(s["a1"])[:, :], ACT.Silu).then_inc(s_gate_silu, 1)

            def resid(s):
                n, d = s.n, s["d"]
                act.wait_ge(s_gemm_mm, plan.last_gemm[s["acc"]] + 1)
                if s["gate"] is not None:
                    m, w = s["gate"]
                    act.wait_ge(s_mod_done, m + 1)
                    if n >= 2:
                        act.wait_ge(s_resid_z, n - 1)
                    A_(tmp_a[n % 2][:, :], acc(s["acc"])[:, :], ACT.Identity,
                           scale=mod[:, m, 16 + d:17 + d]).then_inc(s_resid_y, 1)
                if s["stats"]:
                    act.wait_ge(s_resid_z, n + 1)
                    square(d)

            squares = [0]

            def square(d):
                j = squares[0]
                if j >= 2:
                    act.wait_ge(s_stat_mm, j - 1)
                A_(tmp_b[j % 2][:, :], x[:, d, :], ACT.Square).then_inc(s_square, 1)
                squares[0] += 1

            def sqx(s):
                act.wait_ge(s_norm_x, s.before["norm_x"] * KD)
                square(s["d"])

            def norm(s):
                hx = s["h"]
                if s["stats"]:
                    act.wait_ge(s_norm_var, s["sn"] + 1)
                    A_(st2[:, 0:4], st2[:, 4:8], ACT.Sqrt,
                           bias=col("eps5") if s["center"] else col("eps6")).then_inc(s_norm_std, 1)
                if hx is not None:
                    for d in range(KD):
                        n = s["hn"] * KD + d
                        if n >= 2:
                            act.wait_ge(s_h_lo, n - 1)
                        if s["stats"]:
                            act.wait_ge(s_norm_t, s["sn"] * KD + d + 1)
                        if hx[0] == "mod":
                            m = hx[1]
                            if d == 0:
                                act.wait_ge(s_mod_done, m + 1)
                            A_(tmp_h[d % 2][:, :], x[:, d, :], ACT.Identity,
                                   scale=modg[:, m, d:d + 1], bias=modg[:, m, 8 + d:9 + d]).then_inc(s_h_act, 1)
                        else:
                            A_(tmp_h[d % 2][:, :], tmp_a[d % 2][:, :], ACT.Identity,
                                   scale=col("norm2", hx[1] * KD + d)).then_inc(s_h_act, 1)
                if s["x"] is not None:
                    for d in range(KD):
                        if hx is None:
                            act.wait_ge(s_norm_t, s["sn"] * KD + d + 1)
                        else:
                            act.wait_ge(s_h_act, s["hn"] * KD + d + 1)
                        A_(x[:, d, :], x[:, d, :], ACT.Identity, scale=col("ln_g", s["x"] * KD + d),
                               bias=col("ln_b", s["x"] * KD + d)).then_inc(s_norm_x, 1)

            def gd(s):
                l = s["l"]
                act.wait_ge(s_gemm_mm, plan.last_gemm[s["acc"]] + 1)
                ps = acc(s["acc"])[:, 0:TT * 28].rearrange("p (t c) -> p t c", t=TT)
                act.wait_ge(s_gd_x, s.n + 1)
                link(A_(gates[:, :, :], ps[:, :, 0:24], ACT.Sigmoid))
                link(A_(dtmp2[:, :, :], dtmp[:, :, :], ACT.Abs))
                link(A_(dtmp2[:, :, :], dtmp2[:, :, :], ACT.Exp, scale=-1.0))
                link(A_(dtmp2[:, :, :], dtmp2[:, :, :], ACT.Ln, bias=1.0))
                A_(row("a_log", 4 * l, 4), row("a_log", 4 * l, 4), ACT.Exp).then_inc(s_gd_ln, 1)
                act.dma_start(cw2[:, :, :], A["cmp2"][l]).then_inc(s_small_dma, 16)
                act.dma_start(gw[:, :, :], A["gws"][l]).then_inc(s_small_dma, 16)
                load_toep(l, 0)

            def proj(s):
                l, c = s["l"], s["c"]
                ps = acc(s["acc"])
                if not proj_on_act(c):
                    return
                act.wait_ge(s_gemm_mm, plan.last_gemm[s["acc"]] + 1)
                if c < 4:
                    A_(q1[:, c, :], ps[:, :], ACT.Copy, scale=QSCALE).then_inc(s_proj_act, 1)
                elif c < 16:
                    dst = (ug, vg, zg)[(c - 10) // 2][:, :, (c % 2) * P:(c % 2 + 1) * P]
                    src = ps[:, :].rearrange("p (t c) -> p t c", t=TT)
                    A_(dst, src, ACT.Silu if c >= 14 else ACT.Gelu_apprx_tanh).then_inc(s_proj_act, 1)
                else:
                    k = l * 6 + c - 16
                    if k >= 1:
                        act.wait_ge(s_conv, k)
                    A_(xpad[:, 3:T + 3], ps[:, :], ACT.Copy).then_inc(s_proj_act, 1)
                    act.wait_ge(s_conv, k + 1)
                    A_(xbc[:, c - 16, :], xbc[:, c - 16, :], ACT.Silu,
                           bias=col("conv_b", l * 6 + c - 16)).then_inc(s_xbc, 1)

            def cmph(s):
                act.wait_ge(s_cmph_b, s.n + 1)
                if s.n >= 1:
                    act.wait_ge(s_cmpo_mm, s.n)
                link(A_(hid[:, 0, :], acc(s["a0"])[:, 0:62], ACT.Gelu_apprx_tanh, bias=b1c[:, 0:1]))
                A_(hid[:, 1, :], acc(s["a1"])[:, 0:62], ACT.Gelu_apprx_tanh, bias=b1c[:, 1:2]).then_inc(s_cmph_act, 1)

            def toep_step(s):
                act.wait_ge(s_s_ready, s.before.get("scores", 0))
                load_toep(s["l"], s["hp"])

            def softmax(s):
                j, L = s.n, job_len(s)
                g, i = s["group"] % 8, s["slot"]
                act.wait_ge(s_s_ready, j + 1)
                if j >= 3:
                    act.wait_ge(s_turn_mm, j - 2)
                if s["slot"] == 0 and s["group"] >= 8:
                    act.wait_ge(s_heads_done, s["group"] - 7)
                A_(pT[j % 3][:, 0:L], sT[j % 2][:, 0:L], ACT.Exp, scale=-1.0,
                       bias=mn[:, g, i:i + 1], accum_out=zs[:, g, i:i + 1]).then_inc(s_p_ready, 1)

            def copy_pt(s):
                j, L = s.n, job_len(s)
                nb, K = (L + P - 1) // P, min(L, P)
                act.wait_ge(s_turn_mm, j + 1)
                if j >= 2:
                    act.wait_ge(s_values_mm, j - 1)
                A_(ptT[j % 2][0:K, 0:nb * P], pt_bank[0:K, 0:nb * P], ACT.Copy).then_inc(s_pt_copied, 1)

            def heads(s):
                if s["fam"] == "dsw":
                    g = s["g"] % 8
                    act.wait_ge(s_p_ready, s["j"] + 1)
                    act.wait_ge(s_heads_rz, s["nd"] + 1)
                    A_(rz[:, 4:8], zs[:, g, :], ACT.Ln).then_inc(s_heads_ln, 1)

            def mixout(s):
                n, t, dst = s.n, s["tile"], s["dst"]
                act.wait_ge(s_mixout_mm, n + 1)
                if s["pair"] is not None:
                    return
                sc = col(*s["scale"]) if s["scale"] else col("one")
                A_(act_hi[dst][:, t, :], acc(s["acc"])[:, :], ACT.Identity, scale=sc).then_inc(s_mixout_hi, 1)

            def sss_exp(s):
                b, i, h = s["b"], s["i"], s["h"]
                k = s.n
                ps = s_bank[b % 2]
                if i == 0:
                    act.wait_ge(s_ssb_mask, b + 1)
                    act.wait_ge(s_cs_col, s["l"] + 1)
                if k >= 2:
                    act.wait_ge(s_sss_mul, k - 1)
                E = sT[k % 2]
                diag = ptT[0][:, i * P:(i + 1) * P]
                if i == TT - 1:
                    A_(E[:, 0:P], diag, ACT.Exp, bias=csc[:, i, h:h + 1]).then_inc(s_sss_e, 1)
                else:
                    link(A_(E[:, 0:P], diag, ACT.Exp, bias=csc[:, i, h:h + 1]))
                    A_(E[:, P:(TT - i) * P], ps[:, (i + 1) * P:T], ACT.Exp, bias=csc[:, i, h:h + 1]).then_inc(s_sss_e, 1)

            def xtok_(s):
                n, t = s.n, s["t"]
                act.wait_ge(s_xtok_mm, n + 1)
                A_(xtok[:, :, t * P:(t + 1) * P], acc(s["acc"])[:, :].rearrange("p (t c) -> p t c", t=TT),
                       ACT.Copy).then_inc(s_xtok_copy, 1)

            def ssn(s):
                act.wait_ge(s_ssg_out, 2 * s.n + 1 + 1)
                A_(tmp_a[0][:, :], opair[:, :, :].rearrange("p t c -> p (t c)"), ACT.Square).then_inc(s_ssn_sq, 1)
                act.wait_ge(s_ssn_sum, s.n + 1)
                A_(gstd[:, :], mv[:, :, 0], ACT.Sqrt, scale=1.0 / P, bias=col("eps5")).then_inc(s_ssn_std, 1)

            def gln(s):
                act.wait_ge(s_gln_mv, s.n + 1)
                A_(gstd[:, :], mv[:, :, 1], ACT.Sqrt, bias=col("eps5")).then_inc(s_gln_std, 1)

            def fgate(s):
                act.wait_ge(s_fgate_x, 1)
                link(A_(fl2[:, :, :], fl[:, :, :], ACT.Abs))
                link(A_(fl2[:, :, :], fl2[:, :, :], ACT.Exp, scale=-1.0))
                A_(fl2[:, :, :], fl2[:, :, :], ACT.Ln, bias=1.0).then_inc(s_fgate_ln, 1)

            def fbias(s):
                n = s.n
                act.wait_ge(s_fbias_mm, n + 1)
                if n >= 2:
                    act.wait_ge(s_s_ready, s.before.get("scores", 0))
                A_(fb[:, s["hh"], :], acc(s["acc"])[:, :], ACT.Copy).then_inc(s_fbias_out, 1)

            def qkn(s):
                n = s.n
                act.wait_ge(s_gemm_mm, plan.last_gemm[s["acc"]] + 1)
                A_(tmp_a[0][:, :], acc(s["acc"])[:, :], ACT.Square).then_inc(s_qkn_sq, 1)
                act.wait_ge(s_qkn_ss, n + 1)
                A_(ss2[:, :], ss[:, :], ACT.Sqrt, scale=1.0 / HD, bias=col("eps6")).then_inc(s_qkn_std, 1)
                act.wait_ge(s_qkn_mm, n + 1)
                which, g = s["which"]
                if s.before.get("scores", 0):
                    act.wait_ge(s_scores_mm, s.before.get("scores", 0))
                sc = col(*s["col"])
                dst = (q2 if which == "q" else k2)[:, g, :]
                A_(dst, acc(s["acc2"])[:, :], ACT.Identity, scale=sc).then_inc(s_qkn_out, 1)

            def vcopy(s):
                act.wait_ge(s_gemm_mm, plan.last_gemm[s["acc"]] + 1)
                if s.before.get("scores", 0):
                    act.wait_ge(s_values_mm, s.before.get("scores", 0))
                A_(v2[:, s["slot"], :, :], acc(s["acc"])[:, :].rearrange("p (t c) -> p t c", t=TT),
                       ACT.Copy).then_inc(s_vcopy_out, 1)

            def sgate(s):
                act.wait_ge(s_gemm_mm, plan.last_gemm[s["acc"]] + 1)
                act.wait_ge(s_mixout_lo, s.before["mixout"])
                if s.before.get("blend", 0):
                    act.wait_ge(s_blend_out, s.before["blend"])
                A_(sg[:, :], acc(s["acc"])[:, :], ACT.Silu).then_inc(s_sgate_out, 1)

            def unperm(s):
                n, g = s.n, s["dg"]
                act.wait_ge(s_unperm_mm, 2 * n + 1)
                if n >= GROUPS:
                    act.wait_ge(s_blend_out, n // GROUPS)
                a, b = acc(s["acc"]), acc(s["acc2"])

                A_(perm_tiles(og[:, g, :], g), perm_tiles(a[:, :], 0), ACT.Copy).then_inc(s_unperm_o, 1)
                act.wait_ge(s_unperm_mm, 2 * n + 1 + 1)
                A_(perm_tiles(lg[:, g, :], g), perm_tiles(b[:, :], 0), ACT.Copy).then_inc(s_unperm_l, 1)

            def rot(s):
                act.dma_start(pos_i[:, :], A["pos"]).then_inc(s_pos_dma, 16)
                act.wait_ge(s_rot_ang, 1)
                link(A_(cs8[:, 1, :, :], ang[:, :, :], ACT.Sin))
                link(A_(an2[:, :, :], ang[:, :, :], ACT.Abs))
                A_(cs8[:, 0, :, :], an2[:, :, :], ACT.Sin, scale=-1.0, bias=col("halfpi")).then_inc(s_rot_cs, 1)

            def blend(s):
                n = s.n
                act.wait_ge(s_blend_sub, n + 1)
                for g in range(GROUPS):
                    ins = A_(lg[:, g, :], lg[:, g, :], ACT.Exp)
                    link(ins) if g < GROUPS - 1 else ins.then_inc(s_blend_exp, 1)

            parts = dict(start=start, gemm=unit, ada=unit, cmp=unit, gate=gate, resid=resid, sqx=sqx, norm=norm, gd=gd, proj=proj,
                         cmph=cmph, toep=toep_step, scores=softmax, turn=copy_pt, heads=heads, mixout=mixout,
                         sss=sss_exp, xtok=xtok_, ssn=ssn, gln=gln, fgate=fgate, fbias=fbias, qkn=qkn,
                         vcopy=vcopy, sgate=sgate, unperm=unperm, rot=rot, blend=blend)
            for s in plan.steps:
                if s.kind in parts:
                    parts[s.kind](s)

        @block.vector
        def _(dve):
            link = chain_of(dve, s_dve_chain)
            V = nc.vector
            dve.wait_ge(s_const, 16 * n_const)

            def start(s):
                V.memset(rel[32:33, :], BIG).then_inc(s_rel_big, 1)
                for c in range(16):
                    dve.wait_ge(s_rev_mm, c + 1)
                    V.tensor_copy(revs[:, c // 2, (c % 2) * 512:(c % 2 + 1) * 512], acc_bank[c % 2][:, :]).then_inc(s_rev_copy, 1)

            def mod_(s):
                m = s["m"]
                l, sub = divmod(m, NSUB)
                dve.wait_ge(s_ada_mm, m * 24 + 23 + 1)
                ps = m_bank[:, (m % 2) * 24:(m % 2) * 24 + 24]
                link(V.tensor_tensor(mod[:, m, :], ps, col("ada_b", m * 24, 24), ALU.add))
                link(V.tensor_scalar(mod[:, m, 8:24], mod[:, m, 8:24], 1.0, None, ALU.add))
                w = 1.0 if sub == 1 else 0.5
                link(V.tensor_scalar(mod[:, m, 16:24], mod[:, m, 16:24], w, None, ALU.mult))
                if m == 0:
                    link(V.tensor_copy(modg[:, m, 0:8], mod[:, m, 8:16]))
                    V.tensor_copy(modg[:, m, 8:16], mod[:, m, 0:8]).then_inc(s_mod_done, 1)
                else:
                    g, b = col("ln_g", (m - 1) * KD, KD), col("ln_b", (m - 1) * KD, KD)
                    link(V.tensor_tensor(modg[:, m, 0:8], mod[:, m, 8:16], g, ALU.mult))
                    link(V.tensor_tensor(modg[:, m, 8:16], mod[:, m, 8:16], b, ALU.mult))
                    V.tensor_tensor(modg[:, m, 8:16], modg[:, m, 8:16], mod[:, m, 0:8], ALU.add).then_inc(s_mod_done, 1)

            def gate(s):
                n, t = s.n, s["t"]
                dve.wait_ge(s_gate_silu, n + 1)
                dve.wait_ge(s_gemm_mm, plan.last_gemm[s["a3"]] + 1)
                V.tensor_tensor(tmp_h[n % 2][:, :], acc(s["a3"])[:, :], tmp_a[n % 2][:, :],
                                ALU.mult).then_inc(s_gate_mul, 1)
                dve.wait_ge(s_gate_mul, n + 1)
                link(V.tensor_copy(act_hi["gu"][:, t, :], tmp_h[n % 2][:, :]))
                V.tensor_tensor(act_lo["gu"][:, t, :], tmp_h[n % 2][:, :],
                                    act_hi["gu"][:, t, :].bitcast(F32), ALU.subtract).then_inc(s_gate_lo, 1)

            def resid(s):
                n, d = s.n, s["d"]
                if s["gate"] is not None:
                    dve.wait_ge(s_resid_y, n + 1)
                    if s.before.get("norm_x", 0):
                        dve.wait_ge(s_norm_x, (s.before["norm_x"] - 1) * KD + d + 1)
                    V.scalar_tensor_tensor(out=x[:, d, :], in0=x[:, d, :], scalar=ALPHA,
                                               in1=tmp_a[n % 2][:, :], op0=ALU.mult, op1=ALU.add).then_inc(s_resid_z, 1)
                else:
                    dve.wait_ge(s_gemm_mm, plan.last_gemm[s["acc"]] + 1)
                    V.tensor_tensor(x[:, d, :], x[:, d, :], acc(s["acc"])[:, :], ALU.add).then_inc(s_resid_z, 1)

            def norm(s):
                if s["stats"]:
                    dve.wait_ge(s_stat_mm, s.before["stat"])
                    if s["center"]:
                        link(V.tensor_scalar(st[:, 0:8], o_bank[:, 0:8], STAT_N, None, ALU.mult))
                        link(V.tensor_tensor(st2[:, 4:8], st[:, 0:4], st[:, 0:4], ALU.mult))
                        V.tensor_tensor(st2[:, 4:8], st[:, 4:8], st2[:, 4:8], ALU.subtract).then_inc(s_norm_var, 1)
                    else:
                        V.tensor_scalar(st2[:, 4:8], o_bank[:, 4:8], STAT_N, None, ALU.mult).then_inc(s_norm_var, 1)
                    dve.wait_ge(s_norm_std, s["sn"] + 1)
                    V.reciprocal(st[:, 4:8], st2[:, 0:4]).then_inc(s_norm_r, 1)
                    dve.wait_ge(s_norm_bc, s["sn"] + 1)
                for d in range(KD):
                    if s["stats"]:
                        if s["center"]:
                            link(V.tensor_tensor(x[:, d, :], x[:, d, :], acc(s["am"])[:, :], ALU.subtract))
                            V.tensor_tensor(x[:, d, :], x[:, d, :], acc(s["ar"])[:, :], ALU.mult).then_inc(s_norm_t, 1)
                        else:
                            if d >= 2:
                                dve.wait_ge(s_h_act, s["hn"] * KD + d - 1)
                            V.tensor_tensor(tmp_a[d % 2][:, :], x[:, d, :], acc(s["ar"])[:, :], ALU.mult).then_inc(s_norm_t, 1)
                    if s["h"] is not None:
                        if d >= 1:
                            high(s, d - 1)
                if s["h"] is not None:
                    high(s, KD - 1)

            def high(s, d):
                n = s["hn"] * KD + d
                dve.wait_ge(s_h_act, n + 1)
                V.tensor_copy(act_hi["h"][:, d, :], tmp_h[d % 2][:, :]).then_inc(s_h_hi, 1)

            def gd(s):
                l = s["l"]
                dve.wait_ge(s_gemm_mm, plan.last_gemm[s["acc"]] + 1)
                ps = acc(s["acc"])[:, 0:TT * 28].rearrange("p (t c) -> p t c", t=TT)
                b = row("dt_b", 4 * l, 4).unsqueeze(1).to_broadcast([P, TT, 4])
                V.tensor_tensor(dtmp[:, :, :], ps[:, :, 24:28], b, ALU.add).then_inc(s_gd_x, 1)
                dve.wait_ge(s_gd_ln, s.n + 1)
                link(V.tensor_scalar(dtmp[:, :, :], dtmp[:, :, :], 0.0, None, ALU.max))
                link(V.tensor_tensor(dts[:, :, 0:4], dtmp[:, :, :], dtmp2[:, :, :], ALU.add))
                a = row("a_log", 4 * l, 4).unsqueeze(1).to_broadcast([P, TT, 4])
                link(V.tensor_tensor(dts[:, :, 4:8], dts[:, :, 0:4], a, ALU.mult))
                V.tensor_scalar(dts[:, :, 4:8], dts[:, :, 4:8], -1.0, None, ALU.mult).then_inc(s_gd_a, 1)
                link(V.memset(xpad[:, 0:3], 0.0))
                for j in range(2):
                    link(V.memset(cmpr[:, j, :, 62:64], 0.0))
                    link(V.tensor_copy(cmpr[:, j, :, 62:63], col("pe", (l * 2 + j) * 16, 16).unsqueeze(2)))

            def proj(s):
                l, c = s["l"], s["c"]
                ps = acc(s["acc"])
                if c >= 16:
                    k = l * 6 + c - 16
                    dve.wait_ge(s_proj_act, proj_ordinal(l, c) + 1)
                    y = xbc[:, c - 16, :]
                    w = [col("conv_w", (l * 6 + c - 16) * 4 + t) for t in range(4)]
                    link(V.tensor_scalar(y, xpad[:, 0:T], w[0], None, ALU.mult))
                    for t in range(1, 4):
                        ins = V.scalar_tensor_tensor(out=y, in0=xpad[:, t:t + T], scalar=w[t], in1=y,
                                                     op0=ALU.mult, op1=ALU.add)
                        link(ins) if t < 3 else ins.then_inc(s_conv, 1)
                    return
                if proj_on_act(c):
                    return
                dve.wait_ge(s_gemm_mm, plan.last_gemm[s["acc"]] + 1)
                if c in (4, 5):
                    j = c - 4
                    for g in range(2):
                        for l2 in range(2):
                            for half in range(2):
                                src = ps[g * HD:(g + 1) * HD, half * 16:half * 16 + NCMP * 16]
                                src = src.rearrange("p (n j l) -> p j n l", j=8, l=2)[:, :, :, l2]
                                dst = cmpr[l2 * HD:(l2 + 1) * HD, j, half * 8:half * 8 + 8,
                                           g * NCMP:(g + 1) * NCMP]
                                ins = V.tensor_copy(dst, src)
                                if (g, l2, half) == (1, 1, 1):
                                    ins.then_inc(s_proj_dve, 1)
                                else:
                                    link(ins)
                elif c in (6, 8):
                    b = (c - 6)
                    for g in range(2):
                        for half in range(2):
                            ins = V.tensor_copy(kd[half * HD:(half + 1) * HD, b + g, :],
                                                ps[g * HD:(g + 1) * HD, :])
                            if (g, half) == (1, 1):
                                ins.then_inc(s_proj_dve, 1)
                            else:
                                link(ins)
                else:
                    V.tensor_copy(v1[:, (c - 7) // 2, :, :], ps[:, :].rearrange("p (t c) -> p t c", t=TT)).then_inc(s_proj_dve, 1)

            def cmph(s):
                l, j = s["l"], s["j"]
                dve.wait_ge(s_cmp_mm, 4 * (s.n + 1))
                if s.n:
                    dve.wait_ge(s_cmph_act, s.n)
                b = COL["cmp_b1"] + (l * 2 + j) * 2
                link(V.tensor_tensor(b1c[:, 0:1], acc(s["a0"])[:, 62:63], cols[:, b:b + 1], ALU.add))
                V.tensor_tensor(b1c[:, 1:2], acc(s["a1"])[:, 62:63], cols[:, b + 1:b + 2], ALU.add).then_inc(s_cmph_b, 1)

            def cmpo(s):
                dve.wait_ge(s_cmpo_mm, s.n + 1)
                if s["j"] == 0:
                    V.tensor_copy(kc[:, :, :], acc(s["acc"])[:, 0:62].rearrange("p (g n) -> p g n", g=2)).then_inc(s_cmpo_out, 1)
                else:
                    V.tensor_copy(vc[:, :, :], acc(s["acc"])[0:NCMP, 0:128].rearrange("p (g n) -> p g n", g=2)).then_inc(s_cmpo_out, 1)

            def scores(s):
                j, L = s.n, job_len(s)
                g, i = s["group"] % 8, s["slot"]
                dve.wait_ge(s_scores_mm, j + 1)
                if j >= 2:
                    dve.wait_ge(s_p_ready, j - 1)
                if s["fam"] == "nsa" and s["br"] == 0 and s["slot"] == 0 and s["h"] % 2 == 0:
                    hp = s["h"] // 2
                    dve.wait_ge(s_toep[hp % 2], 32 * (2 * s["l"] + hp // 2 + 1))
                if s["fam"] == "fox" and s["slot"] == 0:
                    dve.wait_ge(s_fbias_out, 2 * s["pair"] + s["hh"] + 1)
                if s["slot"] == 0 and s["group"] >= 8:
                    dve.wait_ge(s_heads_done, s["group"] - 7)
                V.tensor_tensor_reduce(sT[j % 2][:, 0:L], s_bank[j % 2][:, 0:L], job_bias(s), 1.0, 3.0e38,
                                           ALU.add, ALU.min, mn[:, g, i:i + 1]).then_inc(s_s_ready, 1)

            def heads(s):
                g = s["g"]
                z = zs[:, g % 8, :]
                dve.wait_ge(s_values_mm, s["j"] + 1)
                half = head_bank[g % 2][:, 0:256].rearrange("p (t c) -> p t c", t=TT)
                link(V.reciprocal(rz[:, 0:4], z))
                if s["fam"] == "nsa":
                    h, br = s["h"], s["br"]
                    b = (h % 2) * HD
                    link(V.tensor_tensor(rz[:, 0:4], rz[:, 0:4], gates[:, :, 3 * h + br], ALU.mult))
                    if br == 0:
                        link(V.tensor_tensor(rz[:, 0:1], rz[:, 0:1], col("valid"), ALU.mult))
                        if h % 2 == 0 and s.before.get("mixout", 0):
                            dve.wait_ge(s_mixout_mm, s.before.get("mixout", 0))
                        V.tensor_tensor(opair[:, :, b:b + HD], half,
                                            rz[:, 0:4].unsqueeze(2).to_broadcast([P, TT, HD]), ALU.mult).then_inc(s_heads_done, 1)
                        dve.wait_ge(s_heads_done, s.n + 1)
                        return
                    link(V.tensor_tensor(otmp[:, :, :], half,
                                         rz[:, 0:4].unsqueeze(2).to_broadcast([P, TT, HD]), ALU.mult))
                    V.tensor_tensor(opair[:, :, b:b + HD], opair[:, :, b:b + HD], otmp[:, :, :], ALU.add).then_inc(s_heads_done, 1)
                    dve.wait_ge(s_heads_done, s.n + 1)
                    return
                b = s["hh"] * HD
                if s["fam"] == "fox":
                    if s["hh"] == 0 and s.before.get("mixout", 0):
                        dve.wait_ge(s_mixout_mm, s.before.get("mixout", 0))
                else:
                    V.tensor_copy(lse[:, :, s["hh"]], mn[:, g % 8, :]).then_inc(s_heads_rz, 1)
                    dve.wait_ge(s_heads_ln, s["nd"] + 1)
                    link(V.tensor_tensor(lse[:, :, s["hh"]], lse[:, :, s["hh"]], rz[:, 4:8], ALU.subtract))
                    if s["hh"] == 0 and s.before.get("unperm", 0):
                        dve.wait_ge(s_unperm_mm, 2 * s.before.get("unperm", 0))
                    link(V.tensor_copy(rep[:, :, b:b + HD],
                                       lse[:, :, s["hh"]].unsqueeze(2).to_broadcast([P, TT, HD])))
                V.tensor_tensor(opair[:, :, b:b + HD], half,
                                    rz[:, 0:4].unsqueeze(2).to_broadcast([P, TT, HD]), ALU.mult).then_inc(s_heads_done, 1)
                dve.wait_ge(s_heads_done, s.n + 1)

            def mixout(s):
                n, t, dst = s.n, s["tile"], s["dst"]
                hi, lo = act_hi[dst][:, t, :], act_lo[dst][:, t, :]
                dve.wait_ge(s_mixout_mm, n + 1)
                if s["pair"] is not None:
                    dve.wait_ge(s_sgate_out, s["pair"] + 1)
                    link(V.tensor_tensor(wsum[:, :], acc(s["acc"])[:, :], sg[:, :], ALU.mult))
                    link(V.tensor_copy(hi, wsum[:, :]))
                    V.tensor_tensor(lo, wsum[:, :], hi.bitcast(F32), ALU.subtract).then_inc(s_mixout_lo, 1)
                    return
                dve.wait_ge(s_mixout_hi, s["hin"] + 1)
                sc = col(*s["scale"]) if s["scale"] else col("one")
                V.scalar_tensor_tensor(out=lo, in0=acc(s["acc"])[:, :], scalar=sc, in1=hi.bitcast(F32),
                                           op0=ALU.mult, op1=ALU.subtract).then_inc(s_mixout_lo, 1)

            def gln(s):
                l = s["l"]
                dve.wait_ge(s_proj_act, proj_ordinal(l, 13) + 1)
                for i in range(TT):
                    link(V.bn_stats(bn[:, i, :], vg[:, i, :]))
                    ins = V.bn_aggr(mv[:, i, :], bn[:, i, :])
                    link(ins) if i < TT - 1 else ins.then_inc(s_gln_mv, 1)
                dve.wait_ge(s_gln_std, s.n + 1)
                link(V.reciprocal(rz[:, 0:4], gstd[:, :]))
                for i in range(TT):
                    link(V.tensor_scalar(vg[:, i, :], vg[:, i, :], mv[:, i, 0:1], rz[:, i:i + 1],
                                         ALU.subtract, ALU.mult))
                g = row("gln_g", 256 * l, 256).unsqueeze(1).to_broadcast([P, TT, 256])
                b = row("gln_b", 256 * l, 256).unsqueeze(1).to_broadcast([P, TT, 256])
                link(V.tensor_tensor(vg[:, :, :], vg[:, :, :], g, ALU.mult))
                link(V.tensor_tensor(vg[:, :, :], vg[:, :, :], b, ALU.add))
                dve.wait_ge(s_small_dma, 32 * (l + 1))
                m = cst("tril_t").unsqueeze(1).to_broadcast([P, 4, P])
                V.tensor_tensor(gw[:, :, :], gw[:, :, :], m, ALU.mult).then_inc(s_gln_out, 1)

            def gsp(s):
                l = s["l"]
                for k in range(4):
                    if k % 2 == 0:
                        dve.wait_ge(s_gsp_mm, 2 * s.n + k // 2 + 1)
                    ps = acc(s["acc"][k // 2])[:, (k % 2) * 256:(k % 2 + 1) * 256].rearrange("p (t c) -> p t c", t=TT)
                    ins = V.scalar_tensor_tensor(out=gm[:, :, k * HD:(k + 1) * HD], in0=ps,
                                                 scalar=col("gmlp_bs", l * 4 + k), in1=ug[:, :, k * HD:(k + 1) * HD],
                                                 op0=ALU.add, op1=ALU.mult)
                    link(ins) if k % 2 == 0 else ins.then_inc(s_gsp_out, 1)

            def cs(s):
                l = s["l"]
                dve.wait_ge(s_cs_mm, s.n + 1)
                ones = con[0:4, CON["ones"]:CON["ones"] + 1].to_broadcast([4, T])
                V.tensor_tensor_scan(csr[:, :], ones, acc(s["acc"])[0:4, :], 0.0, ALU.mult, ALU.add).then_inc(s_cs_scan, 1)
                dve.wait_ge(s_cs_back, s.n + 1)
                V.tensor_scalar(csc[:, :, :], acc(s["acc2"])[:, 0:16].rearrange("p (t c) -> p t c", t=TT),
                                    -1.0, None, ALU.mult).then_inc(s_cs_col, 1)

            def xtok_(s):
                t = s["t"]
                dve.wait_ge(s_xtok_copy, s.n + 1)
                v = slice(t * P, (t + 1) * P)
                V.tensor_tensor(xdt[:, :, v].rearrange("p t (h c) -> p t h c", h=2),
                                    xtok[:, :, v].rearrange("p t (h c) -> p t h c", h=2),
                                    dts[:, :, 2 * t:2 * t + 2].unsqueeze(3).to_broadcast([P, TT, 2, HD]), ALU.mult).then_inc(s_xdt, 1)

            def ssb(s):
                n = s.n
                dve.wait_ge(s_ssb_mm, n + 1)
                if n % 4 == 0:
                    dve.wait_ge(s_values_mm, s.before["values"])
                if n >= 1:
                    dve.wait_ge(s_sss_e, 4 * n)
                m = cst("ssm_mask").unsqueeze(1).to_broadcast([P, TT, P])
                V.tensor_tensor(ptT[0][:, :].rearrange("p (t c) -> p t c", t=TT),
                                    s_bank[n % 2][:, :].rearrange("p (t c) -> p t c", t=TT), m, ALU.add).then_inc(s_ssb_mask, 1)

            def sss(s):
                k, i = s.n, s["i"]
                L = T - i * P
                dve.wait_ge(s_sss_mm, k + 1)
                dve.wait_ge(s_sss_e, k + 1)
                if k >= 2:
                    dve.wait_ge(s_ssy_mm, k - 1)
                V.tensor_tensor(pT[k % 2][:, 0:L], sT[k % 2][:, 0:L], acc(s["acc"])[:, 0:L], ALU.mult).then_inc(s_sss_mul, 1)

            def ssg(s):
                n, h, hh = s.n, s["h"], s["hh"]
                dve.wait_ge(s_ssy_mm, 4 * n + 3 + 1)
                if hh == 0:
                    dve.wait_ge(s_mixout_mm, s.before.get("mixout", 0))
                half = head_bank[n % 2][:, 0:256].rearrange("p (t c) -> p t c", t=TT)
                o = opair[:, :, hh * HD:(hh + 1) * HD]
                v = slice(h * HD, (h + 1) * HD)
                link(V.scalar_tensor_tensor(out=o, in0=xtok[:, :, v], scalar=row("ssm_d", 4 * s["l"] + h, 1),
                                            in1=half, op0=ALU.mult, op1=ALU.add))
                V.tensor_tensor(o, o, zg[:, :, v], ALU.mult).then_inc(s_ssg_out, 1)
                dve.wait_ge(s_ssg_out, n + 1)

            def ssn(s):
                dve.wait_ge(s_ssn_sq, s.n + 1)
                V.tensor_reduce(mv[:, :, 0:1], tmp_a[0][:, :].rearrange("p (t c) -> p t c", t=TT), AX.X, ALU.add).then_inc(s_ssn_sum, 1)
                dve.wait_ge(s_ssn_std, s.n + 1)
                link(V.reciprocal(rz[:, 0:4], gstd[:, :]))
                V.tensor_tensor(opair[:, :, :], opair[:, :, :],
                                    rz[:, 0:4].unsqueeze(2).to_broadcast([P, TT, P]), ALU.mult).then_inc(s_ssn_out, 1)
                dve.wait_ge(s_ssn_out, s.n + 1)

            def fgate(s):
                dve.wait_ge(s_gemm_mm, plan.last_gemm[s["acc"]] + 1)
                b = row("b_f", 0, 16).unsqueeze(1).to_broadcast([P, TT, 16])
                V.tensor_tensor(fl[:, :, :], acc(s["acc"])[:, 0:64].rearrange("p (t c) -> p t c", t=TT), b,
                                    ALU.add).then_inc(s_fgate_x, 1)
                dve.wait_ge(s_fgate_ln, 1)
                link(V.tensor_scalar(fl[:, :, :], fl[:, :, :], 0.0, None, ALU.min))
                V.tensor_tensor(fl[:, :, :], fl[:, :, :], fl2[:, :, :], ALU.subtract).then_inc(s_fgate_ls, 1)
                dve.wait_ge(s_fgate_mm, 1)
                ones = con[0:16, CON["ones"]:CON["ones"] + 1].to_broadcast([16, T])
                V.tensor_tensor_scan(crow, ones, acc(s["acc2"])[0:16, :], 0.0, ALU.mult, ALU.add).then_inc(s_fgate_scan, 1)
                for name, i, n in (("fox_qk", 0, 1), ("dsw_qk", 0, 3)):
                    link(V.tensor_scalar(col(name, i, n), col(name, i, n), QSCALE, None, ALU.mult))

            def qkn(s):
                n = s.n
                dve.wait_ge(s_qkn_sq, n + 1)
                V.tensor_reduce(ss[:, :].unsqueeze(2), tmp_a[0][:, :].rearrange("p (a c) -> p a c", c=HD),
                                    AX.X, ALU.add).then_inc(s_qkn_ss, 1)
                dve.wait_ge(s_qkn_std, n + 1)
                link(V.reciprocal(rz[:, :], ss2[:, :]))
                if n >= 1:
                    dve.wait_ge(s_qkn_mm, n)
                V.tensor_tensor(qn[:, :, :].rearrange("p t (h c) -> p (t h) c", h=2),
                                    acc(s["acc"])[:, :].rearrange("p (a c) -> p a c", c=HD),
                                    rz[:, :].unsqueeze(2).to_broadcast([P, 8, HD]), ALU.mult).then_inc(s_qkn_qn, 1)
                dve.wait_ge(s_qkn_qn, n + 1)
                if s["rot"] is None:
                    return
                r = s["rot"]
                v = qn[:, :, :].rearrange("p t (h c) -> p t h c", h=2)
                t1, t2 = v[:, :, :, 0:8], v[:, :, :, 8:16]

                def tab(i):
                    return rtab[:, r, i, :, :].unsqueeze(2).to_broadcast([P, TT, 2, 8])
                link(V.tensor_tensor(rt[0][:, :, :, :], t1, tab(0), ALU.mult))
                link(V.tensor_tensor(rt[1][:, :, :, :], t2, tab(1), ALU.mult))
                link(V.tensor_tensor(rt[2][:, :, :, :], t2, tab(2), ALU.mult))
                link(V.tensor_tensor(rt[3][:, :, :, :], t1, tab(3), ALU.mult))
                link(V.tensor_tensor(t1, rt[0][:, :, :, :], rt[1][:, :, :, :], ALU.subtract))
                V.tensor_tensor(t2, rt[2][:, :, :, :], rt[3][:, :, :, :], ALU.add).then_inc(s_qkn_rot, 1)

            def rot(s):
                dve.wait_ge(s_pos_dma, 16)
                link(V.tensor_copy(pos[:, :], pos_i[:, :]))
                link(V.tensor_tensor(ang[:, :, :], pos[:, :].unsqueeze(2).to_broadcast([P, TT, 8]),
                                     row("invf", 0, 8).unsqueeze(1).to_broadcast([P, TT, 8]), ALU.mult))
                magic = 12582912.0
                link(V.tensor_scalar(an2[:, :, :], ang[:, :, :], 1.0 / (2 * np.pi), magic, ALU.mult, ALU.add))
                link(V.tensor_scalar(an2[:, :, :], an2[:, :, :], magic, None, ALU.subtract))
                c1 = 6.28125
                c2 = float(np.float32(np.round((2 * np.pi - c1) * 2 ** 22) / 2 ** 22))
                c3 = 2 * np.pi - c1 - c2
                for c in (c1, c2, c3):
                    link(V.scalar_tensor_tensor(out=ang[:, :, :], in0=an2[:, :, :], scalar=-c, in1=ang[:, :, :],
                                                op0=ALU.mult, op1=ALU.add))
                pi = 3.1415925
                V.tensor_scalar(ang[:, :, :], ang[:, :, :], pi, -pi, ALU.min, ALU.max).then_inc(s_rot_ang, 1)
                dve.wait_ge(s_rot_cs, 1)
                for r in range(6):
                    for i, (f, half) in enumerate(((0, 0), (1, 1), (0, 1), (1, 0))):
                        g = row("rot_g", r * 16 + half * 8, 8).unsqueeze(1).to_broadcast([P, TT, 8])
                        link(V.tensor_tensor(rtab[:, r, i, :, :], cs8[:, f, :, :], g, ALU.mult))

            def blend(s):
                n, t = s.n, s["tile"]
                dve.wait_ge(s_unperm_l, GROUPS * n + GROUPS)
                link(V.tensor_tensor(wsum[:, :], lg[:, 0, :], lg[:, 1, :], ALU.min))
                link(V.tensor_tensor(wsum[:, :], wsum[:, :], lg[:, 2, :], ALU.min))
                for g in range(GROUPS):
                    ins = V.tensor_tensor(lg[:, g, :], wsum[:, :], lg[:, g, :], ALU.subtract)
                    link(ins) if g < GROUPS - 1 else ins.then_inc(s_blend_sub, 1)
                dve.wait_ge(s_blend_exp, n + 1)
                for g in range(GROUPS):
                    link(V.tensor_tensor(og[:, g, :], og[:, g, :], lg[:, g, :], ALU.mult))
                link(V.tensor_tensor(wsum[:, :], lg[:, 0, :], lg[:, 1, :], ALU.add))
                link(V.tensor_tensor(wsum[:, :], wsum[:, :], lg[:, 2, :], ALU.add))
                link(V.reciprocal(wsum[:, :], wsum[:, :]))
                link(V.tensor_tensor(og[:, 0, :], og[:, 0, :], og[:, 1, :], ALU.add))
                link(V.tensor_tensor(og[:, 0, :], og[:, 0, :], og[:, 2, :], ALU.add))
                link(V.tensor_tensor(og[:, 0, :], og[:, 0, :], wsum[:, :], ALU.mult))
                dve.wait_ge(s_sgate_out, PAIRS + n + 1)
                link(V.tensor_tensor(og[:, 0, :], og[:, 0, :], sg[:, :], ALU.mult))
                hi, lo = act_hi["mix"][:, t, :], act_lo["mix"][:, t, :]
                link(V.tensor_copy(hi, og[:, 0, :]))
                V.tensor_tensor(lo, og[:, 0, :], hi.bitcast(F32), ALU.subtract).then_inc(s_blend_out, 1)

            parts = dict(start=start, mod=mod_, gate=gate, resid=resid, norm=norm, gd=gd, proj=proj, cmph=cmph,
                         cmpo=cmpo, scores=scores, heads=heads, mixout=mixout, gln=gln, gsp=gsp, cs=cs, xtok=xtok_,
                         ssb=ssb, sss=sss, ssg=ssg, ssn=ssn, fgate=fgate, qkn=qkn, rot=rot, blend=blend)
            for s in plan.steps:
                if s.kind in parts:
                    parts[s.kind](s)

        @block.tensor
        def _(pe):
            mm = nc.tensor.matmul
            pe.wait_ge(s_const, 16 * n_const)

            def bank_free(a):
                if a < ACC_BANKS:
                    return
                u, role = plan.reader[a - ACC_BANKS]
                n, kind = u.n, u.kind
                if kind == "gate":
                    if role == 1:
                        pe.wait_ge(s_gate_silu, n + 1)
                    else:
                        pe.wait_ge(s_gate_mul, n + 1)
                elif kind == "resid":
                    if u["gate"] is not None:
                        pe.wait_ge(s_resid_y, n + 1)
                    else:
                        pe.wait_ge(s_resid_z, n + 1)
                elif kind == "norm":
                    pe.wait_ge(s_norm_t, (u["sn"] + 1) * KD)
                elif kind == "gd":
                    pe.wait_ge(s_gd_ln, n + 1)
                elif kind == "proj":
                    if proj_on_act(u["c"]):
                        pe.wait_ge(s_proj_act, proj_ordinal(u["l"], u["c"]) + 1)
                    else:
                        pe.wait_ge(s_proj_dve, proj_ordinal(u["l"], u["c"]) + 1)
                elif kind == "cmph":
                    pe.wait_ge(s_cmph_act, n + 1)
                elif kind == "cmpo":
                    pe.wait_ge(s_cmpo_out, n + 1)
                elif kind == "mixout":
                    pe.wait_ge(s_mixout_lo, n + 1)
                elif kind == "gsp":
                    pe.wait_ge(s_gsp_out, 2 * n + role + 1)
                elif kind == "cs":
                    if role == 0:
                        pe.wait_ge(s_cs_scan, n + 1)
                    else:
                        pe.wait_ge(s_cs_col, n + 1)
                elif kind == "xtok":
                    pe.wait_ge(s_xtok_copy, n + 1)
                elif kind == "sss":
                    pe.wait_ge(s_sss_mul, n + 1)
                elif kind == "fgate":
                    if role == 0:
                        pe.wait_ge(s_fgate_x, n + 1)
                    else:
                        pe.wait_ge(s_fgate_scan, n + 1)
                elif kind == "qkn":
                    if role == 0:
                        pe.wait_ge(s_qkn_qn, n + 1)
                    else:
                        pe.wait_ge(s_qkn_out, n + 1)
                elif kind == "vcopy":
                    pe.wait_ge(s_vcopy_out, n + 1)
                elif kind == "sgate":
                    pe.wait_ge(s_sgate_out, n + 1)
                elif kind == "fbias":
                    pe.wait_ge(s_fbias_out, n + 1)
                elif kind == "unperm":
                    if role == 0:
                        pe.wait_ge(s_unperm_o, n + 1)
                    else:
                        pe.wait_ge(s_unperm_l, n + 1)

            def turn_tiles(dst, srcs, rows_=P):
                for i, ap in enumerate(srcs):
                    ins = nc.tensor.transpose(dst[:, i * P:(i + 1) * P], ap, ident[:rows_, :rows_])
                return ins

            def start(s):
                pe.wait_ge(s_rel_big, 1)
                for c in range(16):
                    if c >= 2:
                        pe.wait_ge(s_rev_copy, c - 1)
                    mm(acc_bank[c % 2][:, :], rel[:, c // 2:c // 2 + 1].to_broadcast([33, P]),
                           onehot[:, (c % 2) * 512:(c % 2 + 1) * 512], start=True, stop=True).then_inc(s_rev_mm, 1)
                pe.wait_ge(s_rev_copy, 16)

            def ada(s):
                u, m, c = s["u"], s["m"], s["c"]
                loaded(pe, u)
                if c == 0:
                    pe.wait_ge(s_csil, 1)
                    if m >= 1:
                        pe.wait_ge(s_mod_done, m)
                    if s.before.get("heads", 0):
                        pe.wait_ge(s_heads_done, s.before["heads"])
                    if s.before.get("ssg", 0):
                        pe.wait_ge(s_ssg_out, s.before["ssg"])
                at = (m % 2) * 24 + c
                for k in range(KD):
                    ins = mm(m_bank[:, at:at + 1], raw[u % RAW_SLOTS][:, k * P:(k + 1) * P], csil[:, k:k + 1],
                             start=k == 0, stop=k == KD - 1)
                ins.then_inc(s_ada_mm, 1)

            def gemm(s):
                a, w = s["acc"], s["split"] % SPLIT_SLOTS
                pe.wait_ge(s_w_lo, s["split"] + 1)
                if s["reads"] is not None:
                    if s["act"] == "gu":
                        pe.wait_ge(s_gate_lo, s["reads"] + 1)
                    elif s["form"] == "FM" and s["src"] == "wout" or s["src"] == "foxo":
                        pe.wait_ge(s_mixout_lo, s["reads"] + 1)
                    elif s["src"] == "dswo":
                        pe.wait_ge(s_blend_out, s["reads"] + 1)
                    else:
                        pe.wait_ge(s_h_lo, (s["reads"] + 1) * KD)
                if s["start"]:
                    bank_free(a)
                hi, lo = act_hi[s["act"]], act_lo[s["act"]]
                wh, wl = w_hi[w], w_lo[w]
                kc_, n = s["kc"], s["nc"]
                if s["form"] == "FM":
                    for k in range(kc_):
                        ks, kk = slice(k * n, (k + 1) * n), s["k0"] + k
                        mm(acc(a)[:, :], wh[:, ks], hi[:, kk, :], start=s["start"] and k == 0, stop=False)
                        mm(acc(a)[:, :], wh[:, ks], lo[:, kk, :], start=False, stop=False)
                        ins = mm(acc(a)[:, :], wl[:, ks], hi[:, kk, :], start=False, stop=s["stop"] and k == kc_ - 1)
                else:
                    for i in range(TT):
                        o = acc(a)[:, i * n:(i + 1) * n]
                        for k in range(kc_):
                            ks = slice(k * n, (k + 1) * n)
                            ah = perm_tiles(hi[:, k, :], s["perm"])[:, i]
                            al = perm_tiles(lo[:, k, :], s["perm"])[:, i]
                            mm(o, ah, wh[:, ks], start=k == 0, stop=False)
                            mm(o, ah, wl[:, ks], start=False, stop=False)
                            ins = mm(o, al, wh[:, ks], start=False, stop=k == kc_ - 1)
                ins.then_inc(s_gemm_mm, 1)
    
            def stat(s):
                d, j = s["d"], s.n
                pe.wait_ge(s_square, j + 1)
                if s["center"]:
                    pe.wait_ge(s_resid_z, s["r"] + 1)
                if d == 0:
                    if s.before.get("heads", 0):
                        pe.wait_ge(s_heads_done, s.before["heads"])
                    if s.before.get("ssg", 0):
                        pe.wait_ge(s_ssg_out, s.before["ssg"])
                    if s.before.get("norm_stats", 0) > 0:
                        pe.wait_ge(s_norm_var, s.before.get("norm_stats", 0))
                for half, src in enumerate((x[:, d, :], tmp_b[j % 2][:, :])):
                    if half == 0 and not s["center"]:
                        continue
                    for i in range(TT):
                        first = d == 0 and i == 0 and (half == 0 or not s["center"])
                        ins = mm(o_bank[:, half * 4 + i:half * 4 + i + 1], src[:, i * P:(i + 1) * P],
                                 cst("ones")[:, 0:1], start=first, stop=d == KD - 1, skip_group_check=True)
                ins.then_inc(s_stat_mm, 1)

            def norm(s):
                if not s["stats"]:
                    return
                pe.wait_ge(s_norm_r, s["sn"] + 1)
                for a, at in ((s["am"], 0), (s["ar"], 4)):
                    if a is None:
                        continue
                    bank_free(a)
                    for i in range(TT):
                        ins = mm(acc(a)[:, i * P:(i + 1) * P], st[:, at + i:at + i + 1].to_broadcast([P, P]), ident,
                                 start=True, stop=True)
                ins.then_inc(s_norm_bc, 1)

            def cmp_(s):
                u, j, q = s["u"], s["j"], s["q"]
                loaded(pe, u)
                if q == 0:
                    bank_free(s["a0"])
                    bank_free(s["a1"])
                    pe.wait_ge(s_proj_dve, proj_ordinal(s["l"], 9) + 1)
                w = raw[u % RAW_SLOTS][:, 0:1024].rearrange("p (c n) -> p c n", c=4)
                for c in range(4):
                    k = q * 4 + c
                    for hh, a in enumerate((s["a0"], s["a1"])):
                        ins = mm(acc(a)[:, 0:CMPW], w[:, c, hh * P:(hh + 1) * P], cmpr[:, j, k, :],
                                 start=k == 0, stop=k == 15)
                ins.then_inc(s_cmp_mm, 1)

            def cmpo(s):
                a, j = s["acc"], s["j"]
                pe.wait_ge(s_cmph_act, s.n + 1)
                pe.wait_ge(s_small_dma, 32 * (s["l"] + 1))
                bank_free(a)
                if j == 0:
                    for hh in range(2):
                        ins = mm(acc(a)[:, 0:62], cw2[:, hh, 0:P], hid[:, hh, :], start=hh == 0, stop=hh == 1)
                else:
                    for g in range(2):
                        for hh in range(2):
                            ins = mm(acc(a)[0:NCMP, g * HD:(g + 1) * HD], hid[:, hh, g * NCMP:(g + 1) * NCMP],
                                     cw2[:, hh, P:P + HD], start=hh == 0, stop=hh == 1)
                ins.then_inc(s_cmpo_mm, 1)

            def scores(s):
                j, L = s.n, job_len(s)
                if j >= 2:
                    pe.wait_ge(s_s_ready, j - 1)
                if s["slot"] == 0:
                    if s["fam"] == "nsa":
                        pe.wait_ge(s_cmpo_out, 2 * s["l"] + 1 + 1)
                        pe.wait_ge(s_proj_act, proj_ordinal(s["l"], 3) + 1)
                        pe.wait_ge(s_proj_dve, proj_ordinal(s["l"], 9) + 1)
                    else:
                        pe.wait_ge(s_qkn_out, s.before["qkn"])
                mask = s["fam"] == "fox"
                ins = mm(s_bank[j % 2][:, 0:L], job_q(s), job_k(s), start=True, stop=True)
                if mask:
                    ins = mm(s_bank[j % 2][:, L - P:L], ident, cst("causal"), start=False, stop=True,
                             skip_group_check=True)
                ins.then_inc(s_scores_mm, 1)

            def turn(s):
                j, L = s.n, job_len(s)
                pe.wait_ge(s_p_ready, j + 1)
                if j >= 1:
                    pe.wait_ge(s_pt_copied, j)
                for b in range((L + P - 1) // P):
                    w = min(P, L - b * P)
                    ins = nc.tensor.transpose(pt_bank[0:w, b * P:(b + 1) * P], pT[j % 3][:, b * P:b * P + w], ident)
                ins.then_inc(s_turn_mm, 1)

            def values(s):
                j = s.n
                vs = job_v(s)
                pe.wait_ge(s_pt_copied, j + 1)
                if s["slot"] == 0:
                    if s["group"] >= 2:
                        pe.wait_ge(s_heads_done, s["group"] - 1)
                    pe.wait_ge(s_mod_done, s.before["mod"])
                    if s.before["norm_stats"]:
                        pe.wait_ge(s_norm_var, s.before["norm_stats"])
                    if s["fam"] != "nsa":
                        pe.wait_ge(s_vcopy_out, s.before["vcopy"])
                K = NCMP if s["fam"] == "nsa" and s["br"] == 0 else P
                for b, v in enumerate(vs):
                    ins = mm(o_slot(s), ptT[j % 2][0:K, b * P:(b + 1) * P], v, start=b == 0, stop=b == len(vs) - 1)
                ins.then_inc(s_values_mm, 1)

            def mixout(s):
                a = s["acc"]
                if s["src"] == "heads":
                    pe.wait_ge(s_heads_done, s.before["heads"])
                elif s["src"] == "gmlp":
                    pe.wait_ge(s_gsp_out, 2 * s.before["gsp"])
                else:
                    pe.wait_ge(s_ssn_out, s.before["ssn"])
                bank_free(a)
                if s["src"] == "gmlp":
                    srcs = [gm[:, i, s["t"] * P:(s["t"] + 1) * P] for i in range(TT)]
                else:
                    srcs = [opair[:, i, :] for i in range(TT)]
                turn_tiles(acc(a), srcs).then_inc(s_mixout_mm, 1)

            def gsp(s):
                pe.wait_ge(s_gln_out, s.n + 1)
                for k in range(4):
                    a = s["acc"][k // 2]
                    if k % 2 == 0:
                        bank_free(a)
                    ins = mm(acc(a)[:, (k % 2) * 256:(k % 2 + 1) * 256], gw[:, k, :], vg[:, :, k * HD:(k + 1) * HD],
                             start=True, stop=True)
                    if k % 2 == 1:
                        ins.then_inc(s_gsp_mm, 1)

            def cs(s):
                a, a2 = s["acc"], s["acc2"]
                pe.wait_ge(s_gd_a, s["l"] + 1)
                bank_free(a)
                turn_tiles(acc(a)[0:4, :], [dts[:, i, 4:8] for i in range(TT)]).then_inc(s_cs_mm, 1)
                pe.wait_ge(s_cs_scan, s.n + 1)
                bank_free(a2)
                for i in range(TT):
                    ins = nc.tensor.transpose(acc(a2)[:, i * 4:(i + 1) * 4], csr[:, i * P:(i + 1) * P],
                                              con[0:4, CON["ident"]:CON["ident"] + 4])
                ins.then_inc(s_cs_back, 1)

            def xtok_(s):
                a, t = s["acc"], s["t"]
                pe.wait_ge(s_xbc, s["l"] * 6 + 5 + 1)
                bank_free(a)
                turn_tiles(acc(a), [xbc[:, t, i * P:(i + 1) * P] for i in range(TT)]).then_inc(s_xtok_mm, 1)

            def ssb(s):
                h, n = s["h"], s.n
                if n % 4 == 0:
                    pe.wait_ge(s_s_ready, s.before["scores"])
                if n >= 2:
                    pe.wait_ge(s_sss_e, 4 * (n - 2) + 3 + 1)
                sel = con[0:4, CON["ident"] + h:CON["ident"] + h + 1].to_broadcast([4, P])
                mm(s_bank[n % 2][:, :], sel, csr[:, :], start=True, stop=True).then_inc(s_ssb_mm, 1)

            def sss(s):
                a, i, g = s["acc"], s["i"], s["g"]
                bank_free(a)
                mm(acc(a)[:, 0:T - i * P], xbc[:, 2 + g, i * P:(i + 1) * P], xbc[:, 4 + g, i * P:T],
                       start=True, stop=True).then_inc(s_sss_mm, 1)

            def ssy(s):
                k, i, h = s["k"], s["i"], s["h"]
                pe.wait_ge(s_sss_mul, k + 1)
                n = k // 4
                if i == 0:
                    pe.wait_ge(s_xdt, s.before["xtok"])
                    if n >= 2:
                        pe.wait_ge(s_ssg_out, n - 1)
                    pe.wait_ge(s_heads_done, s.before["heads"])
                for j in range(i, TT):
                    ins = mm(head_bank[n % 2][:, j * HD:(j + 1) * HD], pT[k % 2][:, (j - i) * P:(j - i + 1) * P],
                             xdt[:, i, h * HD:(h + 1) * HD], start=i == 0 and j == 0, stop=j == i,
                             skip_group_check=True)
                ins.then_inc(s_ssy_mm, 1)

            def fgate(s):
                pe.wait_ge(s_fgate_ls, 1)
                bank_free(s["acc2"])
                turn_tiles(acc(s["acc2"])[0:16, :], [fl[:, i, :] for i in range(TT)]).then_inc(s_fgate_mm, 1)

            def fbias(s):
                a, h = s["acc"], s["h"]
                pe.wait_ge(s_fgate_scan, 1)
                bank_free(a)
                sel = con[0:16, CON["ident"] + h:CON["ident"] + h + 1].to_broadcast([16, P])
                mm(acc(a)[:, :], sel, crow, start=True, stop=True).then_inc(s_fbias_mm, 1)

            def qkn(s):
                a = s["acc2"]
                pe.wait_ge(s_qkn_qn, s.n + 1)
                if s["rot"] is not None:
                    pe.wait_ge(s_qkn_rot, s["rn"] + 1)
                bank_free(a)
                turn_tiles(acc(a), [qn[:, i, :] for i in range(TT)]).then_inc(s_qkn_mm, 1)

            def unperm(s):
                pe.wait_ge(s_heads_done, s.before["heads"])
                for a, src in ((s["acc"], opair), (s["acc2"], rep)):
                    bank_free(a)
                    turn_tiles(acc(a), [src[:, i, :] for i in range(TT)]).then_inc(s_unperm_mm, 1)

            parts = dict(start=start, ada=ada, gemm=gemm, stat=stat, norm=norm, cmp=cmp_, cmpo=cmpo, scores=scores,
                         turn=turn, values=values, mixout=mixout, gsp=gsp, cs=cs, xtok=xtok_, ssb=ssb, sss=sss,
                         ssy=ssy, fgate=fgate, fbias=fbias, qkn=qkn, unperm=unperm)
            for s in plan.steps:
                if s.kind in parts:
                    parts[s.kind](s)


def _bucket(n):
    if n < 16:
        return max(n, 0)
    return min(16 + int(np.log(n / 16) / np.log(128 / 16) * 16), 31)


def _tiles(w):
    k, n = w.shape[0] // P, w.shape[1] // P
    return np.ascontiguousarray(w.reshape(k, P, n, P).transpose(2, 1, 0, 3).reshape(n, P, k * P))


def _narrow(w):
    k = w.shape[0] // P
    return np.ascontiguousarray(w.reshape(k, P, w.shape[1]).transpose(1, 0, 2).reshape(P, -1))


def _layout(v):
    f = {k: np.asarray(a) for k, a in v.items()}
    L = LAYERS
    o = {}
    o["x"] = np.ascontiguousarray(f["x"][0].T.reshape(KD, P, T).transpose(1, 0, 2))
    o["ada"] = np.stack([_tiles(f["ada_w"][l]) for l in range(L)])
    w1, w3, w2 = (f[n].reshape(2 * L, *f[n].shape[2:]) for n in ("ffn_w1", "ffn_w3", "ffn_w2"))
    o["ffn13"] = np.stack([np.stack([_tiles(w1[i]), _tiles(w3[i])], 1) for i in range(2 * L)])
    at = 0
    for j, k in enumerate(DOWN):
        o[f"ffn2_{j}"] = np.stack([_tiles(w2[i][at * P:(at + k) * P]) for i in range(2 * L)])
        at += k
    w = f["w_in"]
    o["win"] = np.stack([_tiles(np.concatenate([w[l][:, :1280], w[l][:, 1304:2840]], 1)) for l in range(L)])
    o["small"] = np.stack([_narrow(np.concatenate([w[l][:, 1280:1304], w[l][:, 2840:2844]], 1)) for l in range(L)])
    o["wout"] = np.stack([_tiles(f["w_out"][l]) for l in range(L)])
    o["cmp1"] = np.ascontiguousarray(
        f["cmp_w1"].reshape(L, 2, 4, 4, P, 256).transpose(0, 1, 2, 4, 3, 5).reshape(L, 2, 4, P, 1024))
    c2 = f["cmp_w2"].reshape(L, 2, 2, P, HD).transpose(0, 1, 3, 2, 4)
    o["cmp2"] = np.ascontiguousarray(np.concatenate([c2[:, 0], c2[:, 0], c2[:, 1]], -1))
    o["gws"] = np.ascontiguousarray(f["gmlp_ws"].transpose(0, 3, 1, 2))
    fw = f["fox_w_in_2"][0]
    o["fox"] = _tiles(fw[:, :4 * D])
    o["foxf"] = _narrow(fw[:, 4 * D:])
    o["foxo"] = _tiles(f["fox_w_out_2"][0])
    o["dsw"] = _tiles(f["dsw_w_in_2"][0])
    o["dswo"] = _tiles(f["dsw_w_out_2"][0])
    o["rel_bias"] = f["rel_bias"]
    o["pos"] = np.ascontiguousarray(f["positions_2"][0].reshape(TT, P).T)

    def by_col(a):
        return a.reshape(-1, P).T

    fq, fk = f["fox_q_norm_2"][0], f["fox_k_norm_2"][0]
    dq, dk = f["dsw_q_norm_2"][0], f["dsw_k_norm_2"][0]
    one16 = np.ones(16, np.float32)
    parts = {
        "ada_b": by_col(f["ada_b"]), "ln_g": by_col(f["ln_g"]), "ln_b": by_col(f["ln_b"]),
        "cmp_b1": by_col(f["cmp_b1"]),
        "pe": f["cmp_pe"].reshape(L, 2, 16, 2, HD).transpose(3, 4, 0, 1, 2).reshape(P, 64),
        "conv_w": f["ssm_conv_w"].reshape(L, 4, 6, P).transpose(3, 0, 2, 1).reshape(P, 48),
        "conv_b": by_col(f["ssm_conv_b"]), "ssm_g": by_col(f["ssm_norm_g"]), "gmlp_bs": by_col(f["gmlp_bs"]),
        "norm2": by_col(f["norm_g_2"]),
        "fox_qk": np.stack([np.concatenate([g, g]) for g in (fq, fk)], 1),
        "dsw_qk": np.stack([np.concatenate([one16, g[16:], one16, g[16:]]) for a in (dq, dk) for g in a], 1),
        "eps5": np.full((P, 1), 1e-5, np.float32), "eps6": np.full((P, 1), 1e-6, np.float32),
        "valid": (np.arange(P) >= 31).astype(np.float32)[:, None], "one": np.ones((P, 1), np.float32),
        "halfpi": np.full((P, 1), np.pi / 2, np.float32), "c": by_col(f["c"]),
    }
    o["cols"] = np.ascontiguousarray(np.concatenate([parts[n] for n, _ in _COLS], 1))
    inv = (500000.0 ** (-np.arange(0, 16, 2, dtype=np.float32) / np.float32(16))).astype(np.float32)
    parts = {
        "dt_b": f["ssm_dt_bias"], "a_log": f["ssm_a_log"], "ssm_d": f["ssm_d"], "b_f": f["fox_b_f_2"],
        "gln_g": f["gmlp_ln_g"], "gln_b": f["gmlp_ln_b"],
        "rot_g": np.concatenate([dq[:, :16], dk[:, :16]]), "invf": inv,
    }
    o["rows"] = np.concatenate([parts[n].reshape(-1) for n, _ in _ROWS])
    a, b = np.arange(P)[:, None], np.arange(P)[None, :]
    big = np.float32(BIG)
    parts = {
        "ident": a == b, "prev": (b < a) * big, "causal": (b > a) * big,
        "blockmask": ((a % 4 != b % 4) | (b > a)) * big, "ssm_mask": (b < a) * -big,
        "tril_t": b >= a, "ones": np.ones((P, P)),
    }
    o["con"] = np.concatenate([parts[n].astype(np.float32) for n, _ in _CON], 1)
    e = np.zeros((33, REV), np.float32)
    for u in range(REV):
        n = DIST0 - u
        if n >= 0:
            e[_bucket(n), u] = -1.0
        else:
            e[32, u] = 1.0
    o["onehot"] = e
    return o


def kernel(**inputs):
    import concourse.bacc as _bacc
    from concourse import mybir as _mybir
    from concourse.bass_utils import run_bass_kernel_spmd as _run

    nc = _bacc.Bacc("TRN2", target_bir_lowering=False, num_devices=1)
    arrays, args = {}, {}
    for name, a in _layout(inputs).items():
        arrays[f"in_{name}_dram"] = a
        args[name] = nc.dram_tensor(f"in_{name}_dram", a.shape, _mybir.dt.from_np(a.dtype),
                                    kind="ExternalInput").ap()
    out = nc.dram_tensor("out_0_dram", (KD, P, T), _mybir.dt.float32, kind="ExternalOutput").ap()
    program(nc, args, out)
    r = _run(nc, [arrays], core_ids=[0])
    got = r.results[0]["out_0_dram"]
    return np.ascontiguousarray(got.reshape(D, T).T)[None]
```

```python
from contextlib import ExitStack

import numpy as np

import concourse.bass as bass
from concourse import mybir

F32 = mybir.dt.float32
F32R = mybir.dt.float32r
I32 = mybir.dt.int32
ALU = mybir.AluOpType
ACT = mybir.ActivationFunctionType
AX = mybir.AxisListType

P = 128
T = 512
TT = T // P
D = 1024
KD = D // P
LAYERS = 2
FF = 2816
KF = FF // P
DOWN = (8, 7, 7)
NSUB = 3
NMOD = NSUB * LAYERS
ALPHA = (2 * LAYERS) ** 0.25
HD = 64
QSCALE = -(HD ** -0.5)
BIG = 1.0e30
NCMP = 31
CMPW = 64
TOEP = 896
REV = 1024
DIST0 = 511
PAIRS = 8
GROUPS = 3
ZRING = 12
DSW_GROUP0 = LAYERS * 4 * 6 + PAIRS * 2

RAW_SLOTS = 4
SPLIT_SLOTS = 3
SLOT = KD * P
ACC_BANKS = 3
STAT_N = 1.0 / D

_COLS = [("ada_b", 2 * 72), ("ln_g", 48), ("ln_b", 48), ("cmp_b1", 8), ("pe", 64), ("conv_w", 48), ("conv_b", 12),
         ("ssm_g", 4), ("gmlp_bs", 8), ("norm2", 16), ("fox_qk", 2), ("dsw_qk", 6),
         ("eps5", 1), ("eps6", 1), ("valid", 1), ("one", 1), ("halfpi", 1), ("c", 8)]
COL = {}
NCOL = 0
for _n, _w in _COLS:
    COL[_n] = NCOL
    NCOL += _w
_ROWS = [("dt_b", 8), ("a_log", 8), ("ssm_d", 8), ("b_f", 16), ("gln_g", 512), ("gln_b", 512),
         ("rot_g", 96), ("invf", 8)]
ROW = {}
NROW = 0
for _n, _w in _ROWS:
    ROW[_n] = NROW
    NROW += _w
_CON = [("ident", 128), ("prev", 128), ("causal", 128), ("blockmask", 128), ("ssm_mask", 128),
        ("tril_t", 128), ("ones", 128)]
CON = {}
NCON = 0
for _n, _w in _CON:
    CON[_n] = NCON
    NCON += _w


class Step:
    def __init__(self, kind, n, before, **f):
        self.kind, self.n = kind, n
        self.before = before
        self.f = f

    def __getitem__(self, k):
        return self.f[k]


class Plan:

    def __init__(self):
        self.steps, self.count = [], {}
        self.units = []
        self.nsplit = 0
        self.acc = 0
        self.last_gemm = {}
        self.reader = {}
        self.flipped = {}
        self.pending = []

    def add(self, kind, **f):
        n = self.bump(kind)
        s = Step(kind, n, dict(self.count), **f)
        self.steps.append(s)
        return s

    def bump(self, kind):
        n = self.count.get(kind, 0)
        self.count[kind] = n + 1
        return n

    def new_acc(self):
        self.acc += 1
        return self.acc - 1

    def read(self, a, step, role=0):
        self.reader[a] = (step, role)

    def unit(self, kind, where, width, split=True, **f):
        u = len(self.units)
        s = self.add(kind, u=u, split=self.nsplit if split else None, **f)
        self.units.append((where, width, self.nsplit if split else None, u, kind, s.n))
        if split:
            self.nsplit += 1
        return s


def make_plan():
    p = Plan()

    later = []
    filler = []
    owed = []

    def after(k, fn, acc=None):
        later.append([k, fn, acc])
        if acc is not None:
            fill(owed.pop() if owed else 0)

    def fresh(n=1):
        held = [e for e in later if e[2] is not None and e[2] <= p.acc + n - 1 - ACC_BANKS]
        while held:
            later.remove(held[0])
            held[0][1]()
            held = [e for e in later if e[2] is not None and e[2] <= p.acc + n - 1 - ACC_BANKS]
        return p.new_acc()

    queue, at, base, due_now, squared, age = [], [0], [0], [], [], [0]

    def turn():
        i, n = at[0], len(queue)
        at[0] += 1
        if i < n:
            before, f, _, _ = queue[i]
            for b in before:
                b()
            p.add("scores", **f)
        if base[0] <= i - 1 < n:
            p.add("soft", **queue[i - 1][1])
        if base[0] <= i - 2 < n:
            p.add("turn", **queue[i - 2][1])
        if base[0] <= i - 3 < n:
            _, f, last, behind = queue[i - 3]
            p.add("values", **f)
            if last:
                p.add("heads", j=i - 3, **f["evac"])
            due_now.extend(behind)
        age[0] += 1

    def fill(k, within=False):
        n = 0
        while n < k:
            if squared and age[0] > 1:
                squared[0]()
            elif due_now:
                if within and due_now[0][1]:
                    break
                due_now.pop(0)[0]()
            elif at[0] < len(queue):
                if within and queue[at[0]][0]:
                    break
                turn()
            else:
                break
            n += 1
        return n

    def force(scored, valued):
        while at[0] < scored or at[0] - 3 < valued:
            if at[0] == len(queue):
                drain()
                return
            settle()
            turn()
        settle()

    def settle():
        while due_now:
            due_now.pop(0)[0]()

    def drain():
        settle()
        while base[0] < len(queue) and at[0] < len(queue) + 3:
            turn()
            settle()
        at[0] = base[0] = len(queue)

    def flush():
        while later:
            e = min(later, key=lambda e: e[2] is None)
            later.remove(e)
            e[1]()

    def gemm(src, act, acc, kc=KD, k0=0, start=True, stop=True, reads=None, lead=None, per=0):
        s = p.unit("gemm", src, kc * P, src=src[0], act=act, acc=acc, kc=kc, k0=k0, start=start, stop=stop,
                   reads=reads, lead=lead, batch=None, upto=kc)
        if lead == 2:
            gs = [t for t in p.steps if t.kind == "gemm"][-3:]
            s.f["batch"] = gs
        p.last_gemm[acc] = s.n
        if per and lead is None:
            cut = 1 if per > 4 else 2
            s.f["upto"] = k = cut
            while k < kc:
                per -= fill(1, within=True)
                p.add("part", g=s, at=k, upto=k + cut)
                k += cut
        if lead in (0, 1):
            return s
        due = []
        for e in list(later):
            e[0] -= 1
            if e[0] <= 0:
                due.append(e)
        for e in sorted(due, key=lambda e: e[2] is None):
            if e in later:
                later.remove(e)
                e[1]()
        if per:
            owed.append(max(per, 0))
        return s

    def narrow(src, acc, nc_):
        s = p.unit("gemm", src, KD * nc_, src=src[0], act="h", acc=acc, kc=KD, k0=0, start=True, stop=True,
                   reads=None, lead="narrow", batch=None, nc=nc_)
        p.last_gemm[acc] = s.n

    def fcopy(a):
        s = p.add("fcopy", acc=a)
        p.read(a, s)
        return s

    def flip(c, perm):
        b = fresh()
        s = p.add("flip", acc2=b, perm=perm)
        assert s.n == c.n
        p.flipped[b] = s.n
        return b

    def ada(k):
        for _ in range(min(k, len(p.pending))):
            m, c = p.pending.pop(0)
            l, s = divmod(m, NSUB)
            p.unit("ada", ("ada", (l, s * 24 + c)), D, split=False, m=m, c=c)
            if c == 23:
                p.add("mod", m=m)

    def queue_mod(m):
        if m < NMOD:
            p.pending += [(m, c) for c in range(24)]

    hcount = [0]

    def norm(center, h, x, stats=True):
        sn = p.bump("norm_stats") if stats else None
        s = p.add("norm", center=center, h=h, x=x, stats=stats, hn=hcount[0], sn=sn)
        if x is not None:
            p.bump("norm_x")
        if h is not None:
            hcount[0] += 1
        return hcount[0] - 1

    def project_out(act, srcs, deps, gate, stats):
        last = None
        for d in range(KD):
            a = p.new_acc()
            for j, (src, kc, k0) in enumerate(srcs(d)):
                gemm(src, act, a, kc=kc, k0=k0, start=j == 0, stop=j == len(srcs(d)) - 1,
                     reads=deps(j) if d == 0 else None)
            s = p.add("resid", d=d, acc=a, gate=gate, stats=stats)
            p.read(a, s)
            if last is not None and stats:
                p.add("stat", d=last["d"], r=last.n, src="resid", center=gate is not None)
            last = s
        if stats:
            p.add("stat", d=last["d"], r=last.n, src="resid", center=gate is not None)

    def ffn(f, hn, m):
        l, j = divmod(f, 2)
        g0 = p.count.get("gate", 0)
        tiles = [(p.new_acc(), p.new_acc())]

        def gate(t):
            s = p.add("gate", t=t, a1=tiles[t][0], a3=tiles[t][1])
            p.read(tiles[t][0], s, 1)
            p.read(tiles[t][1], s, 3)
        for t in range(KF):
            if t > 1:
                tiles.append((p.new_acc(), p.new_acc()))
            if t != 1:
                gemm(("ffn13", (f, t, 0)), "h", tiles[t][0], reads=hn if t == 0 else None, lead=0 if t == 0 else None)
            gemm(("ffn13", (f, t, 1)), "h", tiles[t][1], lead=1 if t == 0 else None)
            if t == 0:
                tiles.append((p.new_acc(), p.new_acc()))
                gemm(("ffn13", (f, 1, 0)), "h", tiles[1][0], lead=2)
            gate(t)
            ada(2 if t < 3 else 1)
        ada(24)
        at = [sum(DOWN[:j]) for j in range(len(DOWN) + 1)]
        project_out("gu", lambda d: [((f"ffn2_{j}", (f, d)), DOWN[j], at[j]) for j in range(len(DOWN))],
                    lambda j: g0 + at[j + 1] - 1, gate=(m, 0.5), stats=True)

    def jobs(js, before=(), behind=()):
        for i, f in enumerate(js):
            last = i == len(js) - 1
            queue.append((list(before) if i == 0 else [], f,
                          last or js[i + 1]["group"] != f["group"], list(behind) if last else []))

    gcount = [0]

    def group(js, evac):
        g = gcount[0]
        gcount[0] += 1
        z = (g - DSW_GROUP0 if evac["fam"] == "dsw" else g) % ZRING
        return [dict(j, group=g, z=z, slot=i, evac=dict(evac, g=g, z=z)) for i, j in enumerate(js)]

    def mixout(tile, dst, scale=None, pair=None, src="heads", t=0):
        a = fresh()
        s = p.add("mixout", tile=tile, dst=dst, scale=scale, pair=pair, acc=a, src=src, t=t,
                  hin=p.bump("mixout_hi") if pair is None else None)
        p.read(a, s)
        return s

    queue_mod(0)
    p.add("start")
    for c in range(16):
        ada(1)
        p.add("rev", c=c)
    ada(24)
    hn = norm(False, ("mod", 0), None, stats=False)
    for l in range(LAYERS):
        queue_mod(3 * l + 1)
        ffn(2 * l, hn, 3 * l)
        hn = norm(True, ("mod", 3 * l + 1), 3 * l)

        queue_mod(3 * l + 2)
        def proj(c, lead=None, per=0):
            a = fresh()
            gemm(("win", (l, c)), "h", a, reads=hn if lead == 0 else None, lead=lead, per=per)
            flat = c in (7, 9) or 10 <= c < 16
            fc = fcopy(a) if flat else None

            def post():
                b = flip(fc, 0) if flat else a
                s = p.add("proj", l=l, c=c, acc=b, flat=flat)
                p.read(b, s)
            return post, None if flat else a
        posts = [proj(c, lead=c) for c in range(3)]
        for f, _ in posts:
            f()
        a = fresh()
        narrow(("small", (l,)), a, 28)
        s = p.add("gd", l=l, acc=a)
        p.read(a, s)
        for c in range(3, 10):
            after(1, *proj(c))
            ada(3)
        ada(24)
        flush()
        for j in range(2):
            a0, a1 = fresh(2), fresh()
            for q in range(4):
                p.unit("cmp", ("cmp1", (l, j, q)), 1024, split=False, l=l, j=j, q=q, a0=a0, a1=a1)
            s = p.add("cmph", l=l, j=j, a0=a0, a1=a1)
            p.read(a0, s)
            p.read(a1, s)
            a = fresh()
            s = p.add("cmpo", l=l, j=j, acc=a)
            p.read(a, s)
        for hp in range(4):
            js = []
            for hh in range(2):
                for br in range(3):
                    js += group([dict(fam="nsa", l=l, h=2 * hp + hh, br=br, i=i) for i in range(TT)],
                                dict(fam="nsa", h=2 * hp + hh, br=br, l=l))
            jobs(js, behind=[(lambda hp=hp: p.add("toep", l=l, hp=hp + 2), False)] if hp < 2 else [])
        for c in range(10, 22):
            after(1, *proj(c, per=9))
            fill(owed.pop() if owed else 0)
        flush()
        drain()
        for hp in range(4):
            mixout(hp, "h")
        p.add("gln", l=l)
        a = [fresh() for _ in range(2)]
        s = p.add("gsp", l=l, acc=a)
        p.read(a[0], s, 0)
        p.read(a[1], s, 1)
        for t in range(2):
            mixout(4 + t, "h", src="gmlp", t=t)
        a = fresh()
        a2 = fresh()
        s = p.add("cs", l=l, acc=a, acc2=a2)
        p.read(a, s, 0)
        p.read(a2, s, 1)
        for t in range(2):
            a = fresh()
            s = p.add("xtok", l=l, t=t, acc=a)
            p.read(a, s)
        for g in range(2):
            for hh in range(2):
                s = p.add("ssb", l=l, g=g, h=2 * g + hh)
                for i in range(TT):
                    a = fresh()
                    sc = p.add("sss", l=l, g=g, h=2 * g + hh, i=i, acc=a, b=s.n)
                    p.read(a, sc)
                    if i > 0:
                        p.add("ssy", **last_sss)
                    last_sss = dict(h=2 * g + hh, i=i, k=sc.n, hh=hh)
                p.add("ssy", **last_sss)
                p.add("ssg", l=l, h=2 * g + hh, hh=hh, g=g)
            p.add("ssn", l=l, g=g)
            mixout(6 + g, "h", scale=("ssm_g", 2 * l + g), src="ssm")
        mo = p.count["mixout"]
        project_out("h", lambda d: [(("wout", (l, d)), KD, 0)], lambda j: mo - 1,
                    gate=(3 * l + 1, 1.0), stats=True)
        hn = norm(True, ("mod", 3 * l + 2), 3 * l + 1)

        queue_mod(3 * l + 3)
        ffn(2 * l + 1, hn, 3 * l + 2)
        if l == 0:
            hn = norm(True, ("mod", 3), 2)
        else:
            norm(True, None, 5)
            for d in range(KD):
                p.add("sqx", d=d)
                if d:
                    p.add("stat", d=d - 1, r=d - 1, src="sqx", center=False)
            p.add("stat", d=KD - 1, r=KD - 1, src="sqx", center=False)
    hn = norm(False, ("rms", 0), None)

    start2, ends = len(queue), []

    def owners(st):
        return ends[st - 2] if st >= 2 else start2

    backs = []

    def complete(st):
        while squared:
            squared[0]()
        for e in [e for t, e in backs if t == st and e in later]:
            later.remove(e)
            e[1]()

    def qk(src, st, which, col, rot, reads=None, lead=None, per=0):
        force(owners(st), 0)
        a = fresh()
        gemm(src, "h", a, reads=reads, lead=lead, per=per)

        fc = fcopy(a)

        def normed():
            while squared:
                squared[0]()
            b = flip(fc, 0)
            p.read(b, p.add("qkn", acc=b))

            def scale():
                if scale not in squared:
                    return
                squared.remove(scale)
                n = p.add("qks", rot=rot, rn=None if rot is None else p.bump("rotated"))
                if held in later:
                    later.remove(held)
                after(1, lambda: back(n))
                backs.append((st, later[-1]))

            def back(n):
                b = fresh()
                s = p.add("qkt", acc=b, which=(which, st % 2), used=owners(st), col=col, q=n.n, rot=rot, rn=n["rn"])
                p.read(b, s)
            held = [1, scale, None]
            squared.append(scale)
            age[0] = 0
            later.append(held)
        after(1, normed)
        fill(owed.pop() if owed else 0)

    def vproj(src, st, perm, lead=None, per=0):
        force(0, owners(st))
        a = fresh()
        gemm(src, "h", a, lead=lead, per=per)

        fc = fcopy(a)

        def post():
            b = flip(fc, perm)
            s = p.add("vcopy", slot=st % 2, acc=b, used=owners(st))
            p.read(b, s)
        after(1, post)
        fill(owed.pop() if owed else 0)

    def gproj(src, st, per=0):
        if st >= 0:
            force(0, ends[st])
        a = fresh()
        gemm(src, "h", a, per=per)
        s = p.add("sgate", acc=a)
        p.read(a, s)
        fill(owed.pop() if owed else 0)

    def fox_jobs(hp):
        complete(hp)

        def bias(hh):
            a = fresh()
            s = p.add("fbias", h=2 * hp + hh, hh=hh, acc=a)
            p.read(a, s)
        for hh in range(2):
            js = group([dict(fam="fox", hh=hh, i=i, pair=hp, set=hp % 2) for i in range(TT)],
                        dict(fam="fox", hh=hh, pair=hp))
            jobs(js, before=[lambda hh=hh: bias(hh)],
                 behind=[(lambda: mixout(hp, "mix", pair=hp), True)] if hh == 1 else [])
        ends.append(len(queue))

    for hp in range(PAIRS):
        lead = hp == 0
        qk(("fox", (hp,)), hp, "q", ("fox_qk", 0), None, hn if lead else None, 0 if lead else None, per=4)
        qk(("fox", (8 + hp,)), hp, "k", ("fox_qk", 1), None, None, 1 if lead else None, per=4)
        vproj(("fox", (16 + hp,)), hp, 0, 2 if lead else None, per=4)
        if lead:
            flush()
            a = fresh()
            narrow(("foxf", ()), a, 16)
            a2 = fresh()
            s = p.add("fgate", acc=a, acc2=a2)
            p.read(a, s, 0)
            p.read(a2, s, 1)
        gproj(("fox", (24 + hp,)), hp - 2, per=4)
        after(1, lambda hp=hp: fox_jobs(hp))
    flush()
    drain()
    mo = p.count["mixout"]
    project_out("mix", lambda d: [(("foxo", (d,)), KD, 0)], lambda j: mo - 1,
                gate=None, stats=True)
    hn = norm(False, ("rms", 1), None)
    hd = hn
    p.add("rot")

    def unperm(g, hp, k):
        a, a2 = fresh(2), fresh()
        s = p.add("unperm", dg=g, acc=a, acc2=a2)
        p.read(a, s, 0)
        p.read(a2, s, 1)

    def dsw_jobs(hp, g):
        complete(PAIRS + GROUPS * hp + g)
        js = []
        for hh in range(2):
            js += group([dict(fam="dsw", dg=g, hh=hh, i=i, pair=hp, set=(GROUPS * hp + g) % 2) for i in range(TT)],
                        dict(fam="dsw", dg=g, hh=hh, pair=hp))
        behind = []
        if g == GROUPS - 1:
            behind.append((lambda: p.add("lse", z=js[0]["z"] - 4), False))
            for k in range(GROUPS):
                behind.append((lambda k=k: unperm(k, hp, k), True))
            behind.append((lambda: p.add("blend", tile=hp), False))
        jobs(js, behind=behind)
        ends.append(len(queue))

    for hp in range(PAIRS):
        for g in range(GROUPS):
            st_ = PAIRS + GROUPS * hp + g
            lead = hp == 0 and g == 0
            qk(("dsw", (g * 8 + hp,)), st_, "q", ("dsw_qk", g), g, hn if lead else None, 0 if lead else None, per=4)
            qk(("dsw", (24 + g * 8 + hp,)), st_, "k", ("dsw_qk", 3 + g), 3 + g, None, 1 if lead else None, per=4)
            if g == GROUPS - 1:
                gproj(("dsw", (72 + hp,)), PAIRS + GROUPS * hp - 4 if hp >= 2 else -1, per=4)
            vproj(("dsw", (48 + g * 8 + hp,)), st_, g, 2 if lead else None, per=4)
            after(2, lambda hp=hp, g=g: dsw_jobs(hp, g))
    flush()
    drain()
    mo = p.count["blend"]
    project_out("mix", lambda d: [(("dswo", (d,)), KD, 0)], lambda j: mo - 1,
                gate=None, stats=False)
    p.add("finish")
    return p


def proj_on_act(c):
    return c < 4 or 10 <= c < 22


def proj_ordinal(l, c):
    cs = [x for x in range(22) if proj_on_act(x) == proj_on_act(c)]
    return l * len(cs) + cs.index(c)


def program(nc, A, out):
    plan = make_plan()
    units = plan.units
    with ExitStack() as ctx:
        def sb(name, shape, dt=F32):
            return ctx.enter_context(nc.sbuf_tensor(name, shape, dt))

        def sem(name):
            return ctx.enter_context(nc.semaphore(name))

        x = sb("x", [P, KD, T])
        act_hi = {"h": sb("h_hi", [P, KD, T], F32R)}
        act_lo = {"h": sb("h_lo", [P, KD, T], F32R)}
        raw = [sb(f"raw{i}", [P, SLOT]) for i in range(RAW_SLOTS)]
        w_hi = [sb(f"w_hi{i}", [P, SLOT], F32R) for i in range(SPLIT_SLOTS)]
        w_lo = [sb(f"w_lo{i}", [P, SLOT], F32R) for i in range(SPLIT_SLOTS)]
        cols = sb("cols", [P, NCOL])
        rows = sb("rows", [P, NROW])
        con = sb("con", [P, NCON])
        mod = sb("mod", [P, NMOD, 24])
        modg = sb("modg", [P, NMOD, 16])
        csil = sb("csil", [P, KD])
        st = sb("st", [P, 8])
        st2 = sb("st2", [P, 8])
        tmp_a = [sb(f"tmp_a{i}", [P, T]) for i in range(2)]
        tmp_b = [sb(f"tmp_b{i}", [P, T]) for i in range(2)]
        tmp_h = [sb(f"tmp_h{i}", [P, T]) for i in range(2)]
        tmp_f = tmp_b

        def col(name, i=0, n=1):
            return cols[:, COL[name] + i:COL[name] + i + n]

        def row(name, i, n):
            return rows[:, ROW[name] + i:ROW[name] + i + n]

        def cst(name):
            return con[:, CON[name]:CON[name] + P]

        ident = cst("ident")

        with ExitStack() as one:
            act_hi["gu"] = one.enter_context(nc.sbuf_tensor("gu_hi", [P, KF, T], F32R))
            act_lo["gu"] = one.enter_context(nc.sbuf_tensor("gu_lo", [P, KF, T], F32R))
        with ExitStack() as one:
            def ph(name, shape, dt=F32):
                return one.enter_context(nc.sbuf_tensor(name, shape, dt))

            sT = [ph(f"scores{i}", [P, T]) for i in range(2)]
            pT = [ph(f"probs{i}", [P, T]) for i in range(3)]
            ptT = [ph(f"probs_t{i}", [P, T]) for i in range(2)]
            mn = ph("row_min", [P, ZRING, 4])
            zs = ph("row_sum", [P, ZRING, 4])
            otmp = ph("otmp", [P, TT, HD])
            rz = ph("rz", [P, 8])
            with ExitStack() as two:
                def p1(name, shape, dt=F32):
                    return two.enter_context(nc.sbuf_tensor(name, shape, dt))

                otok = p1("otok", [P, TT, T])
                opair = otok[:, :, 0:P]
                q1 = p1("q1", [P, 4, T])
                kd = p1("kd", [P, 4, T])
                v1 = p1("v1", [P, 2, TT, P])
                gates = p1("gates", [P, TT, 24])
                dts = p1("dts", [P, TT, 8])
                dtmp = p1("dtmp", [P, TT, 4])
                dtmp2 = p1("dtmp2", [P, TT, 4])
                toep = p1("toep_bias", [P, 2, 2, TOEP])
                ug = p1("ug", [P, TT, 256])
                vg = p1("vg", [P, TT, 256])
                zg = p1("zg", [P, TT, 256])
                xbc = p1("xbc", [P, 6, T])
                xpad = p1("xpad", [P, T + 3])
                cmpr = p1("cmpr", [P, 2, 16, CMPW])
                b1c = p1("b1c", [P, 2])
                hid = p1("hid", [P, 2, 62])
                cw2 = p1("cw2", [P, 2, 192])
                kc = p1("kc", [P, 2, NCMP])
                vc = p1("vc", [NCMP, 2, HD])
                gw = kd[:, 2, :].rearrange("p (k c) -> p k c", k=4)
                csr = kd[0:4, 0, :]
                bn = p1("bn", [P, TT, 6])
                mv = p1("mv", [P, TT, 2])
                gstd = p1("gstd", [P, TT])
                gm = cmpr[:, :, :, :].rearrange("p j k c -> p (j k c)")[:, 0:1024].rearrange("p (t c) -> p t c", t=TT)
                csc = p1("csc", [P, TT, 4])
                xtok = q1[:, 0:2, :].rearrange("p a (t c) -> p (a t) c", t=2)
                xdt = q1[:, 2:4, :].rearrange("p a (t c) -> p (a t) c", t=2)
            with ExitStack() as two:
                def p2(name, shape, dt=F32):
                    return two.enter_context(nc.sbuf_tensor(name, shape, dt))

                act_hi["mix"] = p2("mix_hi", [P, KD, T], F32R)
                act_lo["mix"] = p2("mix_lo", [P, KD, T], F32R)
                o3 = p2("o3", [P, GROUPS, TT, P])
                q2 = p2("q2", [P, 2, T])
                k2 = p2("k2", [P, 2, T])
                v2 = p2("v2", [P, 2, TT, P])
                sg = [p2(f"sg{i}", [P, T]) for i in range(2)]
                qn = [p2(f"qn{i}", [P, TT, P]) for i in range(2)]
                rq = p2("rq", [P, 8])
                ss = p2("ss", [P, 8])
                ss2 = p2("ss2", [P, 8])
                var = p2("var", [P, 8])
                rt = [p2(f"rt{i}", [P, TT, 2, 8]) for i in range(4)]
                fl = p2("fl", [P, TT, 16])
                fl2 = p2("fl2", [P, TT, 16])
                lnz = p2("lnz", [P, 2 * GROUPS, TT])
                lse = p2("lse", [P, 2 * GROUPS, TT])
                rep = p2("rep", [P, TT, P])
                og = p2("og", [P, GROUPS, T])
                lg = p2("lg", [P, GROUPS, T])
                fb = lg[:, 0:2, :]
                crow = og[0:16, 0, :]
                wsum = p2("wsum", [P, T])
                pos_i = p2("pos_i", [P, TT], I32)
                pos = p2("pos", [P, TT])
                ang = p2("ang", [P, TT, 8])
                an2 = p2("an2", [P, TT, 8])
                cs8 = p2("cs8", [P, 2, TT, 8])
                rtab = p2("rtab", [P, 6, 4, TT, 8])
            del two
        with ExitStack() as one:
            rel = one.enter_context(nc.sbuf_tensor("rel", [33, 8], F32))
            onehot = one.enter_context(nc.sbuf_tensor("onehot", [33, REV], F32))
            revs = one.enter_context(nc.sbuf_tensor("revs", [P, 8, REV], F32))
        rev_d = nc.dram_tensor("rev_scratch", (8, P, REV), F32)

        acc_bank = [ctx.enter_context(nc.psum_tensor(f"acc{i}", [P, 512], F32)) for i in range(ACC_BANKS)]
        s_bank = [ctx.enter_context(nc.psum_tensor(f"sps{i}", [P, 512], F32)) for i in range(2)]
        pt_bank = ctx.enter_context(nc.psum_tensor("ptps", [P, 512], F32))
        o_bank = ctx.enter_context(nc.psum_tensor("ops", [P, 512], F32))
        m_bank = ctx.enter_context(nc.psum_tensor("mps", [P, 512], F32))

        head_bank = [o_bank, m_bank]

        def acc(a):
            return acc_bank[a % ACC_BANKS]

        def perm_tiles(ap, g):
            if g == 0:
                return ap.rearrange("p (t j) -> p t j", t=TT)
            return ap.rearrange("p (j t) -> p t j", t=TT)

        s_raw = [sem(f"raw{i}") for i in range(RAW_SLOTS)]
        s_toep = [sem(f"toep{i}") for i in range(2)]
        s_act_chain = sem("act_chain")
        s_ada_mm = sem("ada_mm")
        s_blend_exp = sem("blend_exp")
        s_blend_out = sem("blend_out")
        s_blend_sub = sem("blend_sub")
        s_cmp_mm = sem("cmp_mm")
        s_cmph_act = sem("cmph_act")
        s_cmph_b = sem("cmph_b")
        s_cmpo_mm = sem("cmpo_mm")
        s_cmpo_out = sem("cmpo_out")
        s_const = sem("const")
        s_conv = sem("conv")
        s_cs_back = sem("cs_back")
        s_cs_col = sem("cs_col")
        s_cs_mm = sem("cs_mm")
        s_cs_scan = sem("cs_scan")
        s_csil = sem("csil")
        s_dve_chain = sem("dve_chain")
        s_fbias_mm = sem("fbias_mm")
        s_fbias_out = sem("fbias_out")
        s_fgate_ln = sem("fgate_ln")
        s_fgate_ls = sem("fgate_ls")
        s_fgate_mm = sem("fgate_mm")
        s_fgate_scan = sem("fgate_scan")
        s_fgate_x = sem("fgate_x")
        s_gate_lo = sem("gate_lo")
        s_gate_mul = sem("gate_mul")
        s_gate_silu = sem("gate_silu")
        s_gd_a = sem("gd_a")
        s_gd_ln = sem("gd_ln")
        s_gd_x = sem("gd_x")
        s_gemm_mm = sem("gemm_mm")
        s_unperm_rep = sem("unperm_rep")
        s_qkt_out = sem("qkt_out")
        s_qkt_mm = sem("qkt_mm")
        s_lse_ln = sem("lse_ln")
        s_flip_mm = sem("flip_mm")
        s_flip_copy = sem("flip_copy")
        s_gln_mv = sem("gln_mv")
        s_gln_out = sem("gln_out")
        s_gln_std = sem("gln_std")
        s_gsp_mm = sem("gsp_mm")
        s_gsp_out = sem("gsp_out")
        s_gw_dma = sem("gw_dma")
        s_h_act = sem("h_act")
        s_h_hi = sem("h_hi")
        s_h_lo = sem("h_lo")
        s_heads_done = sem("heads_done")
        s_mixout_hi = sem("mixout_hi")
        s_mixout_lo = sem("mixout_lo")
        s_mixout_mm = sem("mixout_mm")
        s_mod_done = sem("mod_done")
        s_norm_bc = sem("norm_bc")
        s_norm_r = sem("norm_r")
        s_norm_std = sem("norm_std")
        s_norm_t = sem("norm_t")
        s_norm_var = sem("norm_var")
        s_norm_x = sem("norm_x")
        s_p_ready = sem("p_ready")
        s_pos_dma = sem("pos_dma")
        s_proj_act = sem("proj_act")
        s_proj_dve = sem("proj_dve")
        s_pt_copied = sem("pt_copied")
        s_qkn_copy = sem("qkn_copy")
        s_qkn_qn = sem("qkn_qn")
        s_qkn_rot = sem("qkn_rot")
        s_qkn_sq = sem("qkn_sq")
        s_qkn_ss = sem("qkn_ss")
        s_qkn_std = sem("qkn_std")
        s_rel_big = sem("rel_big")
        s_resid_y = sem("resid_y")
        s_resid_z = sem("resid_z")
        s_rev_copy = sem("rev_copy")
        s_rev_dma = sem("rev_dma")
        s_rev_mm = sem("rev_mm")
        s_rot_ang = sem("rot_ang")
        s_rot_cs = sem("rot_cs")
        s_s_ready = sem("s_ready")
        s_scores_mm = sem("scores_mm")
        s_sgate_out = sem("sgate_out")
        s_small_dma = sem("small_dma")
        s_square = sem("square")
        s_ssb_mask = sem("ssb_mask")
        s_ssb_mm = sem("ssb_mm")
        s_ssg_out = sem("ssg_out")
        s_ssn_out = sem("ssn_out")
        s_ssn_sq = sem("ssn_sq")
        s_ssn_std = sem("ssn_std")
        s_ssn_sum = sem("ssn_sum")
        s_sss_e = sem("sss_e")
        s_sss_mm = sem("sss_mm")
        s_sss_mul = sem("sss_mul")
        s_ssy_mm = sem("ssy_mm")
        s_stat_mm = sem("stat_mm")
        s_stored = sem("stored")
        s_turn_mm = sem("turn_mm")
        s_unperm_l = sem("unperm_l")
        s_unperm_mm = sem("unperm_mm")
        s_unperm_o = sem("unperm_o")
        s_values_mm = sem("values_mm")
        s_vcopy_out = sem("vcopy_out")
        s_w_hi = sem("w_hi")
        s_w_lo = sem("w_lo")
        s_xbc = sem("xbc")
        s_xdt = sem("xdt")
        s_xtok_copy = sem("xtok_copy")
        s_xtok_mm = sem("xtok_mm")
        block = ctx.enter_context(nc.Block())

        def chain_of(eng, s_chain):
            count = [0]

            def link(ins):
                count[0] += 1
                ins.then_inc(s_chain, 1)
                eng.wait_ge(s_chain, count[0])
            return link

        n_const = 6

        def job_q(s):
            if s["fam"] == "nsa":
                b = (s["h"] % 2) * HD
                return q1[b:b + HD, s["h"] // 2, s["i"] * P:(s["i"] + 1) * P]
            b = s["hh"] * HD
            if s["fam"] == "fox":
                return q2[b:b + HD, s["set"], s["i"] * P:(s["i"] + 1) * P]
            return perm_tiles(q2[b:b + HD, s["set"], :], s["dg"])[:, s["i"]]

        def job_k(s):
            i = s["i"]
            if s["fam"] == "nsa":
                b, g = (s["h"] % 2) * HD, s["h"] // 4
                if s["br"] == 0:
                    return kc[b:b + HD, g, :]
                return kd[b:b + HD, (s["br"] - 1) * 2 + g, 0:(i + 1) * P]
            b = s["hh"] * HD
            if s["fam"] == "fox":
                return k2[b:b + HD, s["set"], 0:(i + 1) * P]
            if s["dg"] == 0:
                return k2[b:b + HD, s["set"], max(i - 1, 0) * P:(i + 1) * P]
            return perm_tiles(k2[b:b + HD, s["set"], :], s["dg"])[:, i]

        def job_len(s):
            i = s["i"]
            if s["fam"] == "nsa":
                return NCMP if s["br"] == 0 else (i + 1) * P
            if s["fam"] == "fox":
                return (i + 1) * P
            return 2 * P if s["dg"] == 0 and i > 0 else P

        def job_bias(s):
            i, n = s["i"], job_len(s)
            if s["fam"] == "nsa":
                t = toep[:, (s["h"] // 2) % 2, s["h"] % 2, :]
                if s["br"] == 0:
                    at = 415 - i * P
                    return t[:, at:at + 16 * (NCMP - 1) + 1:16]
                return t[:, 384 - i * P:384 - i * P + n]
            if s["fam"] == "fox":
                return fb[:, s["hh"], 0:n]
            if s["dg"] == 0:
                return con[:, CON["causal"] + P - n:CON["causal"] + P]
            return cst("causal") if s["dg"] == 1 else cst("blockmask")

        def job_v(s):
            i = s["i"]
            if s["fam"] == "nsa":
                g = s["h"] // 4
                if s["br"] == 0:
                    return [vc[:, g, :]]
                return [v1[:, s["br"] - 1, t, g * HD:(g + 1) * HD] for t in range(i + 1)]
            b = s["hh"] * HD
            if s["fam"] == "fox":
                return [v2[:, s["set"], t, b:b + HD] for t in range(i + 1)]
            ts = ([i - 1] if s["dg"] == 0 and i > 0 else []) + [i]
            return [v2[:, s["set"], t, b:b + HD] for t in ts]

        def o_slot(s):
            return head_bank[s["group"] % 2][:, s["slot"] * HD:(s["slot"] + 1) * HD]

        xbc_of = {"x": 0, "B": 2, "C": 4}

        @block.sync
        def _(sp):
            sp.dma_start(cols[:, :], A["cols"]).then_inc(s_const, 16)
            sp.dma_start(con[:, :], A["con"]).then_inc(s_const, 16)
            sp.dma_start(rows[:, :], A["rows"].partition_broadcast(P)).then_inc(s_const, 16)
            sp.dma_start(x[:, :, :], A["x"]).then_inc(s_const, 16)
            sp.dma_start(onehot[:, :], A["onehot"]).then_inc(s_const, 16)
            sp.dma_start(rel[0:32, :], A["rel_bias"]).then_inc(s_const, 16)
            for src, width, split, u, kind, n in units:
                slot = u % RAW_SLOTS
                if u >= RAW_SLOTS:
                    _, _, s0, _, k0, n0 = units[u - RAW_SLOTS]
                    if k0 == "gemm":
                        sp.wait_ge(s_w_lo, s0 + 1)
                    elif k0 == "ada":
                        sp.wait_ge(s_ada_mm, n0 + 1)
                    else:
                        sp.wait_ge(s_cmp_mm, n0 + 1)
                name, idx = src
                ap = A[name]
                for i in idx:
                    ap = ap[i]
                sp.dma_start(raw[slot][:, 0:width], ap).then_inc(s_raw[slot], 16)
            for d in range(KD):
                sp.wait_ge(s_resid_z, plan.count["resid"] - KD + d + 1)
                sp.dma_start(out[d], x[:, d, :]).then_inc(s_stored, 16)
            sp.wait_ge(s_stored, 16 * KD)

        def loaded(eng, u):
            eng.wait_ge(s_raw[u % RAW_SLOTS], 16 * (u // RAW_SLOTS + 1))

        splits = [(u, width) for (_, width, s, u, _, _) in units if s is not None]
        ahead, k = [], 0
        for u in range(len(units)):
            while k < len(splits) and splits[k][0] <= u:
                k += 1
            m = k
            while m < min(k + 2, len(splits)) and splits[m][0] <= u + RAW_SLOTS - 1:
                m += 1
            ahead.append(max(m - 1, ahead[-1] if ahead else 0))

        @block.gpsimd
        def _(pool):
            def w_low(k):
                u, width = splits[k]
                pool.wait_ge(s_w_hi, k + 1)
                nc.gpsimd.tensor_tensor(w_lo[k % SPLIT_SLOTS][:, 0:width], raw[u % RAW_SLOTS][:, 0:width],
                                            w_hi[k % SPLIT_SLOTS][:, 0:width].bitcast(F32), ALU.subtract).then_inc(s_w_lo, 1)

            def h_low(s):
                for d in range(KD):
                    n = s["hn"] * KD + d
                    pool.wait_ge(s_h_hi, n + 1)
                    nc.gpsimd.tensor_tensor(act_lo["h"][:, d, :], tmp_h[d % 2][:, :],
                                                act_hi["h"][:, d, :].bitcast(F32), ALU.subtract).then_inc(s_h_lo, 1)

            low_at = 0
            for s in plan.steps:
                if s.kind in ("gemm", "ada", "cmp"):
                    while low_at <= ahead[s["u"]]:
                        w_low(low_at)
                        low_at += 1
                elif s.kind == "norm" and s["h"] is not None:
                    h_low(s)

        @block.scalar
        def _(act):
            link = chain_of(act, s_act_chain)
            tables = [None]

            def A_(out_, in_, func, **k):
                if func in (ACT.Exp, ACT.Ln):
                    if tables[0] != "exp":
                        nc.scalar.preload_act_table_set("natural_log_exp_and_others")
                    tables[0] = "exp"
                elif func not in (ACT.Copy, ACT.Identity, ACT.Square, ACT.Abs):
                    tables[0] = None
                return nc.scalar.activation(out_, in_, func, **k)
            act.wait_ge(s_const, 16 * n_const)
            hi_at = [0]

            def w_high_up_to(k):
                while hi_at[0] <= k:
                    j = hi_at[0]
                    u, width = splits[j]
                    loaded(act, u)
                    if j >= SPLIT_SLOTS:
                        act.wait_ge(s_gemm_mm, j - SPLIT_SLOTS + 1)
                    A_(w_hi[j % SPLIT_SLOTS][:, 0:width], raw[u % RAW_SLOTS][:, 0:width], ACT.Copy).then_inc(s_w_hi, 1)
                    hi_at[0] += 1

            def start(s):
                A_(csil[:, :], col("c", 0, KD), ACT.Silu).then_inc(s_csil, 1)

            def rev(s):
                if s["c"] == 15:
                    act.wait_ge(s_rev_copy, 16)
                    act.dma_start(rev_d.rearrange("h p c -> p h c"), revs[:, :, :]).then_inc(s_rev_dma, 16)

            def load_toep(l, hp):
                act.wait_ge(s_rev_dma, 16)
                for hh in range(2):
                    src = bass.AP(rev_d, (2 * hp + hh) * P * REV + P - 1, [[REV - 1, P], [1, TOEP]])
                    act.dma_start(toep[:, hp % 2, hh, :], src).then_inc(s_toep[hp % 2], 16)

            def unit(s):
                w_high_up_to(ahead[s["u"]])

            def gate(s):
                n = s.n
                act.wait_ge(s_gemm_mm, plan.last_gemm[s["a1"]] + 1)
                if n >= 2:
                    act.wait_ge(s_gate_mul, n - 1)
                A_(tmp_a[n % 2][:, :], acc(s["a1"])[:, :], ACT.Silu).then_inc(s_gate_silu, 1)

            def resid(s):
                n, d = s.n, s["d"]
                act.wait_ge(s_gemm_mm, plan.last_gemm[s["acc"]] + 1)
                if s["gate"] is not None:
                    m, w = s["gate"]
                    act.wait_ge(s_mod_done, m + 1)
                    if n >= 2:
                        act.wait_ge(s_resid_z, n - 1)
                    A_(tmp_a[n % 2][:, :], acc(s["acc"])[:, :], ACT.Identity,
                           scale=mod[:, m, 16 + d:17 + d]).then_inc(s_resid_y, 1)
                if s["stats"]:
                    act.wait_ge(s_resid_z, n + 1)
                    square(s, d)

            squares = [0]

            def square(s, d):
                j = squares[0]
                if j >= 2:
                    act.wait_ge(s_stat_mm, j - 1)
                if s.before.get("flip", 0):
                    act.wait_ge(s_flip_mm, s.before["flip"])
                A_(tmp_b[j % 2][:, :], x[:, d, :], ACT.Square).then_inc(s_square, 1)
                squares[0] += 1

            def sqx(s):
                act.wait_ge(s_norm_x, s.before["norm_x"] * KD)
                square(s, s["d"])

            def norm(s):
                hx = s["h"]
                if s["stats"]:
                    act.wait_ge(s_norm_var, s["sn"] + 1)
                    A_(st2[:, 0:4], st2[:, 4:8], ACT.Sqrt,
                           bias=col("eps5") if s["center"] else col("eps6")).then_inc(s_norm_std, 1)
                if hx is not None:
                    for d in range(KD):
                        n = s["hn"] * KD + d
                        if n >= 2:
                            act.wait_ge(s_h_lo, n - 1)
                        if s["stats"]:
                            act.wait_ge(s_norm_t, s["sn"] * KD + d + 1)
                        if hx[0] == "mod":
                            m = hx[1]
                            if d == 0:
                                act.wait_ge(s_mod_done, m + 1)
                            A_(tmp_h[d % 2][:, :], x[:, d, :], ACT.Identity,
                                   scale=modg[:, m, d:d + 1], bias=modg[:, m, 8 + d:9 + d]).then_inc(s_h_act, 1)
                        else:
                            A_(tmp_h[d % 2][:, :], tmp_a[d % 2][:, :], ACT.Identity,
                                   scale=col("norm2", hx[1] * KD + d)).then_inc(s_h_act, 1)
                if s["x"] is not None:
                    for d in range(KD):
                        if hx is None:
                            act.wait_ge(s_norm_t, s["sn"] * KD + d + 1)
                        else:
                            act.wait_ge(s_h_act, s["hn"] * KD + d + 1)
                        A_(x[:, d, :], x[:, d, :], ACT.Identity, scale=col("ln_g", s["x"] * KD + d),
                               bias=col("ln_b", s["x"] * KD + d)).then_inc(s_norm_x, 1)

            def gd(s):
                l = s["l"]
                act.wait_ge(s_gemm_mm, plan.last_gemm[s["acc"]] + 1)
                ps = acc(s["acc"])[:, 0:TT * 28].rearrange("p (t c) -> p t c", t=TT)
                act.wait_ge(s_gd_x, s.n + 1)
                link(A_(gates[:, :, :], ps[:, :, 0:24], ACT.Sigmoid))
                link(A_(dtmp2[:, :, :], dtmp[:, :, :], ACT.Abs))
                link(A_(dtmp2[:, :, :], dtmp2[:, :, :], ACT.Exp, scale=-1.0))
                link(A_(dtmp2[:, :, :], dtmp2[:, :, :], ACT.Ln, bias=1.0))
                A_(row("a_log", 4 * l, 4), row("a_log", 4 * l, 4), ACT.Exp).then_inc(s_gd_ln, 1)
                act.dma_start(cw2[:, :, :], A["cmp2"][l]).then_inc(s_small_dma, 16)
                load_toep(l, 0)
                load_toep(l, 1)

            def proj(s):
                l, c = s["l"], s["c"]
                ps = acc(s["acc"])
                if not proj_on_act(c):
                    return
                if s["flat"]:
                    act.wait_ge(s_flip_mm, plan.flipped[s["acc"]] + 1)
                else:
                    act.wait_ge(s_gemm_mm, plan.last_gemm[s["acc"]] + 1)
                if c < 4:
                    A_(q1[:, c, :], ps[:, :], ACT.Copy, scale=QSCALE).then_inc(s_proj_act, 1)
                elif c < 16:
                    dst = (ug, vg, zg)[(c - 10) // 2][:, :, (c % 2) * P:(c % 2 + 1) * P]
                    src = ps[:, :].rearrange("p (t c) -> p t c", t=TT)
                    A_(dst, src, ACT.Silu if c >= 14 else ACT.Gelu_apprx_tanh).then_inc(s_proj_act, 1)
                else:
                    k = l * 6 + c - 16
                    if k >= 1:
                        act.wait_ge(s_conv, k)
                    A_(xpad[:, 3:T + 3], ps[:, :], ACT.Copy).then_inc(s_proj_act, 1)
                    act.wait_ge(s_conv, k + 1)
                    A_(xbc[:, c - 16, :], xbc[:, c - 16, :], ACT.Silu,
                           bias=col("conv_b", l * 6 + c - 16)).then_inc(s_xbc, 1)

            def cmph(s):
                act.wait_ge(s_cmph_b, s.n + 1)
                if s.n >= 1:
                    act.wait_ge(s_cmpo_mm, s.n)
                link(A_(hid[:, 0, :], acc(s["a0"])[:, 0:62], ACT.Gelu_apprx_tanh, bias=b1c[:, 0:1]))
                A_(hid[:, 1, :], acc(s["a1"])[:, 0:62], ACT.Gelu_apprx_tanh, bias=b1c[:, 1:2]).then_inc(s_cmph_act, 1)

            def toep_step(s):
                act.wait_ge(s_s_ready, s.before["values"])
                load_toep(s["l"], s["hp"])

            def fcopy(s):
                n = s.n
                act.wait_ge(s_gemm_mm, plan.last_gemm[s["acc"]] + 1)
                act.wait_ge(s_stat_mm, s.before["stat"])
                if n >= 2:
                    act.wait_ge(s_flip_mm, n - 1)
                A_(tmp_f[n % 2][:, :], acc(s["acc"])[:, :], ACT.Copy).then_inc(s_flip_copy, 1)

            def softmax(s):
                j, L = s.n, job_len(s)
                g, i = s["z"], s["slot"]
                act.wait_ge(s_s_ready, j + 1)
                if j >= 3:
                    act.wait_ge(s_turn_mm, j - 2)
                if s["slot"] == 0 and s["group"] >= 4:
                    act.wait_ge(s_heads_done, s["group"] - 3)
                A_(pT[j % 3][:, 0:L], sT[j % 2][:, 0:L], ACT.Exp, scale=-1.0,
                       bias=mn[:, g, i:i + 1], accum_out=zs[:, g, i:i + 1]).then_inc(s_p_ready, 1)

            def copy_pt(s):
                j, L = s.n, job_len(s)
                nb, K = (L + P - 1) // P, min(L, P)
                act.wait_ge(s_turn_mm, j + 1)
                if j >= 2:
                    act.wait_ge(s_values_mm, j - 1)
                A_(ptT[j % 2][0:K, 0:nb * P], pt_bank[0:K, 0:nb * P], ACT.Copy).then_inc(s_pt_copied, 1)

            def lse_(s):
                z = s["z"]
                act.wait_ge(s_heads_done, s.before["heads"])
                A_(lnz[:, :, :], zs[:, z:z + 2 * GROUPS, :], ACT.Ln).then_inc(s_lse_ln, 1)

            def mixout(s):
                n, t, dst = s.n, s["tile"], s["dst"]
                act.wait_ge(s_mixout_mm, n + 1)
                if s["pair"] is not None:
                    return
                sc = col(*s["scale"]) if s["scale"] else col("one")
                A_(act_hi[dst][:, t, :], acc(s["acc"])[:, :], ACT.Identity, scale=sc).then_inc(s_mixout_hi, 1)

            def sss_exp(s):
                b, i, h = s["b"], s["i"], s["h"]
                k = s.n
                ps = s_bank[b % 2]
                if i == 0:
                    act.wait_ge(s_ssb_mask, b + 1)
                    act.wait_ge(s_cs_col, s["l"] + 1)
                if k >= 2:
                    act.wait_ge(s_sss_mul, k - 1)
                E = sT[k % 2]
                diag = ptT[0][:, i * P:(i + 1) * P]
                if i == TT - 1:
                    A_(E[:, 0:P], diag, ACT.Exp, bias=csc[:, i, h:h + 1]).then_inc(s_sss_e, 1)
                else:
                    link(A_(E[:, 0:P], diag, ACT.Exp, bias=csc[:, i, h:h + 1]))
                    A_(E[:, P:(TT - i) * P], ps[:, (i + 1) * P:T], ACT.Exp, bias=csc[:, i, h:h + 1]).then_inc(s_sss_e, 1)

            def xtok_(s):
                n, t = s.n, s["t"]
                act.wait_ge(s_xtok_mm, n + 1)
                A_(xtok[:, :, t * P:(t + 1) * P], acc(s["acc"])[:, :].rearrange("p (t c) -> p t c", t=TT),
                       ACT.Copy).then_inc(s_xtok_copy, 1)

            def ssn(s):
                act.wait_ge(s_ssg_out, 2 * s.n + 1 + 1)
                A_(tmp_a[0][:, :].rearrange("p (t c) -> p t c", t=TT), opair[:, :, :], ACT.Square).then_inc(s_ssn_sq, 1)
                act.wait_ge(s_ssn_sum, s.n + 1)
                A_(gstd[:, :], mv[:, :, 0], ACT.Sqrt, scale=1.0 / P, bias=col("eps5")).then_inc(s_ssn_std, 1)

            def gln(s):
                act.wait_ge(s_scores_mm, s.before["scores"])
                act.dma_start(gw, A["gws"][s["l"]]).then_inc(s_gw_dma, 16)
                act.wait_ge(s_gln_mv, s.n + 1)
                A_(gstd[:, :], mv[:, :, 1], ACT.Sqrt, bias=col("eps5")).then_inc(s_gln_std, 1)

            def fgate(s):
                act.wait_ge(s_fgate_x, 1)
                link(A_(fl2[:, :, :], fl[:, :, :], ACT.Abs))
                link(A_(fl2[:, :, :], fl2[:, :, :], ACT.Exp, scale=-1.0))
                A_(fl2[:, :, :], fl2[:, :, :], ACT.Ln, bias=1.0).then_inc(s_fgate_ln, 1)

            def fbias(s):
                n = s.n
                act.wait_ge(s_fbias_mm, n + 1)
                if n >= 2:
                    act.wait_ge(s_s_ready, s.before["scores"] - TT)
                A_(fb[:, s["hh"], :], acc(s["acc"])[:, :], ACT.Copy).then_inc(s_fbias_out, 1)

            def qkn(s):
                n = s.n
                act.wait_ge(s_qkn_copy, n + 1)
                A_(tmp_a[0][:, :], qn[n % 2][:, :, :].rearrange("p t c -> p (t c)"), ACT.Square).then_inc(s_qkn_sq, 1)

            def qks(s):
                act.wait_ge(s_qkn_ss, s.n + 1)
                link(A_(ss2[:, :], ss[:, :], ACT.Ln, scale=1.0 / HD, bias=col("eps6")))
                A_(ss2[:, :], ss2[:, :], ACT.Exp, scale=-0.5).then_inc(s_qkn_std, 1)

            def qkt(s):
                which, g = s["which"]
                act.wait_ge(s_qkt_mm, s.n + 1)
                act.wait_ge(s_scores_mm, s["used"])
                sc = col(*s["col"])
                dst = (q2 if which == "q" else k2)[:, g, :]
                A_(dst, acc(s["acc"])[:, :], ACT.Identity, scale=sc).then_inc(s_qkt_out, 1)

            def vcopy(s):
                act.wait_ge(s_flip_mm, plan.flipped[s["acc"]] + 1)
                act.wait_ge(s_values_mm, s["used"])
                A_(v2[:, s["slot"], :, :], acc(s["acc"])[:, :].rearrange("p (t c) -> p t c", t=TT),
                       ACT.Copy).then_inc(s_vcopy_out, 1)

            def sgate(s):
                act.wait_ge(s_gemm_mm, plan.last_gemm[s["acc"]] + 1)
                act.wait_ge(s_mixout_lo, s.before["mixout"])
                if s.before.get("blend", 0):
                    act.wait_ge(s_blend_out, s.before["blend"])
                A_(sg[s.n % 2][:, :], acc(s["acc"])[:, :], ACT.Silu).then_inc(s_sgate_out, 1)

            def unperm(s):
                n, g = s.n, s["dg"]
                act.wait_ge(s_unperm_mm, 2 * n + 1)
                if n >= GROUPS:
                    act.wait_ge(s_blend_out, n // GROUPS)
                a, b = acc(s["acc"]), acc(s["acc2"])

                A_(perm_tiles(og[:, g, :], g), perm_tiles(a[:, :], 0), ACT.Copy).then_inc(s_unperm_o, 1)
                act.wait_ge(s_unperm_mm, 2 * n + 1 + 1)
                A_(perm_tiles(lg[:, g, :], g), perm_tiles(b[:, :], 0), ACT.Copy).then_inc(s_unperm_l, 1)

            def rot(s):
                act.dma_start(pos_i[:, :], A["pos"]).then_inc(s_pos_dma, 16)
                act.wait_ge(s_rot_ang, 1)
                link(A_(cs8[:, 1, :, :], ang[:, :, :], ACT.Sin))
                link(A_(an2[:, :, :], ang[:, :, :], ACT.Abs))
                A_(cs8[:, 0, :, :], an2[:, :, :], ACT.Sin, scale=-1.0, bias=col("halfpi")).then_inc(s_rot_cs, 1)

            def blend(s):
                n = s.n
                act.wait_ge(s_blend_sub, n + 1)
                for g in range(GROUPS):
                    ins = A_(lg[:, g, :], lg[:, g, :], ACT.Exp)
                    link(ins) if g < GROUPS - 1 else ins.then_inc(s_blend_exp, 1)

            parts = dict(start=start, gemm=unit, ada=unit, cmp=unit, gate=gate, resid=resid, sqx=sqx, norm=norm, gd=gd, proj=proj,
                         cmph=cmph, toep=toep_step, soft=softmax, turn=copy_pt, lse=lse_, mixout=mixout, rev=rev, fcopy=fcopy, qkt=qkt,
                         sss=sss_exp, xtok=xtok_, ssn=ssn, gln=gln, fgate=fgate, fbias=fbias, qkn=qkn, qks=qks,
                         vcopy=vcopy, sgate=sgate, unperm=unperm, rot=rot, blend=blend)
            for s in plan.steps:
                if s.kind in parts:
                    parts[s.kind](s)

        @block.vector
        def _(dve):
            link = chain_of(dve, s_dve_chain)
            V = nc.vector
            dve.wait_ge(s_const, 16 * n_const)

            def start(s):
                V.memset(rel[32:33, :], BIG).then_inc(s_rel_big, 1)
                for name, i, n in (("fox_qk", 0, 1), ("dsw_qk", 0, 3)):
                    link(V.tensor_scalar(col(name, i, n), col(name, i, n), QSCALE, None, ALU.mult))

            def rev(s):
                c = s["c"]
                dve.wait_ge(s_rev_mm, c + 1)
                V.tensor_copy(revs[:, c // 2, (c % 2) * 512:(c % 2 + 1) * 512],
                              s_bank[c % 2][:, :]).then_inc(s_rev_copy, 1)

            def mod_(s):
                m = s["m"]
                l, sub = divmod(m, NSUB)
                dve.wait_ge(s_ada_mm, m * 24 + 23 + 1)
                ps = m_bank[:, (m % 2) * 24:(m % 2) * 24 + 24]
                link(V.tensor_tensor(mod[:, m, :], ps, col("ada_b", m * 24, 24), ALU.add))
                link(V.tensor_scalar(mod[:, m, 8:24], mod[:, m, 8:24], 1.0, None, ALU.add))
                w = 1.0 if sub == 1 else 0.5
                link(V.tensor_scalar(mod[:, m, 16:24], mod[:, m, 16:24], w, None, ALU.mult))
                if m == 0:
                    link(V.tensor_copy(modg[:, m, 0:8], mod[:, m, 8:16]))
                    V.tensor_copy(modg[:, m, 8:16], mod[:, m, 0:8]).then_inc(s_mod_done, 1)
                else:
                    g, b = col("ln_g", (m - 1) * KD, KD), col("ln_b", (m - 1) * KD, KD)
                    link(V.tensor_tensor(modg[:, m, 0:8], mod[:, m, 8:16], g, ALU.mult))
                    link(V.tensor_tensor(modg[:, m, 8:16], mod[:, m, 8:16], b, ALU.mult))
                    V.tensor_tensor(modg[:, m, 8:16], modg[:, m, 8:16], mod[:, m, 0:8], ALU.add).then_inc(s_mod_done, 1)

            def gate(s):
                n, t = s.n, s["t"]
                if n == 0:
                    dve.wait_ge(s_rev_dma, 16)
                dve.wait_ge(s_gate_silu, n + 1)
                dve.wait_ge(s_gemm_mm, plan.last_gemm[s["a3"]] + 1)
                V.tensor_tensor(tmp_h[n % 2][:, :], acc(s["a3"])[:, :], tmp_a[n % 2][:, :],
                                ALU.mult).then_inc(s_gate_mul, 1)
                dve.wait_ge(s_gate_mul, n + 1)
                link(V.tensor_copy(act_hi["gu"][:, t, :], tmp_h[n % 2][:, :]))
                V.tensor_tensor(act_lo["gu"][:, t, :], tmp_h[n % 2][:, :],
                                    act_hi["gu"][:, t, :].bitcast(F32), ALU.subtract).then_inc(s_gate_lo, 1)

            def resid(s):
                n, d = s.n, s["d"]
                if s["gate"] is not None:
                    dve.wait_ge(s_resid_y, n + 1)
                    if s.before.get("norm_x", 0):
                        dve.wait_ge(s_norm_x, (s.before["norm_x"] - 1) * KD + d + 1)
                    V.scalar_tensor_tensor(out=x[:, d, :], in0=x[:, d, :], scalar=ALPHA,
                                               in1=tmp_a[n % 2][:, :], op0=ALU.mult, op1=ALU.add).then_inc(s_resid_z, 1)
                else:
                    dve.wait_ge(s_gemm_mm, plan.last_gemm[s["acc"]] + 1)
                    V.tensor_tensor(x[:, d, :], x[:, d, :], acc(s["acc"])[:, :], ALU.add).then_inc(s_resid_z, 1)

            def norm(s):
                if s["stats"]:
                    dve.wait_ge(s_stat_mm, s.before["stat"])
                    if s["center"]:
                        link(V.tensor_scalar(st[:, 0:8], o_bank[:, 0:8], STAT_N, None, ALU.mult))
                        link(V.tensor_tensor(st2[:, 4:8], st[:, 0:4], st[:, 0:4], ALU.mult))
                        V.tensor_tensor(st2[:, 4:8], st[:, 4:8], st2[:, 4:8], ALU.subtract).then_inc(s_norm_var, 1)
                    else:
                        V.tensor_scalar(st2[:, 4:8], o_bank[:, 4:8], STAT_N, None, ALU.mult).then_inc(s_norm_var, 1)
                    dve.wait_ge(s_norm_std, s["sn"] + 1)
                    V.reciprocal(st[:, 4:8], st2[:, 0:4]).then_inc(s_norm_r, 1)
                    dve.wait_ge(s_norm_bc, s["sn"] + 1)
                for d in range(KD):
                    if s["stats"]:
                        if s["center"]:
                            link(V.tensor_tensor(x[:, d, :], x[:, d, :], s_bank[0][:, :], ALU.subtract))
                            V.tensor_tensor(x[:, d, :], x[:, d, :], s_bank[1][:, :], ALU.mult).then_inc(s_norm_t, 1)
                        else:
                            if d >= 2:
                                dve.wait_ge(s_h_act, s["hn"] * KD + d - 1)
                            V.tensor_tensor(tmp_a[d % 2][:, :], x[:, d, :], s_bank[1][:, :], ALU.mult).then_inc(s_norm_t, 1)
                    if s["h"] is not None:
                        if d >= 1:
                            high(s, d - 1)
                if s["h"] is not None:
                    high(s, KD - 1)

            def high(s, d):
                n = s["hn"] * KD + d
                dve.wait_ge(s_h_act, n + 1)
                V.tensor_copy(act_hi["h"][:, d, :], tmp_h[d % 2][:, :]).then_inc(s_h_hi, 1)

            def gd(s):
                l = s["l"]
                dve.wait_ge(s_gemm_mm, plan.last_gemm[s["acc"]] + 1)
                ps = acc(s["acc"])[:, 0:TT * 28].rearrange("p (t c) -> p t c", t=TT)
                b = row("dt_b", 4 * l, 4).unsqueeze(1).to_broadcast([P, TT, 4])
                V.tensor_tensor(dtmp[:, :, :], ps[:, :, 24:28], b, ALU.add).then_inc(s_gd_x, 1)
                dve.wait_ge(s_gd_ln, s.n + 1)
                link(V.tensor_scalar(dtmp[:, :, :], dtmp[:, :, :], 0.0, None, ALU.max))
                link(V.tensor_tensor(dts[:, :, 0:4], dtmp[:, :, :], dtmp2[:, :, :], ALU.add))
                a = row("a_log", 4 * l, 4).unsqueeze(1).to_broadcast([P, TT, 4])
                link(V.tensor_tensor(dts[:, :, 4:8], dts[:, :, 0:4], a, ALU.mult))
                V.tensor_scalar(dts[:, :, 4:8], dts[:, :, 4:8], -1.0, None, ALU.mult).then_inc(s_gd_a, 1)
                link(V.memset(xpad[:, 0:3], 0.0))
                for j in range(2):
                    link(V.memset(cmpr[:, j, :, 62:64], 0.0))
                    link(V.tensor_copy(cmpr[:, j, :, 62:63], col("pe", (l * 2 + j) * 16, 16).unsqueeze(2)))

            def proj(s):
                l, c = s["l"], s["c"]
                ps = acc(s["acc"])
                if c >= 16:
                    k = l * 6 + c - 16
                    dve.wait_ge(s_proj_act, proj_ordinal(l, c) + 1)
                    y = xbc[:, c - 16, :]
                    w = [col("conv_w", (l * 6 + c - 16) * 4 + t) for t in range(4)]
                    link(V.tensor_scalar(y, xpad[:, 0:T], w[0], None, ALU.mult))
                    for t in range(1, 4):
                        ins = V.scalar_tensor_tensor(out=y, in0=xpad[:, t:t + T], scalar=w[t], in1=y,
                                                     op0=ALU.mult, op1=ALU.add)
                        link(ins) if t < 3 else ins.then_inc(s_conv, 1)
                    return
                if proj_on_act(c):
                    return
                if s["flat"]:
                    dve.wait_ge(s_flip_mm, plan.flipped[s["acc"]] + 1)
                else:
                    dve.wait_ge(s_gemm_mm, plan.last_gemm[s["acc"]] + 1)
                if c in (4, 5):
                    j = c - 4
                    for g in range(2):
                        for l2 in range(2):
                            for half in range(2):
                                src = ps[g * HD:(g + 1) * HD, half * 16:half * 16 + NCMP * 16]
                                src = src.rearrange("p (n j l) -> p j n l", j=8, l=2)[:, :, :, l2]
                                dst = cmpr[l2 * HD:(l2 + 1) * HD, j, half * 8:half * 8 + 8,
                                           g * NCMP:(g + 1) * NCMP]
                                ins = V.tensor_copy(dst, src)
                                if (g, l2, half) == (1, 1, 1):
                                    ins.then_inc(s_proj_dve, 1)
                                else:
                                    link(ins)
                elif c in (6, 8):
                    b = (c - 6)
                    for g in range(2):
                        for half in range(2):
                            ins = V.tensor_copy(kd[half * HD:(half + 1) * HD, b + g, :],
                                                ps[g * HD:(g + 1) * HD, :])
                            if (g, half) == (1, 1):
                                ins.then_inc(s_proj_dve, 1)
                            else:
                                link(ins)
                else:
                    V.tensor_copy(v1[:, (c - 7) // 2, :, :], ps[:, :].rearrange("p (t c) -> p t c", t=TT)).then_inc(s_proj_dve, 1)

            def cmph(s):
                l, j = s["l"], s["j"]
                dve.wait_ge(s_cmp_mm, 4 * (s.n + 1))
                if s.n:
                    dve.wait_ge(s_cmph_act, s.n)
                b = COL["cmp_b1"] + (l * 2 + j) * 2
                link(V.tensor_tensor(b1c[:, 0:1], acc(s["a0"])[:, 62:63], cols[:, b:b + 1], ALU.add))
                V.tensor_tensor(b1c[:, 1:2], acc(s["a1"])[:, 62:63], cols[:, b + 1:b + 2], ALU.add).then_inc(s_cmph_b, 1)

            def cmpo(s):
                dve.wait_ge(s_cmpo_mm, s.n + 1)
                if s["j"] == 0:
                    V.tensor_copy(kc[:, :, :], acc(s["acc"])[:, 0:62].rearrange("p (g n) -> p g n", g=2)).then_inc(s_cmpo_out, 1)
                else:
                    V.tensor_copy(vc[:, :, :], acc(s["acc"])[0:NCMP, 0:128].rearrange("p (g n) -> p g n", g=2)).then_inc(s_cmpo_out, 1)

            def scores(s):
                j, L = s.n, job_len(s)
                g, i = s["z"], s["slot"]
                dve.wait_ge(s_scores_mm, j + 1)
                if j >= 2:
                    dve.wait_ge(s_p_ready, j - 1)
                if s["fam"] == "nsa" and s["br"] == 0 and s["slot"] == 0 and s["h"] % 2 == 0:
                    hp = s["h"] // 2
                    dve.wait_ge(s_toep[hp % 2], 32 * (2 * s["l"] + hp // 2 + 1))
                if s["fam"] == "fox" and s["slot"] == 0:
                    dve.wait_ge(s_fbias_out, 2 * s["pair"] + s["hh"] + 1)
                if s["slot"] == 0 and s["group"] >= 4:
                    dve.wait_ge(s_heads_done, s["group"] - 3)
                V.tensor_tensor_reduce(sT[j % 2][:, 0:L], s_bank[j % 2][:, 0:L], job_bias(s), 1.0, 3.0e38,
                                           ALU.add, ALU.min, mn[:, g, i:i + 1]).then_inc(s_s_ready, 1)

            def heads(s):
                dve.wait_ge(s_values_mm, s["j"] + 1)
                out_ = head_bank[s["g"] % 2][:, 0:256].rearrange("p (t c) -> p t c", t=TT)
                link(V.reciprocal(rz[:, 0:4], zs[:, s["z"], :]))
                if s["fam"] == "nsa":
                    h, br = s["h"], s["br"]
                    o = otok[:, :, h * HD:(h + 1) * HD]
                    link(V.tensor_tensor(rz[:, 0:4], rz[:, 0:4], gates[:, :, 3 * h + br], ALU.mult))
                    if br == 0:
                        link(V.tensor_tensor(rz[:, 0:1], rz[:, 0:1], col("valid"), ALU.mult))
                    w = rz[:, 0:4].unsqueeze(2).to_broadcast([P, TT, HD])
                    if br == 0:
                        V.tensor_tensor(o, out_, w, ALU.mult).then_inc(s_heads_done, 1)
                    else:
                        link(V.tensor_tensor(otmp[:, :, :], out_, w, ALU.mult))
                        V.tensor_tensor(o, o, otmp[:, :, :], ALU.add).then_inc(s_heads_done, 1)
                    dve.wait_ge(s_heads_done, s.n + 1)
                    return
                w = rz[:, 0:4].unsqueeze(2).to_broadcast([P, TT, HD])
                b = s["hh"] * HD
                if s["fam"] == "fox":
                    if s["hh"] == 0:
                        dve.wait_ge(s_mixout_mm, s.before["mixout"])
                    o = o3[:, 0, :, b:b + HD]
                else:
                    if s["hh"] == 0 and s.before.get("unperm", 0):
                        dve.wait_ge(s_unperm_mm, 2 * s.before["unperm"])
                    o = o3[:, s["dg"], :, b:b + HD]
                V.tensor_tensor(o, out_, w, ALU.mult).then_inc(s_heads_done, 1)
                dve.wait_ge(s_heads_done, s.n + 1)

            def lse_(s):
                dve.wait_ge(s_lse_ln, s.n + 1)
                link(V.tensor_tensor(lse[:, :, :], mn[:, s["z"]:s["z"] + 2 * GROUPS, :], lnz[:, :, :], ALU.subtract))

            def unperm(s):
                g = s["dg"]
                if s.n >= 1:
                    dve.wait_ge(s_unperm_mm, 2 * s.n)
                V.tensor_copy(rep[:, :, :].rearrange("p t (h c) -> p t h c", h=2),
                              lse[:, 2 * g:2 * g + 2, :].rearrange("p h t -> p t h").unsqueeze(3)
                              .to_broadcast([P, TT, 2, HD])).then_inc(s_unperm_rep, 1)

            def mixout(s):
                n, t, dst = s.n, s["tile"], s["dst"]
                hi, lo = act_hi[dst][:, t, :], act_lo[dst][:, t, :]
                dve.wait_ge(s_mixout_mm, n + 1)
                if s["pair"] is not None:
                    dve.wait_ge(s_sgate_out, s["pair"] + 1)
                    link(V.tensor_tensor(wsum[:, :], acc(s["acc"])[:, :], sg[s["pair"] % 2][:, :], ALU.mult))
                    link(V.tensor_copy(hi, wsum[:, :]))
                    V.tensor_tensor(lo, wsum[:, :], hi.bitcast(F32), ALU.subtract).then_inc(s_mixout_lo, 1)
                    return
                dve.wait_ge(s_mixout_hi, s["hin"] + 1)
                sc = col(*s["scale"]) if s["scale"] else col("one")
                V.scalar_tensor_tensor(out=lo, in0=acc(s["acc"])[:, :], scalar=sc, in1=hi.bitcast(F32),
                                           op0=ALU.mult, op1=ALU.subtract).then_inc(s_mixout_lo, 1)

            def gln(s):
                l = s["l"]
                dve.wait_ge(s_proj_act, proj_ordinal(l, 13) + 1)
                for i in range(TT):
                    link(V.bn_stats(bn[:, i, :], vg[:, i, :]))
                    ins = V.bn_aggr(mv[:, i, :], bn[:, i, :])
                    link(ins) if i < TT - 1 else ins.then_inc(s_gln_mv, 1)
                dve.wait_ge(s_gln_std, s.n + 1)
                link(V.reciprocal(rz[:, 0:4], gstd[:, :]))
                for i in range(TT):
                    link(V.tensor_scalar(vg[:, i, :], vg[:, i, :], mv[:, i, 0:1], rz[:, i:i + 1],
                                         ALU.subtract, ALU.mult))
                g = row("gln_g", 256 * l, 256).unsqueeze(1).to_broadcast([P, TT, 256])
                b = row("gln_b", 256 * l, 256).unsqueeze(1).to_broadcast([P, TT, 256])
                link(V.tensor_tensor(vg[:, :, :], vg[:, :, :], g, ALU.mult))
                link(V.tensor_tensor(vg[:, :, :], vg[:, :, :], b, ALU.add))
                dve.wait_ge(s_gw_dma, 16 * (l + 1))
                m = cst("tril_t").unsqueeze(1).to_broadcast([P, 4, P])
                V.tensor_tensor(gw, gw, m, ALU.mult).then_inc(s_gln_out, 1)

            def gsp(s):
                l = s["l"]
                for k in range(4):
                    if k % 2 == 0:
                        dve.wait_ge(s_gsp_mm, 2 * s.n + k // 2 + 1)
                    ps = acc(s["acc"][k // 2])[:, (k % 2) * 256:(k % 2 + 1) * 256].rearrange("p (t c) -> p t c", t=TT)
                    ins = V.scalar_tensor_tensor(out=gm[:, :, k * HD:(k + 1) * HD], in0=ps,
                                                 scalar=col("gmlp_bs", l * 4 + k), in1=ug[:, :, k * HD:(k + 1) * HD],
                                                 op0=ALU.add, op1=ALU.mult)
                    link(ins) if k % 2 == 0 else ins.then_inc(s_gsp_out, 1)

            def cs(s):
                l = s["l"]
                dve.wait_ge(s_cs_mm, s.n + 1)
                ones = con[0:4, CON["ones"]:CON["ones"] + 1].to_broadcast([4, T])
                V.tensor_tensor_scan(csr, ones, acc(s["acc"])[0:4, :], 0.0, ALU.mult, ALU.add).then_inc(s_cs_scan, 1)
                dve.wait_ge(s_cs_back, s.n + 1)
                V.tensor_scalar(csc[:, :, :], acc(s["acc2"])[:, 0:16].rearrange("p (t c) -> p t c", t=TT),
                                    -1.0, None, ALU.mult).then_inc(s_cs_col, 1)

            def xtok_(s):
                t = s["t"]
                dve.wait_ge(s_xtok_copy, s.n + 1)
                v = slice(t * P, (t + 1) * P)
                V.tensor_tensor(xdt[:, :, v].rearrange("p t (h c) -> p t h c", h=2),
                                    xtok[:, :, v].rearrange("p t (h c) -> p t h c", h=2),
                                    dts[:, :, 2 * t:2 * t + 2].unsqueeze(3).to_broadcast([P, TT, 2, HD]), ALU.mult).then_inc(s_xdt, 1)

            def ssb(s):
                n = s.n
                dve.wait_ge(s_ssb_mm, n + 1)
                if n % 4 == 0:
                    dve.wait_ge(s_values_mm, s.before["values"])
                if n >= 1:
                    dve.wait_ge(s_sss_e, 4 * n)
                m = cst("ssm_mask").unsqueeze(1).to_broadcast([P, TT, P])
                V.tensor_tensor(ptT[0][:, :].rearrange("p (t c) -> p t c", t=TT),
                                    s_bank[n % 2][:, :].rearrange("p (t c) -> p t c", t=TT), m, ALU.add).then_inc(s_ssb_mask, 1)

            def sss(s):
                k, i = s.n, s["i"]
                L = T - i * P
                dve.wait_ge(s_sss_mm, k + 1)
                dve.wait_ge(s_sss_e, k + 1)
                if k >= 2:
                    dve.wait_ge(s_ssy_mm, k - 1)
                V.tensor_tensor(pT[k % 2][:, 0:L], sT[k % 2][:, 0:L], acc(s["acc"])[:, 0:L], ALU.mult).then_inc(s_sss_mul, 1)

            def ssg(s):
                n, h, hh = s.n, s["h"], s["hh"]
                dve.wait_ge(s_ssy_mm, 4 * n + 3 + 1)
                if hh == 0:
                    dve.wait_ge(s_mixout_mm, s.before.get("mixout", 0))
                half = head_bank[n % 2][:, 0:256].rearrange("p (t c) -> p t c", t=TT)
                o = opair[:, :, hh * HD:(hh + 1) * HD]
                v = slice(h * HD, (h + 1) * HD)
                link(V.scalar_tensor_tensor(out=o, in0=xtok[:, :, v], scalar=row("ssm_d", 4 * s["l"] + h, 1),
                                            in1=half, op0=ALU.mult, op1=ALU.add))
                V.tensor_tensor(o, o, zg[:, :, v], ALU.mult).then_inc(s_ssg_out, 1)
                dve.wait_ge(s_ssg_out, n + 1)

            def ssn(s):
                dve.wait_ge(s_ssn_sq, s.n + 1)
                V.tensor_reduce(mv[:, :, 0:1], tmp_a[0][:, :].rearrange("p (t c) -> p t c", t=TT), AX.X, ALU.add).then_inc(s_ssn_sum, 1)
                dve.wait_ge(s_ssn_std, s.n + 1)
                link(V.reciprocal(rz[:, 0:4], gstd[:, :]))
                V.tensor_tensor(opair[:, :, :], opair[:, :, :],
                                    rz[:, 0:4].unsqueeze(2).to_broadcast([P, TT, P]), ALU.mult).then_inc(s_ssn_out, 1)
                dve.wait_ge(s_ssn_out, s.n + 1)

            def fgate(s):
                dve.wait_ge(s_gemm_mm, plan.last_gemm[s["acc"]] + 1)
                b = row("b_f", 0, 16).unsqueeze(1).to_broadcast([P, TT, 16])
                V.tensor_tensor(fl[:, :, :], acc(s["acc"])[:, 0:64].rearrange("p (t c) -> p t c", t=TT), b,
                                    ALU.add).then_inc(s_fgate_x, 1)
                dve.wait_ge(s_fgate_ln, 1)
                link(V.tensor_scalar(fl[:, :, :], fl[:, :, :], 0.0, None, ALU.min))
                V.tensor_tensor(fl[:, :, :], fl[:, :, :], fl2[:, :, :], ALU.subtract).then_inc(s_fgate_ls, 1)
                dve.wait_ge(s_fgate_mm, 1)
                ones = con[0:16, CON["ones"]:CON["ones"] + 1].to_broadcast([16, T])
                V.tensor_tensor_scan(crow, ones, acc(s["acc2"])[0:16, :], 0.0, ALU.mult, ALU.add).then_inc(s_fgate_scan, 1)

            def qkn(s):
                n = s.n
                dve.wait_ge(s_flip_mm, plan.flipped[s["acc"]] + 1)
                if n >= 2:
                    dve.wait_ge(s_qkt_mm, n - 1)
                V.tensor_copy(qn[n % 2][:, :, :].rearrange("p t c -> p (t c)"), acc(s["acc"])[:, :]).then_inc(s_qkn_copy, 1)
                dve.wait_ge(s_qkn_sq, n + 1)
                V.tensor_reduce(ss[:, :].unsqueeze(2), tmp_a[0][:, :].rearrange("p (a c) -> p a c", c=HD),
                                    AX.X, ALU.add).then_inc(s_qkn_ss, 1)
                dve.wait_ge(s_qkn_ss, n + 1)
                link(V.tensor_scalar(var[:, :], ss[:, :], 1.0 / HD, 1e-6, ALU.mult, ALU.add))

            def qks(s):
                n = s.n
                dve.wait_ge(s_qkn_std, n + 1)
                link(V.tensor_tensor(rq[:, :], ss2[:, :], ss2[:, :], ALU.mult))
                link(V.scalar_tensor_tensor(out=rq[:, :], in0=rq[:, :], scalar=-0.5, in1=var[:, :],
                                            op0=ALU.mult, op1=ALU.mult))
                link(V.scalar_tensor_tensor(out=rq[:, :], in0=rq[:, :], scalar=1.5, in1=ss2[:, :],
                                            op0=ALU.add, op1=ALU.mult))
                V.tensor_tensor(qn[n % 2][:, :, :].rearrange("p t (h c) -> p (t h) c", h=2),
                                    qn[n % 2][:, :, :].rearrange("p t (h c) -> p (t h) c", h=2),
                                    rq[:, :].unsqueeze(2).to_broadcast([P, 8, HD]), ALU.mult).then_inc(s_qkn_qn, 1)
                dve.wait_ge(s_qkn_qn, n + 1)
                if s["rot"] is None:
                    return
                r = s["rot"]
                v = qn[n % 2][:, :, :].rearrange("p t (h c) -> p t h c", h=2)
                t1, t2 = v[:, :, :, 0:8], v[:, :, :, 8:16]

                def tab(i):
                    return rtab[:, r, i, :, :].unsqueeze(2).to_broadcast([P, TT, 2, 8])
                link(V.tensor_tensor(rt[0][:, :, :, :], t1, tab(0), ALU.mult))
                link(V.tensor_tensor(rt[1][:, :, :, :], t2, tab(1), ALU.mult))
                link(V.tensor_tensor(rt[2][:, :, :, :], t2, tab(2), ALU.mult))
                link(V.tensor_tensor(rt[3][:, :, :, :], t1, tab(3), ALU.mult))
                link(V.tensor_tensor(t1, rt[0][:, :, :, :], rt[1][:, :, :, :], ALU.subtract))
                V.tensor_tensor(t2, rt[2][:, :, :, :], rt[3][:, :, :, :], ALU.add).then_inc(s_qkn_rot, 1)

            def rot(s):
                dve.wait_ge(s_pos_dma, 16)
                link(V.tensor_copy(pos[:, :], pos_i[:, :]))
                link(V.tensor_tensor(ang[:, :, :], pos[:, :].unsqueeze(2).to_broadcast([P, TT, 8]),
                                     row("invf", 0, 8).unsqueeze(1).to_broadcast([P, TT, 8]), ALU.mult))
                magic = 12582912.0
                link(V.tensor_scalar(an2[:, :, :], ang[:, :, :], 1.0 / (2 * np.pi), magic, ALU.mult, ALU.add))
                link(V.tensor_scalar(an2[:, :, :], an2[:, :, :], magic, None, ALU.subtract))
                c1 = 6.28125
                c2 = float(np.float32(np.round((2 * np.pi - c1) * 2 ** 22) / 2 ** 22))
                c3 = 2 * np.pi - c1 - c2
                for c in (c1, c2, c3):
                    link(V.scalar_tensor_tensor(out=ang[:, :, :], in0=an2[:, :, :], scalar=-c, in1=ang[:, :, :],
                                                op0=ALU.mult, op1=ALU.add))
                pi = 3.1415925
                V.tensor_scalar(ang[:, :, :], ang[:, :, :], pi, -pi, ALU.min, ALU.max).then_inc(s_rot_ang, 1)
                dve.wait_ge(s_rot_cs, 1)
                for r in range(6):
                    for i, (f, half) in enumerate(((0, 0), (1, 1), (0, 1), (1, 0))):
                        g = row("rot_g", r * 16 + half * 8, 8).unsqueeze(1).to_broadcast([P, TT, 8])
                        link(V.tensor_tensor(rtab[:, r, i, :, :], cs8[:, f, :, :], g, ALU.mult))

            def blend(s):
                n, t = s.n, s["tile"]
                dve.wait_ge(s_unperm_l, GROUPS * n + GROUPS)
                link(V.tensor_tensor(wsum[:, :], lg[:, 0, :], lg[:, 1, :], ALU.min))
                link(V.tensor_tensor(wsum[:, :], wsum[:, :], lg[:, 2, :], ALU.min))
                for g in range(GROUPS):
                    ins = V.tensor_tensor(lg[:, g, :], wsum[:, :], lg[:, g, :], ALU.subtract)
                    link(ins) if g < GROUPS - 1 else ins.then_inc(s_blend_sub, 1)
                dve.wait_ge(s_blend_exp, n + 1)
                for g in range(GROUPS):
                    link(V.tensor_tensor(og[:, g, :], og[:, g, :], lg[:, g, :], ALU.mult))
                link(V.tensor_tensor(wsum[:, :], lg[:, 0, :], lg[:, 1, :], ALU.add))
                link(V.tensor_tensor(wsum[:, :], wsum[:, :], lg[:, 2, :], ALU.add))
                link(V.reciprocal(wsum[:, :], wsum[:, :]))
                link(V.tensor_tensor(og[:, 0, :], og[:, 0, :], og[:, 1, :], ALU.add))
                link(V.tensor_tensor(og[:, 0, :], og[:, 0, :], og[:, 2, :], ALU.add))
                link(V.tensor_tensor(og[:, 0, :], og[:, 0, :], wsum[:, :], ALU.mult))
                dve.wait_ge(s_sgate_out, PAIRS + n + 1)
                link(V.tensor_tensor(og[:, 0, :], og[:, 0, :], sg[(PAIRS + n) % 2][:, :], ALU.mult))
                hi, lo = act_hi["mix"][:, t, :], act_lo["mix"][:, t, :]
                link(V.tensor_copy(hi, og[:, 0, :]))
                V.tensor_tensor(lo, og[:, 0, :], hi.bitcast(F32), ALU.subtract).then_inc(s_blend_out, 1)

            parts = dict(start=start, mod=mod_, gate=gate, resid=resid, norm=norm, gd=gd, proj=proj, cmph=cmph,
                         cmpo=cmpo, scores=scores, heads=heads, rev=rev, lse=lse_, unperm=unperm, mixout=mixout, gln=gln, gsp=gsp, cs=cs, xtok=xtok_,
                         ssb=ssb, sss=sss, ssg=ssg, ssn=ssn, fgate=fgate, qkn=qkn, qks=qks, rot=rot, blend=blend)
            for s in plan.steps:
                if s.kind in parts:
                    parts[s.kind](s)

        @block.tensor
        def _(pe):
            mm = nc.tensor.matmul
            pe.wait_ge(s_const, 16 * n_const)

            def bank_free(a):
                if a < ACC_BANKS:
                    return
                u, role = plan.reader[a - ACC_BANKS]
                n, kind = u.n, u.kind
                if kind == "gate":
                    if role == 1:
                        pe.wait_ge(s_gate_silu, n + 1)
                    else:
                        pe.wait_ge(s_gate_mul, n + 1)
                elif kind == "resid":
                    if u["gate"] is not None:
                        pe.wait_ge(s_resid_y, n + 1)
                    else:
                        pe.wait_ge(s_resid_z, n + 1)
                elif kind == "fcopy":
                    pe.wait_ge(s_flip_copy, n + 1)
                elif kind == "gd":
                    pe.wait_ge(s_gd_ln, n + 1)
                elif kind == "proj":
                    if proj_on_act(u["c"]):
                        pe.wait_ge(s_proj_act, proj_ordinal(u["l"], u["c"]) + 1)
                    else:
                        pe.wait_ge(s_proj_dve, proj_ordinal(u["l"], u["c"]) + 1)
                elif kind == "cmph":
                    pe.wait_ge(s_cmph_act, n + 1)
                elif kind == "cmpo":
                    pe.wait_ge(s_cmpo_out, n + 1)
                elif kind == "mixout":
                    pe.wait_ge(s_mixout_lo, n + 1)
                elif kind == "gsp":
                    pe.wait_ge(s_gsp_out, 2 * n + role + 1)
                elif kind == "cs":
                    if role == 0:
                        pe.wait_ge(s_cs_scan, n + 1)
                    else:
                        pe.wait_ge(s_cs_col, n + 1)
                elif kind == "xtok":
                    pe.wait_ge(s_xtok_copy, n + 1)
                elif kind == "sss":
                    pe.wait_ge(s_sss_mul, n + 1)
                elif kind == "fgate":
                    if role == 0:
                        pe.wait_ge(s_fgate_x, n + 1)
                    else:
                        pe.wait_ge(s_fgate_scan, n + 1)
                elif kind == "qkn":
                    pe.wait_ge(s_qkn_copy, n + 1)
                elif kind == "qkt":
                    pe.wait_ge(s_qkt_out, n + 1)
                elif kind == "vcopy":
                    pe.wait_ge(s_vcopy_out, n + 1)
                elif kind == "sgate":
                    pe.wait_ge(s_sgate_out, n + 1)
                elif kind == "fbias":
                    pe.wait_ge(s_fbias_out, n + 1)
                elif kind == "unperm":
                    if role == 0:
                        pe.wait_ge(s_unperm_o, n + 1)
                    else:
                        pe.wait_ge(s_unperm_l, n + 1)

            def turn_tiles(dst, srcs, rows_=P):
                for i, ap in enumerate(srcs):
                    ins = nc.tensor.transpose(dst[:, i * P:(i + 1) * P], ap, ident[:rows_, :rows_])
                return ins

            def start(s):
                pe.wait_ge(s_rel_big, 1)

            def rev(s):
                c = s["c"]
                if c >= 2:
                    pe.wait_ge(s_rev_copy, c - 1)
                mm(s_bank[c % 2][:, :], rel[:, c // 2:c // 2 + 1].to_broadcast([33, P]),
                           onehot[:, (c % 2) * 512:(c % 2 + 1) * 512], start=True, stop=True).then_inc(s_rev_mm, 1)

            def ada(s):
                u, m, c = s["u"], s["m"], s["c"]
                loaded(pe, u)
                if c == 0:
                    pe.wait_ge(s_csil, 1)
                    if m >= 1:
                        pe.wait_ge(s_mod_done, m)
                    if s.before.get("heads", 0):
                        pe.wait_ge(s_heads_done, s.before["heads"])
                    if s.before.get("ssg", 0):
                        pe.wait_ge(s_ssg_out, s.before["ssg"])
                at = (m % 2) * 24 + c
                for k in range(KD):
                    ins = mm(m_bank[:, at:at + 1], raw[u % RAW_SLOTS][:, k * P:(k + 1) * P], csil[:, k:k + 1],
                             start=k == 0, stop=k == KD - 1)
                ins.then_inc(s_ada_mm, 1)

            def product(s, k):
                a, w, kk, ks = s["acc"], s["split"] % SPLIT_SLOTS, s["k0"] + k, slice(k * P, (k + 1) * P)
                hi, lo = act_hi[s["act"]][:, kk, :], act_lo[s["act"]][:, kk, :]
                mm(acc(a)[:, :], w_hi[w][:, ks], hi, start=s["start"] and k == 0, stop=False, skip_group_check=True)
                mm(acc(a)[:, :], w_hi[w][:, ks], lo, start=False, stop=False, skip_group_check=True)
                return mm(acc(a)[:, :], w_lo[w][:, ks], hi, start=False, stop=s["stop"] and k == s["kc"] - 1,
                          skip_group_check=True)

            def gemm(s):
                if s["lead"] in (0, 1):
                    return
                if s["lead"] == "narrow":
                    narrow(s)
                    return
                if s["lead"] == 2:
                    for g in s["batch"]:
                        pe.wait_ge(s_w_lo, g["split"] + 1)
                        bank_free(g["acc"])
                    for k in range(KD):
                        pe.wait_ge(s_h_lo, s["batch"][0]["reads"] * KD + k + 1)
                        for g in s["batch"]:
                            ins = product(g, k)
                            if k == KD - 1:
                                ins.then_inc(s_gemm_mm, 1)
                    return
                pe.wait_ge(s_w_lo, s["split"] + 1)
                if s["reads"] is not None:
                    if s["act"] == "gu":
                        pe.wait_ge(s_gate_lo, s["reads"] + 1)
                    elif s["src"] == "dswo":
                        pe.wait_ge(s_blend_out, s["reads"] + 1)
                    else:
                        pe.wait_ge(s_mixout_lo, s["reads"] + 1)
                if s["start"]:
                    bank_free(s["acc"])
                parts_of(s, 0, s["upto"])

            def parts_of(s, k0, k1):
                for k in range(k0, k1):
                    ins = product(s, k)
                if k1 == s["kc"]:
                    ins.then_inc(s_gemm_mm, 1)

            def part(s):
                parts_of(s["g"], s["at"], s["upto"])

            def narrow(s):
                a, w, n = s["acc"], s["split"] % SPLIT_SLOTS, s["nc"]
                pe.wait_ge(s_w_lo, s["split"] + 1)
                bank_free(a)
                for i in range(TT):
                    o, tok = acc(a)[:, i * n:(i + 1) * n], slice(i * P, (i + 1) * P)
                    for k in range(KD):
                        ks = slice(k * n, (k + 1) * n)
                        mm(o, act_hi["h"][:, k, tok], w_hi[w][:, ks], start=k == 0, stop=False)
                        mm(o, act_hi["h"][:, k, tok], w_lo[w][:, ks], start=False, stop=False)
                        ins = mm(o, act_lo["h"][:, k, tok], w_hi[w][:, ks], start=False, stop=k == KD - 1)
                ins.then_inc(s_gemm_mm, 1)

            def flip(s):
                n = s.n
                pe.wait_ge(s_flip_copy, n + 1)
                bank_free(s["acc2"])
                tiles = perm_tiles(tmp_f[n % 2][:, :], s["perm"])
                turn_tiles(acc(s["acc2"]), [tiles[:, i] for i in range(TT)]).then_inc(s_flip_mm, 1)

            def stat(s):
                d, j = s["d"], s.n
                pe.wait_ge(s_square, j + 1)
                if s["center"]:
                    pe.wait_ge(s_resid_z, s["r"] + 1)
                if d == 0:
                    if s.before.get("heads", 0):
                        pe.wait_ge(s_heads_done, s.before["heads"])
                    if s.before.get("ssg", 0):
                        pe.wait_ge(s_ssg_out, s.before["ssg"])
                    if s.before.get("norm_stats", 0) > 0:
                        pe.wait_ge(s_norm_var, s.before.get("norm_stats", 0))
                for half, src in enumerate((x[:, d, :], tmp_b[j % 2][:, :])):
                    if half == 0 and not s["center"]:
                        continue
                    for i in range(TT):
                        first = d == 0 and i == 0 and (half == 0 or not s["center"])
                        ins = mm(o_bank[:, half * 4 + i:half * 4 + i + 1], src[:, i * P:(i + 1) * P],
                                 cst("ones")[:, 0:1], start=first, stop=d == KD - 1, skip_group_check=True)
                ins.then_inc(s_stat_mm, 1)

            def norm(s):
                if not s["stats"]:
                    return
                pe.wait_ge(s_norm_r, s["sn"] + 1)
                if s.before.get("scores", 0):
                    pe.wait_ge(s_s_ready, s.before["scores"])
                if s.before.get("sss", 0):
                    pe.wait_ge(s_sss_e, s.before["sss"])
                if s["sn"] >= 1:
                    pe.wait_ge(s_norm_t, s["sn"] * KD)
                for bank, at in ((0, 0), (1, 4)) if s["center"] else ((1, 4),):
                    for i in range(TT):
                        ins = mm(s_bank[bank][:, i * P:(i + 1) * P], st[:, at + i:at + i + 1].to_broadcast([P, P]), ident,
                                 start=True, stop=True)
                ins.then_inc(s_norm_bc, 1)

            def cmp_(s):
                u, j, q = s["u"], s["j"], s["q"]
                loaded(pe, u)
                if q == 0:
                    bank_free(s["a0"])
                    bank_free(s["a1"])
                    pe.wait_ge(s_proj_dve, proj_ordinal(s["l"], 9) + 1)
                w = raw[u % RAW_SLOTS][:, 0:1024].rearrange("p (c n) -> p c n", c=4)
                for c in range(4):
                    k = q * 4 + c
                    for hh, a in enumerate((s["a0"], s["a1"])):
                        ins = mm(acc(a)[:, 0:CMPW], w[:, c, hh * P:(hh + 1) * P], cmpr[:, j, k, :],
                                 start=k == 0, stop=k == 15)
                ins.then_inc(s_cmp_mm, 1)

            def cmpo(s):
                a, j = s["acc"], s["j"]
                pe.wait_ge(s_cmph_act, s.n + 1)
                pe.wait_ge(s_small_dma, 16 * (s["l"] + 1))
                bank_free(a)
                if j == 0:
                    for hh in range(2):
                        ins = mm(acc(a)[:, 0:62], cw2[:, hh, 0:P], hid[:, hh, :], start=hh == 0, stop=hh == 1)
                else:
                    for g in range(2):
                        for hh in range(2):
                            ins = mm(acc(a)[0:NCMP, g * HD:(g + 1) * HD], hid[:, hh, g * NCMP:(g + 1) * NCMP],
                                     cw2[:, hh, P:P + HD], start=hh == 0, stop=hh == 1)
                ins.then_inc(s_cmpo_mm, 1)

            def scores(s):
                j, L = s.n, job_len(s)
                if j >= 2:
                    pe.wait_ge(s_s_ready, j - 1)
                if s["slot"] == 0:
                    if s["fam"] == "nsa":
                        pe.wait_ge(s_cmpo_out, 2 * s["l"] + 1 + 1)
                        pe.wait_ge(s_proj_act, proj_ordinal(s["l"], 3) + 1)
                        pe.wait_ge(s_proj_dve, proj_ordinal(s["l"], 9) + 1)
                    else:
                        pe.wait_ge(s_qkt_out, s.before["qkt"])
                mask = s["fam"] == "fox"
                ins = mm(s_bank[j % 2][:, 0:L], job_q(s), job_k(s), start=True, stop=True)
                if mask:
                    ins = mm(s_bank[j % 2][:, L - P:L], ident, cst("causal"), start=False, stop=True,
                             skip_group_check=True)
                ins.then_inc(s_scores_mm, 1)

            def turn(s):
                j, L = s.n, job_len(s)
                pe.wait_ge(s_p_ready, j + 1)
                if j >= 1:
                    pe.wait_ge(s_pt_copied, j)
                for b in range((L + P - 1) // P):
                    w = min(P, L - b * P)
                    ins = nc.tensor.transpose(pt_bank[0:w, b * P:(b + 1) * P], pT[j % 3][:, b * P:b * P + w], ident)
                ins.then_inc(s_turn_mm, 1)

            def values(s):
                j = s.n
                vs = job_v(s)
                pe.wait_ge(s_pt_copied, j + 1)
                if s["slot"] == 0:
                    if s["group"] >= 2:
                        pe.wait_ge(s_heads_done, s["group"] - 1)
                    pe.wait_ge(s_mod_done, s.before["mod"])
                    if s.before["norm_stats"]:
                        pe.wait_ge(s_norm_var, s.before["norm_stats"])
                    if s["fam"] != "nsa":
                        pe.wait_ge(s_vcopy_out, s.before["vcopy"])
                K = NCMP if s["fam"] == "nsa" and s["br"] == 0 else P
                for b, v in enumerate(vs):
                    ins = mm(o_slot(s), ptT[j % 2][0:K, b * P:(b + 1) * P], v, start=b == 0, stop=b == len(vs) - 1)
                ins.then_inc(s_values_mm, 1)

            def mixout(s):
                a = s["acc"]
                if s["src"] == "heads":
                    pe.wait_ge(s_heads_done, s.before["heads"])
                elif s["src"] == "gmlp":
                    pe.wait_ge(s_gsp_out, 2 * s.before["gsp"])
                else:
                    pe.wait_ge(s_ssn_out, s.before["ssn"])
                bank_free(a)
                if s["src"] == "gmlp":
                    srcs = [gm[:, i, s["t"] * P:(s["t"] + 1) * P] for i in range(TT)]
                else:
                    srcs = [opair[:, i, :] for i in range(TT)]
                    if s["src"] == "heads":
                        t = s["tile"]
                        srcs = [o3[:, 0, i, :] if s["pair"] is not None else otok[:, i, t * P:(t + 1) * P]
                                for i in range(TT)]
                turn_tiles(acc(a), srcs).then_inc(s_mixout_mm, 1)

            def gsp(s):
                pe.wait_ge(s_gln_out, s.n + 1)
                for k in range(4):
                    a = s["acc"][k // 2]
                    if k % 2 == 0:
                        bank_free(a)
                    ins = mm(acc(a)[:, (k % 2) * 256:(k % 2 + 1) * 256], gw[:, k, :], vg[:, :, k * HD:(k + 1) * HD],
                             start=True, stop=True)
                    if k % 2 == 1:
                        ins.then_inc(s_gsp_mm, 1)

            def cs(s):
                a, a2 = s["acc"], s["acc2"]
                pe.wait_ge(s_gd_a, s["l"] + 1)
                bank_free(a)
                turn_tiles(acc(a)[0:4, :], [dts[:, i, 4:8] for i in range(TT)]).then_inc(s_cs_mm, 1)
                pe.wait_ge(s_cs_scan, s.n + 1)
                bank_free(a2)
                for i in range(TT):
                    ins = nc.tensor.transpose(acc(a2)[:, i * 4:(i + 1) * 4], csr[:, i * P:(i + 1) * P],
                                              con[0:4, CON["ident"]:CON["ident"] + 4])
                ins.then_inc(s_cs_back, 1)

            def xtok_(s):
                a, t = s["acc"], s["t"]
                pe.wait_ge(s_xbc, s["l"] * 6 + 5 + 1)
                bank_free(a)
                turn_tiles(acc(a), [xbc[:, t, i * P:(i + 1) * P] for i in range(TT)]).then_inc(s_xtok_mm, 1)

            def ssb(s):
                h, n = s["h"], s.n
                if n % 4 == 0:
                    pe.wait_ge(s_s_ready, s.before["scores"])
                if n >= 2:
                    pe.wait_ge(s_sss_e, 4 * (n - 2) + 3 + 1)
                sel = con[0:4, CON["ident"] + h:CON["ident"] + h + 1].to_broadcast([4, P])
                mm(s_bank[n % 2][:, :], sel, csr, start=True, stop=True).then_inc(s_ssb_mm, 1)

            def sss(s):
                a, i, g = s["acc"], s["i"], s["g"]
                bank_free(a)
                mm(acc(a)[:, 0:T - i * P], xbc[:, 2 + g, i * P:(i + 1) * P], xbc[:, 4 + g, i * P:T],
                       start=True, stop=True).then_inc(s_sss_mm, 1)

            def ssy(s):
                k, i, h = s["k"], s["i"], s["h"]
                pe.wait_ge(s_sss_mul, k + 1)
                n = k // 4
                if i == 0:
                    pe.wait_ge(s_xdt, s.before["xtok"])
                    if n >= 2:
                        pe.wait_ge(s_ssg_out, n - 1)
                    pe.wait_ge(s_heads_done, s.before["heads"])
                for j in range(i, TT):
                    ins = mm(head_bank[n % 2][:, j * HD:(j + 1) * HD], pT[k % 2][:, (j - i) * P:(j - i + 1) * P],
                             xdt[:, i, h * HD:(h + 1) * HD], start=i == 0 and j == 0, stop=j == i,
                             skip_group_check=True)
                ins.then_inc(s_ssy_mm, 1)

            def fgate(s):
                pe.wait_ge(s_fgate_ls, 1)
                bank_free(s["acc2"])
                turn_tiles(acc(s["acc2"])[0:16, :], [fl[:, i, :] for i in range(TT)]).then_inc(s_fgate_mm, 1)

            def fbias(s):
                a, h = s["acc"], s["h"]
                pe.wait_ge(s_fgate_scan, 1)
                bank_free(a)
                sel = con[0:16, CON["ident"] + h:CON["ident"] + h + 1].to_broadcast([16, P])
                mm(acc(a)[:, :], sel, crow, start=True, stop=True).then_inc(s_fbias_mm, 1)

            def qkt(s):
                pe.wait_ge(s_qkn_qn, s["q"] + 1)
                if s["rot"] is not None:
                    pe.wait_ge(s_qkn_rot, s["rn"] + 1)
                bank_free(s["acc"])
                turn_tiles(acc(s["acc"]), [qn[s["q"] % 2][:, i, :] for i in range(TT)]).then_inc(s_qkt_mm, 1)

            def unperm(s):
                pe.wait_ge(s_heads_done, s.before["heads"])
                pe.wait_ge(s_unperm_rep, s.n + 1)
                for a, src in ((s["acc"], o3[:, s["dg"], :, :]), (s["acc2"], rep)):
                    bank_free(a)
                    turn_tiles(acc(a), [src[:, i, :] for i in range(TT)]).then_inc(s_unperm_mm, 1)

            parts = dict(start=start, ada=ada, gemm=gemm, part=part, stat=stat, norm=norm, cmp=cmp_, cmpo=cmpo, scores=scores,
                         turn=turn, values=values, mixout=mixout, gsp=gsp, cs=cs, xtok=xtok_, ssb=ssb, sss=sss,
                         ssy=ssy, fgate=fgate, fbias=fbias, qkt=qkt, flip=flip, rev=rev, unperm=unperm)
            for s in plan.steps:
                if s.kind in parts:
                    parts[s.kind](s)


def _bucket(n):
    if n < 16:
        return max(n, 0)
    return min(16 + int(np.log(n / 16) / np.log(128 / 16) * 16), 31)


def _tiles(w):
    k, n = w.shape[0] // P, w.shape[1] // P
    return np.ascontiguousarray(w.reshape(k, P, n, P).transpose(2, 1, 0, 3).reshape(n, P, k * P))


def _narrow(w):
    k = w.shape[0] // P
    return np.ascontiguousarray(w.reshape(k, P, w.shape[1]).transpose(1, 0, 2).reshape(P, -1))


def _layout(v):
    f = {k: np.asarray(a) for k, a in v.items()}
    L = LAYERS
    o = {}
    o["x"] = np.ascontiguousarray(f["x"][0].T.reshape(KD, P, T).transpose(1, 0, 2))
    o["ada"] = np.stack([_tiles(f["ada_w"][l]) for l in range(L)])
    w1, w3, w2 = (f[n].reshape(2 * L, *f[n].shape[2:]) for n in ("ffn_w1", "ffn_w3", "ffn_w2"))
    o["ffn13"] = np.stack([np.stack([_tiles(w1[i]), _tiles(w3[i])], 1) for i in range(2 * L)])
    at = 0
    for j, k in enumerate(DOWN):
        o[f"ffn2_{j}"] = np.stack([_tiles(w2[i][at * P:(at + k) * P]) for i in range(2 * L)])
        at += k
    w = f["w_in"]
    o["win"] = np.stack([_tiles(np.concatenate([w[l][:, :1280], w[l][:, 1304:2840]], 1)) for l in range(L)])
    o["small"] = np.stack([_narrow(np.concatenate([w[l][:, 1280:1304], w[l][:, 2840:2844]], 1)) for l in range(L)])
    o["wout"] = np.stack([_tiles(f["w_out"][l]) for l in range(L)])
    o["cmp1"] = np.ascontiguousarray(
        f["cmp_w1"].reshape(L, 2, 4, 4, P, 256).transpose(0, 1, 2, 4, 3, 5).reshape(L, 2, 4, P, 1024))
    c2 = f["cmp_w2"].reshape(L, 2, 2, P, HD).transpose(0, 1, 3, 2, 4)
    o["cmp2"] = np.ascontiguousarray(np.concatenate([c2[:, 0], c2[:, 0], c2[:, 1]], -1))
    o["gws"] = np.ascontiguousarray(f["gmlp_ws"].transpose(0, 3, 1, 2))
    fw = f["fox_w_in_2"][0]
    o["fox"] = _tiles(fw[:, :4 * D])
    o["foxf"] = _narrow(fw[:, 4 * D:])
    o["foxo"] = _tiles(f["fox_w_out_2"][0])
    o["dsw"] = _tiles(f["dsw_w_in_2"][0])
    o["dswo"] = _tiles(f["dsw_w_out_2"][0])
    o["rel_bias"] = f["rel_bias"]
    o["pos"] = np.ascontiguousarray(f["positions_2"][0].reshape(TT, P).T)

    def by_col(a):
        return a.reshape(-1, P).T

    fq, fk = f["fox_q_norm_2"][0], f["fox_k_norm_2"][0]
    dq, dk = f["dsw_q_norm_2"][0], f["dsw_k_norm_2"][0]
    one16 = np.ones(16, np.float32)
    parts = {
        "ada_b": by_col(f["ada_b"]), "ln_g": by_col(f["ln_g"]), "ln_b": by_col(f["ln_b"]),
        "cmp_b1": by_col(f["cmp_b1"]),
        "pe": f["cmp_pe"].reshape(L, 2, 16, 2, HD).transpose(3, 4, 0, 1, 2).reshape(P, 64),
        "conv_w": f["ssm_conv_w"].reshape(L, 4, 6, P).transpose(3, 0, 2, 1).reshape(P, 48),
        "conv_b": by_col(f["ssm_conv_b"]), "ssm_g": by_col(f["ssm_norm_g"]), "gmlp_bs": by_col(f["gmlp_bs"]),
        "norm2": by_col(f["norm_g_2"]),
        "fox_qk": np.stack([np.concatenate([g, g]) for g in (fq, fk)], 1),
        "dsw_qk": np.stack([np.concatenate([one16, g[16:], one16, g[16:]]) for a in (dq, dk) for g in a], 1),
        "eps5": np.full((P, 1), 1e-5, np.float32), "eps6": np.full((P, 1), 1e-6, np.float32),
        "valid": (np.arange(P) >= 31).astype(np.float32)[:, None], "one": np.ones((P, 1), np.float32),
        "halfpi": np.full((P, 1), np.pi / 2, np.float32), "c": by_col(f["c"]),
    }
    o["cols"] = np.ascontiguousarray(np.concatenate([parts[n] for n, _ in _COLS], 1))
    inv = (500000.0 ** (-np.arange(0, 16, 2, dtype=np.float32) / np.float32(16))).astype(np.float32)
    parts = {
        "dt_b": f["ssm_dt_bias"], "a_log": f["ssm_a_log"], "ssm_d": f["ssm_d"], "b_f": f["fox_b_f_2"],
        "gln_g": f["gmlp_ln_g"], "gln_b": f["gmlp_ln_b"],
        "rot_g": np.concatenate([dq[:, :16], dk[:, :16]]), "invf": inv,
    }
    o["rows"] = np.concatenate([parts[n].reshape(-1) for n, _ in _ROWS])
    a, b = np.arange(P)[:, None], np.arange(P)[None, :]
    big = np.float32(BIG)
    parts = {
        "ident": a == b, "prev": (b < a) * big, "causal": (b > a) * big,
        "blockmask": ((a % 4 != b % 4) | (b > a)) * big, "ssm_mask": (b < a) * -big,
        "tril_t": b >= a, "ones": np.ones((P, P)),
    }
    o["con"] = np.concatenate([parts[n].astype(np.float32) for n, _ in _CON], 1)
    e = np.zeros((33, REV), np.float32)
    for u in range(REV):
        n = DIST0 - u
        if n >= 0:
            e[_bucket(n), u] = -1.0
        else:
            e[32, u] = 1.0
    o["onehot"] = e
    return o


def kernel(**inputs):
    import concourse.bacc as _bacc
    from concourse import mybir as _mybir
    from concourse.bass_utils import run_bass_kernel_spmd as _run

    nc = _bacc.Bacc("TRN2", target_bir_lowering=False, num_devices=1)
    arrays, args = {}, {}
    for name, a in _layout(inputs).items():
        arrays[f"in_{name}_dram"] = a
        args[name] = nc.dram_tensor(f"in_{name}_dram", a.shape, _mybir.dt.from_np(a.dtype),
                                    kind="ExternalInput").ap()
    out = nc.dram_tensor("out_0_dram", (KD, P, T), _mybir.dt.float32, kind="ExternalOutput").ap()
    program(nc, args, out)
    r = _run(nc, [arrays], core_ids=[0])
    got = r.results[0]["out_0_dram"]
    return np.ascontiguousarray(got.reshape(D, T).T)[None]
```
